# Optimizing a Trainium2 kernel written in Bass

```python
import jax, jax.numpy as jnp
from jax import lax
import numpy as np

D_MODEL = 1024
BATCH = 1
SEQ = 1024
DEPTH = 1
DEC_BATCH = 8
DEC_SEQ = 16
PAST_LEN = 512

CHUNK = 64
HEAD_DIM = 64
N_HEADS = D_MODEL // HEAD_DIM
H_B = (5 * N_HEADS) // 16
H_C = (5 * N_HEADS) // 16
H_A = N_HEADS - H_B - H_C
D_MIX = N_HEADS * HEAD_DIM
D_IN = 3 * D_MIX + H_A
BAND_CHUNKS = 8
BAND = BAND_CHUNKS * CHUNK
REL_CLIP = 128
N_REL = 2 * REL_CLIP + 1
Q_BLOCK = 128
N_GROUPS = 4
EXPERTS_PER_GROUP = 4
N_EXPERTS = N_GROUPS * EXPERTS_PER_GROUP
TOP_K = 2
D_EXPERT = D_MODEL // 4
D_PLE = 256
FORGET_BIAS = 2.0
EPS = 1e-6
ATTN_SCALE = HEAD_DIM ** -0.5
NEG_INF = -1e30

kernel_name = 'streaming_hybrid_fox_band_stickbreak_hmoe'

def rms_norm(x, g=None):
    xf = x.astype(jnp.float32)
    y = xf * lax.rsqrt(jnp.mean(xf * xf, axis=-1, keepdims=True) + EPS)
    if g is not None:
        y = y * g.astype(jnp.float32)
    return y.astype(x.dtype)

def project_heads(xn, w_in, b_f, g_qa, g_ka, g_qb, g_kb):
    b, t, _ = xn.shape
    z = xn @ w_in
    q, k, v = (z[..., j * D_MIX:(j + 1) * D_MIX].reshape(b, t, N_HEADS, HEAD_DIM) for j in range(3))
    logf = jax.nn.log_sigmoid(z[..., 3 * D_MIX:].astype(jnp.float32) + b_f.astype(jnp.float32))
    sa, sb, sc = slice(0, H_A), slice(H_A, H_A + H_B), slice(H_A + H_B, N_HEADS)
    return (rms_norm(q[:, :, sa], g_qa), rms_norm(k[:, :, sa], g_ka), v[:, :, sa], logf,
            rms_norm(q[:, :, sb], g_qb), rms_norm(k[:, :, sb], g_kb), v[:, :, sb],
            q[:, :, sc], k[:, :, sc], v[:, :, sc])

def sweep_query_blocks(fn, q_pos, *qs):
    s = q_pos.shape[0]
    nb = s // Q_BLOCK
    blocks = tuple(jnp.moveaxis(a.reshape((a.shape[0], nb, Q_BLOCK) + a.shape[2:]), 1, 0) for a in qs)
    out = lax.map(lambda xs: fn(xs[0], *xs[1]), (q_pos.reshape(nb, Q_BLOCK), blocks))
    out = jnp.moveaxis(out, 0, 1)
    return out.reshape((out.shape[0], s) + out.shape[3:])

def forgetting_attention(q, k, v, cq, ck, q_pos, k_pos):
    s = jnp.einsum('bqhd,bkhd->bhqk', q, k).astype(jnp.float32) * ATTN_SCALE
    s = s + jnp.swapaxes(cq, 1, 2)[..., :, None] - jnp.swapaxes(ck, 1, 2)[..., None, :]
    s = jnp.where(k_pos[None, :] <= q_pos[:, None], s, NEG_INF)
    p = jax.nn.softmax(s, axis=-1)
    return jnp.einsum('bhqk,bkhd->bqhd', p.astype(v.dtype), v)

def stick_breaking_attention(q, k, v, q_pos, k_pos):
    z = jnp.einsum('bqhd,bkhd->bhqk', q, k).astype(jnp.float32) * ATTN_SCALE
    seen = k_pos[None, :] < q_pos[:, None]
    log_1m_beta = jnp.where(seen, jax.nn.log_sigmoid(-z), 0.0)
    tail = lax.cumsum(log_1m_beta, axis=3, reverse=True) - log_1m_beta
    a = jnp.where(seen, jnp.exp(jax.nn.log_sigmoid(z) + tail), 0.0)
    return jnp.einsum('bhqk,bkhd->bqhd', a.astype(v.dtype), v)

def rel_bias_lookup(rel_bias, rel):
    return rel_bias[:, jnp.clip(rel, -REL_CLIP, REL_CLIP) + REL_CLIP].astype(jnp.float32)

def band_attention_prompt(q, k, v, rel_bias):
    b, s, h, d = q.shape
    nc = s // CHUNK
    width = (BAND_CHUNKS + 1) * CHUNK
    pad = ((0, 0), (BAND, 0), (0, 0), (0, 0))
    band_idx = jnp.arange(nc)[:, None] + jnp.arange(BAND_CHUNKS + 1)[None, :]
    kb = jnp.pad(k, pad).reshape(b, nc + BAND_CHUNKS, CHUNK, h, d)[:, band_idx].reshape(b, nc, width, h, d)
    vb = jnp.pad(v, pad).reshape(b, nc + BAND_CHUNKS, CHUNK, h, d)[:, band_idx].reshape(b, nc, width, h, d)
    qb = q.reshape(b, nc, CHUNK, h, d)
    k_off = jnp.arange(width) - BAND
    bias = rel_bias_lookup(rel_bias, jnp.arange(CHUNK)[:, None] - k_off[None, :])
    valid = (jnp.arange(nc)[:, None] * CHUNK + k_off[None, :]) >= 0
    sc = jnp.einsum('bcqhd,bckhd->bchqk', qb, kb).astype(jnp.float32) * ATTN_SCALE + bias
    sc = jnp.where(valid[None, :, None, None, :], sc, NEG_INF)
    p = jax.nn.softmax(sc, axis=-1)
    return jnp.einsum('bchqk,bckhd->bcqhd', p.astype(v.dtype), vb).reshape(b, s, h, d)

def band_attention_sample(q, k, v, q_pos, k_pos, rel_bias):
    s = jnp.einsum('bqhd,bkhd->bhqk', q, k).astype(jnp.float32) * ATTN_SCALE
    s = s + rel_bias_lookup(rel_bias, q_pos[:, None] - k_pos[None, :])
    p = jax.nn.softmax(s, axis=-1)
    return jnp.einsum('bhqk,bkhd->bqhd', p.astype(v.dtype), v)

def mix_prompt(heads, rel_bias):
    qa, ka, va, logf, qb, kb, vb, qc, kc, vc = heads
    s = qa.shape[1]
    pos = jnp.arange(s)
    c = jnp.cumsum(logf, axis=1)
    oa = sweep_query_blocks(lambda qp, qblk, cblk: forgetting_attention(qblk, ka, va, cblk, c, qp, pos), pos, qa, c)
    ob = band_attention_prompt(qb, kb, vb, rel_bias)
    oc = sweep_query_blocks(lambda qp, qblk: stick_breaking_attention(qblk, kc, vc, qp, pos), pos, qc)
    keep = max(s - BAND, 0)
    return (oa, ob, oc), (ka, va, logf, kb[:, keep:], vb[:, keep:], kc, vc)

def mix_sample(heads, cache_a_k, cache_a_v, cache_a_logf, cache_b_k, cache_b_v, cache_c_k, cache_c_v, rel_bias):
    qa, ka, va, logf, qb, kb, vb, qc, kc, vc = heads
    t = qa.shape[1]
    past = cache_a_k.shape[1]
    rows_b = cache_b_k.shape[1]
    q_pos = past + jnp.arange(t)
    k_pos = jnp.arange(past + t)
    c = jnp.cumsum(jnp.concatenate([cache_a_logf.astype(jnp.float32), logf], axis=1), axis=1)
    oa = forgetting_attention(qa, jnp.concatenate([cache_a_k, ka], axis=1), jnp.concatenate([cache_a_v, va], axis=1),
                              c[:, past:], c, q_pos, k_pos)
    kb_pos = jnp.concatenate([past - rows_b + jnp.arange(rows_b), q_pos])
    ob = band_attention_sample(qb, jnp.concatenate([cache_b_k, kb], axis=1), jnp.concatenate([cache_b_v, vb], axis=1),
                               q_pos, kb_pos, rel_bias)
    oc = stick_breaking_attention(qc, jnp.concatenate([cache_c_k, kc], axis=1), jnp.concatenate([cache_c_v, vc], axis=1),
                                  q_pos, k_pos)
    return (oa, ob, oc), (ka, va, logf, kb, vb, kc, vc)

def hier_moe(x, w_rg, b_rg, w_re, b_re, w_eg, w_eu, w_ed):
    xf = x.astype(jnp.float32)
    p_group = jax.nn.softmax(xf @ w_rg.astype(jnp.float32) + b_rg.astype(jnp.float32), axis=-1)
    g_sel = jnp.argmax(p_group, axis=-1)
    p_g = jnp.max(p_group, axis=-1, keepdims=True)
    e_logits = (xf @ w_re.astype(jnp.float32) + b_re.astype(jnp.float32)).reshape(-1, N_GROUPS, EXPERTS_PER_GROUP)
    e_logits = jnp.einsum('tge,tg->te', e_logits, jax.nn.one_hot(g_sel, N_GROUPS, dtype=jnp.float32))
    top_p, top_i = lax.top_k(jax.nn.softmax(e_logits, axis=-1), TOP_K)
    w = p_g * top_p / jnp.sum(top_p, axis=-1, keepdims=True)
    e_idx = g_sel[:, None] * EXPERTS_PER_GROUP + top_i
    gates = jnp.einsum('tk,tke->te', w, jax.nn.one_hot(e_idx, N_EXPERTS, dtype=jnp.float32))
    act = jax.nn.silu(jnp.einsum('td,edf->tef', x, w_eg)) * jnp.einsum('td,edf->tef', x, w_eu)
    act = act * gates[..., None].astype(act.dtype)
    return jnp.einsum('tef,efd->td', act, w_ed)

def finish_layer(h, outs, p_i, g_mix_out, w_out, norm_ffn, w_rg, b_rg, w_re, b_re,
                 w_eg, w_eu, w_ed, w_ple, norm_ple, w_ple_gate):
    b, t, _ = h.shape
    merged = jnp.concatenate([rms_norm(og.reshape(b, t, -1)) for og in outs], axis=-1)
    merged = (merged * g_mix_out).astype(h.dtype)
    h = h + merged @ w_out
    y = hier_moe(rms_norm(h, norm_ffn).reshape(b * t, D_MODEL), w_rg, b_rg, w_re, b_re, w_eg, w_eu, w_ed)
    h = h + y.reshape(b, t, D_MODEL).astype(h.dtype)
    gate = jax.nn.sigmoid((rms_norm(h, norm_ple) @ w_ple_gate).astype(jnp.float32))
    return h + ((p_i @ w_ple).astype(jnp.float32) * gate).astype(h.dtype)

def setup_inputs(seed: int = 0) -> dict:
    key = jax.random.key(seed)
    keys = iter(jax.random.split(key, 40))

    def normal(shape, scale=1.0, shift=0.0):
        return shift + scale * jax.random.normal(next(keys), shape, jnp.float32)

    rows_b = min(BAND, PAST_LEN)
    return {
        'x_prompt': normal((BATCH, SEQ, D_MODEL)),
        'x_sample': normal((DEC_BATCH, DEC_SEQ, D_MODEL)),
        'p_prompt': normal((DEPTH, BATCH, SEQ, D_PLE)),
        'p_sample': normal((DEPTH, DEC_BATCH, DEC_SEQ, D_PLE)),
        'cache_a_k': normal((DEPTH, DEC_BATCH, PAST_LEN, H_A, HEAD_DIM)),
        'cache_a_v': normal((DEPTH, DEC_BATCH, PAST_LEN, H_A, HEAD_DIM)),
        'cache_a_logf': jax.nn.log_sigmoid(normal((DEPTH, DEC_BATCH, PAST_LEN, H_A), 1.0, FORGET_BIAS)),
        'cache_b_k': normal((DEPTH, DEC_BATCH, rows_b, H_B, HEAD_DIM)),
        'cache_b_v': normal((DEPTH, DEC_BATCH, rows_b, H_B, HEAD_DIM)),
        'cache_c_k': normal((DEPTH, DEC_BATCH, PAST_LEN, H_C, HEAD_DIM)),
        'cache_c_v': normal((DEPTH, DEC_BATCH, PAST_LEN, H_C, HEAD_DIM)),
        'norm_mix': normal((DEPTH, D_MODEL), 0.1, 1.0),
        'w_in': normal((DEPTH, D_MODEL, D_IN), D_MODEL ** -0.5),
        'b_f': normal((DEPTH, H_A), 0.1, FORGET_BIAS),
        'g_qa': normal((DEPTH, HEAD_DIM), 0.1, 1.0),
        'g_ka': normal((DEPTH, HEAD_DIM), 0.1, 1.0),
        'g_qb': normal((DEPTH, HEAD_DIM), 0.1, 1.0),
        'g_kb': normal((DEPTH, HEAD_DIM), 0.1, 1.0),
        'rel_bias': normal((DEPTH, H_B, N_REL), 0.2),
        'g_mix_out': normal((DEPTH, D_MIX), 0.1, 1.0),
        'w_out': normal((DEPTH, D_MIX, D_MODEL), D_MIX ** -0.5),
        'norm_ffn': normal((DEPTH, D_MODEL), 0.1, 1.0),
        'w_router_group': normal((DEPTH, D_MODEL, N_GROUPS), D_MODEL ** -0.5),
        'b_router_group': normal((DEPTH, N_GROUPS), 0.01),
        'w_router_expert': normal((DEPTH, D_MODEL, N_EXPERTS), D_MODEL ** -0.5),
        'b_router_expert': normal((DEPTH, N_EXPERTS), 0.01),
        'w_exp_gate': normal((DEPTH, N_EXPERTS, D_MODEL, D_EXPERT), D_MODEL ** -0.5),
        'w_exp_up': normal((DEPTH, N_EXPERTS, D_MODEL, D_EXPERT), D_MODEL ** -0.5),
        'w_exp_down': normal((DEPTH, N_EXPERTS, D_EXPERT, D_MODEL), D_EXPERT ** -0.5),
        'w_ple': normal((DEPTH, D_PLE, D_MODEL), D_PLE ** -0.5),
        'norm_ple': normal((DEPTH, D_MODEL), 0.1, 1.0),
        'w_ple_gate': normal((DEPTH, D_MODEL, D_MODEL), D_MODEL ** -0.5),
    }

def reference(x_prompt, x_sample, p_prompt, p_sample,
              cache_a_k, cache_a_v, cache_a_logf, cache_b_k, cache_b_v, cache_c_k, cache_c_v,
              norm_mix, w_in, b_f, g_qa, g_ka, g_qb, g_kb, rel_bias, g_mix_out, w_out,
              norm_ffn, w_router_group, b_router_group, w_router_expert, b_router_expert,
              w_exp_gate, w_exp_up, w_exp_down, w_ple, norm_ple, w_ple_gate):
    hp, hs = x_prompt, x_sample
    new_p = [[] for _ in range(7)]
    new_s = [[] for _ in range(7)]
    for i in range(DEPTH):
        proj_w = (w_in[i], b_f[i], g_qa[i], g_ka[i], g_qb[i], g_kb[i])
        post_w = (g_mix_out[i], w_out[i], norm_ffn[i], w_router_group[i], b_router_group[i],
                  w_router_expert[i], b_router_expert[i], w_exp_gate[i], w_exp_up[i], w_exp_down[i],
                  w_ple[i], norm_ple[i], w_ple_gate[i])
        outs_p, rows_p = mix_prompt(project_heads(rms_norm(hp, norm_mix[i]), *proj_w), rel_bias[i])
        hp = finish_layer(hp, outs_p, p_prompt[i], *post_w)
        outs_s, rows_s = mix_sample(project_heads(rms_norm(hs, norm_mix[i]), *proj_w),
                                    cache_a_k[i], cache_a_v[i], cache_a_logf[i], cache_b_k[i], cache_b_v[i],
                                    cache_c_k[i], cache_c_v[i], rel_bias[i])
        hs = finish_layer(hs, outs_s, p_sample[i], *post_w)
        for j in range(7):
            new_p[j].append(rows_p[j])
            new_s[j].append(rows_s[j])
    a_k_p, a_v_p, a_f_p, b_k_p, b_v_p, c_k_p, c_v_p = [jnp.stack(r, axis=0) for r in new_p]
    a_k_s, a_v_s, a_f_s, b_k_s, b_v_s, c_k_s, c_v_s = [jnp.stack(r, axis=0) for r in new_s]
    return (hp, hs, a_k_p, a_v_p, a_f_p, b_k_p, b_v_p, c_k_p, c_v_p,
            a_k_s, a_v_s, a_f_s, b_k_s, b_v_s, c_k_s, c_v_s)


_drawn_inputs = setup_inputs


def setup_inputs(seed=0):
    import zlib

    import numpy as np

    out = dict(_drawn_inputs(seed))
    spreads = {}
    factors = {'b_router_group': 6.933, 'b_router_expert': 15.12, 'norm_ple': 4.025}
    for name, (base, spread) in spreads.items():
        noise = np.random.default_rng([zlib.crc32(name.encode()), seed]).standard_normal(out[name].shape)
        drawn = base * np.exp(spread * noise) if base else spread * noise
        out[name] = __import__('jax').numpy.asarray(drawn.astype(out[name].dtype))
    for name, factor in factors.items():
        out[name] = (out[name] * factor).astype(out[name].dtype)
    return out
```

```python
from contextlib import ExitStack

import concourse.bass as bass
from concourse import mybir

F32 = mybir.dt.float32
BF16 = mybir.dt.bfloat16
ACT = mybir.ActivationFunctionType
ALU = mybir.AluOpType
AX = mybir.AxisListType
ds = bass.ds

P = 128
D = 1024
KD = D // P
SEQ = 1024
NB, TS = 8, 16
PAST = 512
TOK = SEQ + NB * TS
NT = TOK // P
QT = SEQ // P
H, HD = 16, 64
HA, HB, HC = 6, 5, 5
GROUPS = ((0, HA), (HA, HB), (HA + HB, HC))
DIN = 3 * D + HA
REL = 257
EXT = 1792
PT = PAST // P
NE, NG, EG, DE = 16, 4, 4, 256
DP = 256
EPS = 1e-6
NEG = -1e30
SCALE = HD ** -0.5


def wait(e, sem, count, own=None):
    if isinstance(count, int) and count <= 0:
        return
    e.wait_ge(sem, count)
    if own is not None and not isinstance(count, int):
        e.sem_inc(own, 1)


class Steps:

    def __init__(self, e, sem, base, own=None):
        self.e, self.sem, self.base, self.n, self.own = e, sem, base, 0, own

    def then(self, ins):
        self.n += 1
        ins.then_inc(self.sem, 1)
        wait(self.e, self.sem, self.base + self.n, self.own)


def over_tiles(e, body):
    body(0, 0, 0)
    body(1, 1, 0)
    with e.Fori(1, NT // 2) as m:
        body(2 * m, 0, m)
        body(2 * m + 1, 1, m)
    body(NT - 1, 0, NT // 2)


def over_heads(e, n, body):
    with e.Fori(0, n // 2) as m:
        body(2 * m, 0, m)
        body(2 * m + 1, 1, m)
    if n % 2:
        body(n - 1, 0, n // 2)


def over_stages(e, enter, main, leave):
    def step(n, u, m, un, mn, ul, ml):
        if not (isinstance(n, int) and n + 1 >= NT):
            enter(n + 1, un, mn)
        if not (isinstance(n, int) and n == 0):
            leave(n - 1, ul, ml)
        main(n, u, m)

    enter(0, 0, 0)
    step(0, 0, 0, 1, 0, None, None)
    step(1, 1, 0, 0, 1, 0, 0)
    with e.Fori(1, NT // 2) as m:
        step(2 * m, 0, m, 1, m, 1, m - 1)
        step(2 * m + 1, 1, m, 0, m + 1, 0, m)
    step(NT - 1, 0, NT // 2, None, None, 1, NT // 2 - 1)
    leave(NT - 1, 0, NT // 2)


def constants(nc, sb, sem):
    c = {}
    c["ident"] = sb("ident", [P, P], F32)
    c["identb"] = sb("identb", [P, P], BF16)
    c["flip"] = sb("flip", [P, P], F32)
    c["negtri"] = sb("negtri", [P, P], F32)
    c["negones"] = sb("negones", [P, P], F32)
    c["ones"] = sb("ones", [P, P], F32)
    c["keep_stick"] = sb("keep_stick", [P, P], F32)
    c["keep_stick_s"] = sb("keep_stick_s", [P, P], F32)
    for name in ("causal", "band_diag", "band_far", "causal_s", "same_s", "stick", "stick_s"):
        c[name] = sb("mask_" + name, [P, P], BF16)
    c["eps"] = sb("eps", [P, 1], F32)
    c["zero"] = sb("zero", [P, 1], F32)
    c["one"] = sb("one", [P, 1], F32)
    made = sem("constants_made")

    with nc.Block() as block:
        @block.gpsimd
        def _(pool):
            s = Steps(pool, made, 0)

            def select(t, value, base, pattern, mult, op, fill):
                v = t[:, :]
                if len(pattern) == 2:
                    v = v.rearrange("p (b t) -> p b t", t=pattern[1][1])
                s.then(pool.affine_select(out=v, in_=v, compare_op=op, fill=fill, base=base,
                                          pattern=pattern, channel_multiplier=mult))

            def same_sample(t, fill):
                select(t, None, 0, [[-TS, NB], [0, TS]], 1, ALU.is_ge, fill)
                select(t, None, TS - 1, [[TS, NB], [0, TS]], -1, ALU.is_ge, fill)

            for name, v in (("ident", 0.0), ("identb", 0.0), ("flip", 0.0), ("negtri", -1.0), ("negones", -1.0), ("ones", 1.0),
                            ("keep_stick", 1.0), ("keep_stick_s", 1.0), ("causal", 0.0),
                            ("causal_s", 0.0), ("same_s", 0.0), ("stick", 0.0), ("stick_s", 0.0),
                            ("band_diag", 0.0), ("band_far", 0.0), ("eps", EPS), ("zero", 0.0), ("one", 1.0)):
                s.then(pool.memset(c[name][:, :], v))
            for name in ("ident", "identb"):
                select(c[name], None, 0, [[-1, P]], 1, ALU.not_equal, 1.0)
            select(c["flip"], None, -(P - 1), [[1, P]], 1, ALU.not_equal, 1.0)
            select(c["negtri"], None, 0, [[-1, P]], 1, ALU.is_ge, 0.0)
            for name, fill in (("keep_stick", 0.0), ("stick", NEG), ("keep_stick_s", 0.0), ("stick_s", NEG)):
                select(c[name], None, -1, [[1, P]], -1, ALU.is_ge, fill)
            for name in ("causal", "causal_s"):
                select(c[name], None, 0, [[-1, P]], 1, ALU.is_ge, NEG)
            for name, fill in (("keep_stick_s", 0.0), ("stick_s", NEG), ("causal_s", NEG), ("same_s", NEG)):
                same_sample(c[name], fill)
            s.then(pool.memset(c["band_diag"][0:HD, HD:P], NEG))
            s.then(pool.memset(c["band_far"][HD:P, 0:HD], NEG))
    return c


def projection(nc, c, a, dram, zeroed):
    with ExitStack() as ctx:
        sb = lambda n, s, d=F32: ctx.enter_context(nc.sbuf_tensor(n, s, d))
        ps = lambda n, s: ctx.enter_context(nc.psum_tensor(n, s, F32))
        used = []

        def sem(n):
            used.append(ctx.enter_context(nc.semaphore(n)))
            return used[-1]
        NGRP = 7
        WG = [512] * 6 + [HA]
        BANK = [0, 1, 2, 0, 1, 2, 1]
        FREE = [-3, 0, -1, 1, 2, 3, 5]
        w_in = sb("w_in", [P, KD, DIN])
        xT = sb("xT", [P, 2, KD, P])
        xr = sb("xr", [P, 2, D])
        sqx = sb("sqx", [P, D])
        gmix = sb("gmix", [P, KD])
        grow = sb("grow", [P, 2, D])
        bf = sb("bf", [P, HA])
        z = sb("z", [P, 2, DIN])
        sq = sb("sq", [P, 2, (HA + HB) * HD])
        ssx = sb("ssx", [P, 2, 2])
        hss = sb("hss", [P, 2, 22])
        lft = sb("lft", [P, 3, HA])
        logf = sb("logf", [P, 2, HA])
        qkT = sb("qkT", [P, 16, P])
        lfT = sb("lfT", [HA, TOK])
        biasx = sb("biasx", [HB, EXT])
        zp = ps("zp", [P, 3, 512])
        tp = ps("tp", [P, 4, 512])
        lp = ps("lp", [P, 512])
        ones = sb("ones_row", [P, SEQ])
        cp = sb("cp", [HA, 2, SEQ])
        lc = sb("lc", [HA * NB, PAST + TS])
        cs = sb("cs", [HA * NB, 2, PAST + TS])

        w_loaded = [sem(f"w_loaded{g}") for g in range(NGRP)]
        small_loaded = sem("small_loaded")
        sp_turns = sem("sp_turns")
        x_loaded = [sem(f"x_loaded{u}") for u in range(2)]
        z_stored = [sem(f"z_stored{u}") for u in range(2)]
        qkT_stored = sem("qkT_stored")
        xT_scaled = sem("xT_scaled")
        act_chain = sem("act_chain")
        dve_chain = sem("dve_chain")
        group_done = sem("group_done")
        group_taken = sem("group_taken")
        squares_ready = sem("squares_ready")
        heads_scaled = sem("heads_scaled")
        gates_in = sem("gates_in")
        gates_log = sem("gates_log")
        z_ready = sem("z_ready")
        turned = sem("turned")
        turned_taken = sem("turned_taken")
        grow_ready = sem("grow_ready")
        sums_ready = sem("sums_ready")
        late_stored = sem("late_stored")
        gmix_loaded = sem("gmix_loaded")
        zeros = sb("zeros", [P, D])
        zero_made = sem("zero_made")
        bias_loaded = sem("bias_loaded")
        bias_ready = sem("bias_ready")
        lc_loaded = sem("lc_loaded")
        lc_back = sem("lc_back")

        with nc.Block() as block:
            @block.sync
            def _(sp):
                sp.dma_start(xT[:, 0], a["xT"][0]).then_inc(x_loaded[0], 16)
                sp.dma_start(xr[:, 0, :], a["x"][0:P, :]).then_inc(x_loaded[0], 16)
                sp.dma_start(gmix[:, :], a["norm_mix"]).then_inc(gmix_loaded, 16)
                wv = a["w_in"].rearrange("(k p) n -> p k n", p=P)

                def load_weights(g):
                    sp.dma_start(w_in[:, :, 512 * g:512 * g + WG[g]], wv[:, :, 512 * g:512 * g + WG[g]])\
                      .then_inc(w_loaded[g], 16)
                load_weights(0)
                sp.dma_start(bf[:, :], a["b_f"].partition_broadcast(P)).then_inc(small_loaded, 16)
                for i, (src, lo, n) in enumerate((("g_qa", 0, HA), ("g_qb", HA, HB))):
                    sp.dma_start(grow[:, 0, HD * lo:HD * lo + HD], a[src].partition_broadcast(P))\
                      .then_inc(small_loaded, 16)
                for i, (src, lo, n) in enumerate((("g_ka", 0, HA), ("g_kb", HA, HB))):
                    sp.dma_start(grow[:, 1, HD * lo:HD * lo + HD], a[src].partition_broadcast(P))\
                      .then_inc(small_loaded, 16)
                sp.dma_start(lc[:, 0:PAST], a["cache_logf"]).then_inc(lc_loaded, 16)
                sp.dma_start(biasx[:, 0:REL], a["rel_bias"]).then_inc(bias_loaded, 16)

                for g in range(1, NGRP):
                    load_weights(g)

                def load(n, u, m):
                    wait(sp, group_taken, 7 * (n - 1), sp_turns)
                    sp.dma_start(xT[:, u], a["xT"][ds(n, 1)].rearrange("a p k n -> p (a k) n")).then_inc(x_loaded[u], 16)
                    sp.dma_start(xr[:, u, :], a["x"][ds(n * P, P), :]).then_inc(x_loaded[u], 16)

                def store(n, u, m):
                    wait(sp, z_ready, n + 1, sp_turns)
                    sp.dma_start(a["k_all"][ds(n * P, P), :], z[:, u, D:2 * D]).then_inc(z_stored[u], 16)
                    sp.dma_start(a["v_all"][ds(n * P, P), :], z[:, u, 2 * D:3 * D]).then_inc(z_stored[u], 16)
                    sp.dma_start(a["logf_all"][ds(n * P, P), :], logf[:, u, :]).then_inc(z_stored[u], 16)

                def store_turned(n, u, m):
                    wait(sp, turned_taken, 4 * (n + 1), sp_turns)
                    sp.dma_start(dram["qkT"][:, :, ds(n * P, P)].rearrange("j p n -> p j n"), qkT[:, :, :])\
                      .then_inc(qkT_stored, 16)

                load(1, 1, 0)
                store(0, 0, 0)
                with sp.Fori(1, NT // 2) as m:
                    load(2 * m, 0, m)
                    store(2 * m - 1, 1, m - 1)
                    store_turned(2 * m - 2, 0, m - 1)
                    load(2 * m + 1, 1, m)
                    store(2 * m, 0, m)
                    store_turned(2 * m - 1, 1, m - 1)
                load(8, 0, 4)
                store(7, 1, 3)
                store_turned(6, 0, 3)
                store(8, 0, 4)
                store_turned(7, 1, 3)
                store_turned(8, 0, 4)
                sp.wait_ge(bias_ready, 2)
                sp.dma_start(dram["bias"], biasx[:, :]).then_inc(late_stored, 16)
                sp.wait_ge(late_stored, 16)
                for h in range(HB):
                    src = bass.AP(dram["bias"].tensor, EXT * h, [[1, P], [1, 3 * P]])
                    sp.dma_start(dram["bias_hankel"][h], src).then_inc(late_stored, 16)
                sp.wait_ge(turned_taken, 4 * NT)
                sp.dma_start(dram["lfs"], lfT[:, SEQ:TOK]).then_inc(late_stored, 16)
                sp.wait_ge(late_stored, 16 * 7)
                sp.dma_start(lc[:, PAST:PAST + TS], dram["lfs"].rearrange("h (b t) -> (h b) t", t=TS))\
                  .then_inc(lc_back, 16)
                sp.wait_ge(sums_ready, 1)
                sp.dma_start(dram["c"][0, :, 0:SEQ], cp[:, 0, :]).then_inc(late_stored, 16)
                sp.dma_start(dram["c"][1, :, 0:SEQ], cp[:, 1, :]).then_inc(late_stored, 16)
                for i in range(2):
                    sp.dma_start(dram["c"][i, :, SEQ:TOK].rearrange("h (b t) -> h b t", t=TS),
                                 cs[:, i, PAST:PAST + TS]).then_inc(late_stored, 16)
                sp.dma_start(dram["c_past"].rearrange("h b k -> (h b) k"), cs[:, 1, 0:PAST]).then_inc(late_stored, 16)
                sp.wait_ge(late_stored, 16 * 12)
                sp.wait_ge(qkT_stored, 16 * NT)
                for u in range(2):
                    sp.wait_ge(z_stored[u], 48 * ((NT - u + 1) // 2))

            @block.gpsimd
            def _(pool):
                pool.memset(zeros[:, :], 0.0).then_inc(zero_made, 1)
                pool.wait_ge(gmix_loaded, 16)
                pool.wait_ge(zero_made, 1)

                def scale(n, u, m):
                    pool.wait_ge(x_loaded[u], 32 * (m + 1))
                    pool.tensor_tensor(xT[:, u], xT[:, u], gmix[:, :].unsqueeze(2).to_broadcast([P, KD, P]), ALU.mult)\
                        .then_inc(xT_scaled, 1)
                    for j in range(4):
                        pool.dma_start(dram["grouped"][ds((4 * n + j) * P, P), :], zeros[:, :]).then_inc(zeroed, 16)
                over_tiles(pool, scale)
                pool.wait_ge(zeroed, 16 * 4 * NT)
                pool.wait_ge(bias_loaded, 16)
                pool.memset(biasx[:, REL:EXT], 0.0).then_inc(bias_ready, 1)
                pool.wait_ge(bias_ready, 1)
                pool.tensor_scalar(biasx[:, REL:EXT], biasx[:, REL:EXT], biasx[:, REL - 1:REL], None, ALU.add)\
                    .then_inc(bias_ready, 1)

            @block.tensor
            def _(pe):
                def groups(n, u, m):
                    pe.wait_ge(xT_scaled, n + 1)
                    for g in range(NGRP):
                        wait(pe, group_taken, 7 * n + FREE[g])
                        pe.wait_ge(w_loaded[g], 16)
                        for k in range(KD):
                            mm = pe.matmul(zp[:, BANK[g], 0:WG[g]], xT[:, u, k, :],
                                           w_in[:, k, 512 * g:512 * g + WG[g]], start=(k == 0), stop=(k == KD - 1))
                        mm.then_inc(group_done, 1)

                def turn(n, u, m):
                    pe.wait_ge(z_ready, n + 1)
                    wait(pe, turned_taken, 4 * n)
                    for b in range(4):
                        for j in range(4):
                            col = D * (b // 2) + 512 * (b % 2) + P * j
                            mm = pe.transpose(tp[:, b, P * j:P * j + P], z[:, u, col:col + P], c["ident"][:, :])
                        if b == 3:
                            mm = pe.transpose(lp[0:HA, 0:P], logf[:, u, :], c["ident"][:, :])
                        mm.then_inc(turned, 1)

                groups(0, 0, 0)
                groups(1, 1, 0)
                turn(0, 0, 0)
                with pe.Fori(1, NT // 2) as m:
                    groups(2 * m, 0, m)
                    turn(2 * m - 1, 1, m - 1)
                    groups(2 * m + 1, 1, m)
                    turn(2 * m, 0, m)
                groups(8, 0, 4)
                turn(7, 1, 3)
                turn(8, 0, 4)

            @block.scalar
            def _(act):
                act.preload_act_table_set("natural_log_exp_and_others")
                PER = 6

                def tile(n, u, m):
                    s = Steps(act, act_chain, PER * n)
                    act.wait_ge(x_loaded[u], 32 * (m + 1))
                    s.then(act.activation(sqx[:, :], xr[:, u, :], ACT.Square, accum_out=ssx[:, u, 0:1]))
                    s.then(act.activation(ssx[:, u, 1:2], ssx[:, u, 0:1], ACT.Ln, bias=c["eps"][:, :], scale=1.0 / D))
                    s.then(act.activation(ssx[:, u, 0:1], ssx[:, u, 1:2], ACT.Exp, scale=-0.5))
                    wait(act, z_stored[u], 48 * m)
                    wait(act, turned, 4 * (n - 1))
                    for g in range(NGRP):
                        act.wait_ge(group_done, 7 * n + g + 1)
                        act.activation(z[:, u, 512 * g:512 * g + WG[g]], zp[:, BANK[g], 0:WG[g]], ACT.Copy,
                                       scale=ssx[:, u, 0:1]).then_inc(group_taken, 1)
                    act.wait_ge(squares_ready, n + 1)
                    s.then(act.activation(hss[:, 1, :], hss[:, 0, :], ACT.Ln, bias=c["eps"][:, :], scale=1.0 / HD))
                    act.activation(hss[:, 1, :], hss[:, 1, :], ACT.Exp, scale=-0.5).then_inc(heads_scaled, 1)
                    act.wait_ge(gates_in, n + 1)
                    s.then(act.activation(lft[:, 1, :], lft[:, 0, :], ACT.Abs))
                    s.then(act.activation(lft[:, 1, :], lft[:, 1, :], ACT.Exp, scale=-1.0))
                    act.activation(lft[:, 2, :], lft[:, 1, :], ACT.Ln, bias=c["one"][:, :]).then_inc(gates_log, 1)
                    assert s.n == PER
                over_tiles(act, tile)

            @block.vector
            def _(dve):
                dve.wait_ge(small_loaded, 16 * 5)
                first = Steps(dve, grow_ready, 0)
                for i in range(2):
                    for lo, n in GROUPS[:2]:
                        for h in range(1, n):
                            dve.tensor_copy(grow[:, i, HD * (lo + h):HD * (lo + h + 1)], grow[:, i, HD * lo:HD * lo + HD])
                first.then(dve.memset(grow[:, :, HD * (HA + HB):D], 1.0))
                first.then(dve.tensor_scalar(grow[:, 0, :], grow[:, 0, :], SCALE, None, ALU.mult))
                PER = 4
                NQ = (HA + HB) * HD

                def tile(n, u, m):
                    s = Steps(dve, dve_chain, PER * n)
                    zv = z[:, u, 0:2 * D].rearrange("p (a c) -> p a c", a=2)
                    act_groups = 7 * n + 7
                    dve.wait_ge(group_taken, act_groups)
                    s.then(dve.tensor_tensor(sq[:, :, :], zv[:, :, 0:NQ], zv[:, :, 0:NQ], ALU.mult))
                    dve.tensor_reduce(hss[:, 0, :], sq[:, :, :].rearrange("p a (h d) -> p (a h) d", d=HD),
                                      AX.X, ALU.add).then_inc(squares_ready, 1)
                    dve.tensor_tensor(lft[:, 0, :], z[:, u, 3 * D:DIN], bf[:, :], ALU.add).then_inc(gates_in, 1)
                    dve.wait_ge(heads_scaled, n + 1)
                    for i in range(2):
                        hv = zv[:, i, 0:NQ].rearrange("p (h d) -> p h d", d=HD)
                        ins = dve.tensor_tensor(hv, hv, hss[:, 1, 11 * i:11 * i + 11].unsqueeze(2).to_broadcast([P, 11, HD]),
                                                ALU.mult)
                        s.then(ins)
                    dve.tensor_tensor(zv, zv, grow[:, :, :], ALU.mult)
                    dve.wait_ge(gates_log, n + 1)
                    s.then(dve.tensor_scalar(lft[:, 0, :], lft[:, 0, :], 0.0, None, ALU.min))
                    wait(dve, z_stored[u], 48 * m)
                    dve.tensor_tensor(logf[:, u, :], lft[:, 0, :], lft[:, 2, :], ALU.subtract).then_inc(z_ready, 1)
                    assert s.n == PER

                def copies(n, u, m):
                    wait(dve, qkT_stored, 16 * n)
                    for b in range(4):
                        dve.wait_ge(turned, 4 * n + b + 1)
                        if b == 3:
                            dve.tensor_copy(lfT[:, ds(n * P, P)], lp[0:HA, 0:P])
                        dve.tensor_copy(qkT[:, 4 * b:4 * b + 4, :].rearrange("p j n -> p (j n)"), tp[:, b, :])\
                           .then_inc(turned_taken, 1)

                tile(0, 0, 0)
                tile(1, 1, 0)
                copies(0, 0, 0)
                with dve.Fori(1, NT // 2) as m:
                    tile(2 * m, 0, m)
                    copies(2 * m - 1, 1, m - 1)
                    tile(2 * m + 1, 1, m)
                    copies(2 * m, 0, m)
                tile(8, 0, 4)
                copies(7, 1, 3)
                copies(8, 0, 4)
                last = Steps(dve, dve_chain, PER * NT)
                last.then(dve.memset(ones[:, :], 1.0))
                dve.wait_ge(turned_taken, 4 * NT)
                last.then(dve.tensor_tensor_scan(cp[:, 0, :], ones[0:HA, :], lfT[:, 0:SEQ], 0.0, ALU.mult, ALU.add))
                dve.wait_ge(lc_loaded, 16)
                dve.wait_ge(lc_back, 16)
                last.then(dve.tensor_tensor_scan(cs[:, 0, :], ones[0:HA * NB, 0:PAST + TS], lc[:, :], 0.0,
                                                 ALU.mult, ALU.add))
                dve.tensor_scalar(cp[:, 1, :], cp[:, 0, :], -1.0, None, ALU.mult)
                dve.tensor_scalar(cs[:, 1, :], cs[:, 0, :], -1.0, None, ALU.mult).then_inc(sums_ready, 1)

    return used


def over_units(e, heads, count, emit):
    def steps(k, u, m):
        return [(k, u, m, i) for i in range(count)]

    with e.Fori(0, heads // 2) as m:
        emit(steps(2 * m, 0, m) + steps(2 * m + 1, 1, m))
    if heads % 2:
        emit(steps(heads - 1, 0, heads // 2))


def load_head(sp, own, a, dram, h, k, L, head_free, qT, kT, v, ckT, cv, q2):
    wait(sp, head_free, k + 1, own)
    sp.dma_start(qT[0:HD, :], dram["q_heads"][ds(h, 1)].rearrange("a p n -> (a p) n")).then_inc(L, 16)
    sp.dma_start(kT[0:HD, :], dram["k_heads"][ds(h, 1)].rearrange("a p n -> (a p) n")).then_inc(L, 16)
    sp.dma_start(v[:, :, :], a["v_all"].rearrange("(n p) w -> p n w", p=P)[:, :, ds(h * HD, HD)]).then_inc(L, 16)
    sp.dma_start(ckT[:, :, :], a["cache_kT"][ds(h, 1)].rearrange("a p j n -> (a p) j n")).then_inc(L, 16)
    sp.dma_start(cv[:, :, :, :], a["cache_v"][ds(h, 1)].rearrange("a p b t d -> (a p) b t d")).then_inc(L, 16)
    for half in range(2):
        sp.dma_start(q2[HD * half:HD * half + HD, :],
                     dram["q_heads"][ds(h, 1), :, SEQ:TOK].rearrange("a p n -> (a p) n")).then_inc(L, 16)


def sample_values(pe, c, out, outT_col, out_col, probT, pt_new, pt_past, v, cv, oT, oT_done, oT_copied, k, own):
    pe.matmul(out[0:HD, outT_col:outT_col + P], v[:, QT, :], pt_new, start=True, stop=False, skip_group_check=True)
    for kt in range(PT):
        for b in range(NB):
            mm = pe.matmul(out[0:HD, outT_col + TS * b:outT_col + TS * b + TS], cv[:, b, kt, :],
                           pt_past(kt, b), start=False, stop=(kt == PT - 1 and b == NB - 1), skip_group_check=True)
    mm.then_inc(oT_done, 1)
    wait(pe, oT_copied, k + 1, own)
    return pe.transpose(out[:, out_col:out_col + HD], oT[:, :], c["ident"][0:HD, 0:HD])


def attention(nc, c, a, dram, merged, band):
    h0, nh = GROUPS[1] if band else GROUPS[0]
    name = "band_" if band else "forget_"
    with ExitStack() as ctx:
        sb = lambda n, s, d=F32: ctx.enter_context(nc.sbuf_tensor(name + n, s, d))
        ps = lambda n, s: ctx.enter_context(nc.psum_tensor(name + n, s, F32))
        sem = lambda n: ctx.enter_context(nc.semaphore(name + n))
        two = range(2)
        qT = [sb(f"qT{u}", [HD + 2, TOK]) for u in two]
        kT = [sb(f"kT{u}", [HD + 2, TOK]) for u in two]
        v = [sb(f"v{u}", [P, NT, HD]) for u in two]
        ckT = [sb(f"ckT{u}", [P, NB // 2, PAST]) for u in two]
        cv = [sb(f"cv{u}", [P, NB, PT, HD]) for u in two]
        q2 = [sb(f"q2{u}", [P, NB * TS]) for u in two]
        qm = [sb(f"qm{u}", [P, PT * 160]) for u in two]
        if band:
            near = [sb(f"near{u}", [P, 3, P]) for u in two]
            short1 = [sb(f"short1{u}", [TS, TS]) for u in two]
            short = [sb(f"short{u}", [TS, P]) for u in two]
            flip16 = sb("flip16", [TS, P])
        else:
            srow = [sb(f"srow{u}", [NB + 1, P]) for u in two]
            crow = [sb(f"crow{u}", [NB + 1, PAST]) for u in two]
        prob = sb("prob", [P, 2, SEQ])
        probT = sb("probT", [P, 2, QT, P])
        stat = sb("stat", [P, 3, 4])
        oT = sb("oT", [HD, P])
        score = ps("score", [P, 2, SEQ])
        tp = ps("turn", [P, 2, 512])
        op = ps("out", [P, 2, 512])

        blocks = [list(range(max(0, i - PT) if band else 0, i + 1)) for i in reversed(range(QT))]
        blocks.append(list(range(PT + 1)))
        NU = len(blocks)
        chunks = [(len(b) + 3) // 4 for b in blocks]
        before = [sum(chunks[:i]) for i in range(NU)]
        NCH = sum(chunks)
        assert NCH % 2 == 0 and NU % 3 == 0

        own, pe_turns, pool_turns = sem("sp_turns"), sem("pe_turns"), sem("pool_turns")
        once = sem("once")
        ready = sem("ready")
        loaded = [sem(f"loaded{u}") for u in two]
        head_free = sem("head_free")
        masked = sem("masked")
        scored = sem("scored")
        maxed = sem("maxed")
        expd = sem("expd")
        turned = sem("turned")
        copied = sem("copied")
        summed = sem("summed")
        written = sem("written")
        oT_done = sem("oT_done")
        oT_copied = sem("oT_copied")
        dve_chain = sem("dve_chain")
        pool_chain = sem("pool_chain")
        NL = 11

        slot = lambda u, i: (u * NU + i) % 2

        with nc.Block() as block:
            @block.sync
            def _(sp):
                sp.sem_inc(head_free, 2)
                sp.wait_ge(ready, 1)

                def head(k, u, m):
                    h = h0 + k
                    L = loaded[u]
                    load_head(sp, own, a, dram, h, k, L, head_free, qT[u], kT[u], v[u], ckT[u], cv[u], q2[u])
                    if band:
                        sp.dma_start(kT[u][HD:HD + 1, :], dram["bias"][ds(k, 1), REL:REL + TOK]).then_inc(L, 16)
                        row = dram["bias_hankel"][ds(k, 1)].rearrange("a p n -> (a p) n")
                        for j in two:
                            sp.dma_start(near[u][:, j, :], row[:, 1 + P * j:1 + P * j + P]).then_inc(L, 16)
                        sp.dma_start(short1[u][:, :], row[0:TS, P - TS + 1:P + 1]).then_inc(L, 16)
                    else:
                        sp.dma_start(kT[u][HD:HD + 1, :], dram["c"][1, ds(h, 1), :]).then_inc(L, 16)
                        sp.dma_start(qT[u][HD + 1:HD + 2, :], dram["c"][0, ds(h, 1), :]).then_inc(L, 16)
                        sp.dma_start(crow[u][0:NB, :], dram["c_past"][ds(h, 1)].rearrange("a b n -> (a b) n")).then_inc(L, 16)
                        sp.dma_start(srow[u][NB:NB + 1, :], dram["c"][0, ds(h, 1), SEQ:TOK]).then_inc(L, 16)
                over_heads(sp, nh, head)

            @block.gpsimd
            def _(pool):
                s = Steps(pool, once, 0)
                for u in two:
                    s.then(pool.memset(qm[u][:, :], 0.0))
                    s.then(pool.memset(qT[u][HD:HD + 2, :], 1.0))
                    s.then(pool.memset(kT[u][HD:HD + 2, :], 1.0))
                    if not band:
                        s.then(pool.memset(crow[u][:, :], 1.0))
                        s.then(pool.memset(srow[u][:, :], 1.0))
                        sv = srow[u][0:NB, :].rearrange("p (b t) -> p b t", t=TS)
                        s.then(pool.affine_select(out=sv, in_=sv, compare_op=ALU.is_equal, fill=0.0, base=0,
                                                  pattern=[[-1, NB], [0, TS]], channel_multiplier=1))
                if band:
                    s.then(pool.memset(flip16[:, :], 1.0))
                    fv = flip16[:, :].rearrange("p (b t) -> p b t", t=TS)
                    s.then(pool.affine_select(out=fv, in_=fv, compare_op=ALU.is_equal, fill=0.0, base=-(TS - 1),
                                              pattern=[[0, NB], [1, TS]], channel_multiplier=1))
                pool.sem_inc(ready, 1)

                def head(k, u, m):
                    wait(pool, loaded[u], 16 * NL * (m + 1), pool_turns)
                    if band:
                        chain = Steps(pool, pool_chain, 2 * k, pool_turns)
                        chain.then(pool.tensor_copy(near[u][:, 2, :].rearrange("p (b t) -> p b t", t=TS),
                                                    near[u][:, 1, 0:TS].unsqueeze(1).to_broadcast([P, NB, TS])))
                        chain.then(pool.tensor_copy(short[u][:, :].rearrange("p (b t) -> p b t", t=TS),
                                                    short1[u][:, :].unsqueeze(1).to_broadcast([TS, NB, TS])))
                    for half in two:
                        dst = qm[u][HD * half:HD * half + HD, :].rearrange("p (j c) -> p j c", c=160)
                        src = q2[u][HD * half:HD * half + HD, :].rearrange("p (j c) -> p j c", c=2 * TS)
                        ins = pool.tensor_copy(dst[:, :, TS * half:TS * half + TS], src[:, :, TS * half:TS * half + TS])
                    ins.then_inc(masked, 1)
                    wait(pool, masked, k + 1, pool_turns)
                over_heads(pool, nh, head)

            @block.tensor
            def _(pe):
                pe.wait_ge(ready, 1)
                pe.sem_inc(turned, NCH)

                def mask(region, m, stop=True):
                    return pe.matmul(region, c["identb"][:, :], c[m][:, :], start=False, stop=stop, skip_group_check=True)

                def scores(k, u, m, i):
                    s = slot(u, i)
                    if i == 0:
                        pe.wait_ge(loaded[u], 16 * NL * (m + 1))
                        pe.wait_ge(masked, k + 1)
                    pe.wait_ge(expd, NU * k + i + 1)
                    if i == NU - 1:
                        past = score[:, s, 0:PAST]
                        for j in range(NB // 2):
                            pe.matmul(past, qm[u][:, P * j:P * j + P], ckT[u][:, j, :], start=(j == 0), stop=False,
                                      skip_group_check=True)
                        new = score[:, s, PAST:PAST + P]
                        if band:
                            far = PAST - P
                            pe.matmul(past[:, 0:far], qT[u][HD:HD + 1, SEQ:TOK], kT[u][HD:HD + 1, 0:far], start=False,
                                      stop=False, skip_group_check=True)
                            pe.matmul(past[:, far:PAST], near[u][:, 2, :], c["flip"][:, :], start=False, stop=True,
                                      skip_group_check=True)
                            pe.matmul(new, qT[u][0:HD, SEQ:TOK], kT[u][0:HD, SEQ:TOK], start=True, stop=False,
                                      skip_group_check=True)
                            pe.matmul(new, short[u][:, :], flip16[:, :], start=False, stop=False, skip_group_check=True)
                        else:
                            pe.matmul(past, srow[u][:, :], crow[u][:, :], start=False, stop=True, skip_group_check=True)
                            pe.matmul(new, qT[u][:, SEQ:TOK], kT[u][:, SEQ:TOK], start=True, stop=False,
                                      skip_group_check=True)
                        mask(new, "same_s" if band else "causal_s").then_inc(scored, 1)
                        return
                    q = QT - 1 - i
                    j0 = blocks[i][0]
                    for cc in range(chunks[i]):
                        part = blocks[i][4 * cc:4 * cc + 4]
                        col = lambda j: P * (j - j0)
                        far = [j for j in part if j < q - 1] if band else part
                        close = [j for j in part if j not in far]
                        start = True
                        for js, rows in ((far, HD + 1 if band else HD + 2), (close, HD)):
                            if js:
                                mm = pe.matmul(score[:, s, col(js[0]):col(js[-1]) + P], qT[u][0:rows, P * q:P * q + P],
                                               kT[u][0:rows, P * js[0]:P * js[-1] + P], start=start, stop=True,
                                               skip_group_check=True)
                                start = False
                        for j in close:
                            mm = pe.matmul(score[:, s, col(j):col(j) + P], near[u][:, q - j, :], c["flip"][:, :],
                                           start=False, stop=True, skip_group_check=True)
                        for j in part:
                            if j == q:
                                mm = mask(score[:, s, col(j):col(j) + P], "band_diag" if band else "causal")
                            elif band and j == q - PT:
                                mm = mask(score[:, s, col(j):col(j) + P], "band_far")
                    mm.then_inc(scored, 1)

                def turn(k, u, m, i):
                    s = slot(u, i)
                    pe.wait_ge(expd, NU * k + i + 1 + 2)
                    for cc in range(chunks[i]):
                        pe.wait_ge(copied, NCH * k + before[i] + cc + 1)
                        for j in range(4 * cc, min(4 * cc + 4, len(blocks[i]))):
                            mm = pe.transpose(tp[:, (before[i] + cc) % 2, P * (j % 4):P * (j % 4) + P],
                                              prob[:, s, P * j:P * j + P], c["ident"][:, :])
                        mm.then_inc(turned, 1)

                def values(k, u, m, i):
                    s = slot(u, i)
                    pe.wait_ge(written, NU * k + i + 1)
                    pe.wait_ge(copied, NCH * k + before[i] + chunks[i] + 2)
                    n = len(blocks[i])
                    if i == NU - 1:
                        mm = sample_values(pe, c, op[:, s, :], 0, P, probT, probT[:, s, PT, :],
                                           lambda kt, b: probT[:, s, kt, TS * b:TS * b + TS], v[u], cv[u],
                                           oT, oT_done, oT_copied, k, pe_turns)
                    else:
                        for x, j in enumerate(blocks[i]):
                            mm = pe.matmul(op[:, s, 0:HD], probT[:, s, x, :], v[u][:, j, :], start=(x == 0), stop=(x == n - 1))
                    mm.then_inc(summed, 1)

                def emit(steps):
                    scores(*steps[0])
                    for x, st in enumerate(steps):
                        if x + 1 < len(steps):
                            scores(*steps[x + 1])
                        turn(*st)
                        if x:
                            values(*steps[x - 1])
                    values(*steps[-1])
                over_units(pe, nh, NU, emit)

            @block.scalar
            def _(act):
                act.sem_inc(expd, 2)

                def emit(steps):
                    for k, u, m, i in steps:
                        s = slot(u, i)
                        w = P * len(blocks[i])
                        act.wait_ge(maxed, NU * k + i + 1)
                        act.wait_ge(turned, NCH * k + NCH + (before[i - 1] if i else before[NU - 1] - NCH))
                        act.activation(prob[:, s, 0:w], score[:, s, 0:w], ACT.Exp, bias=stat[:, i % 3, 1:2],
                                       accum_out=stat[:, i % 3, 2:3]).then_inc(expd, 1)
                over_units(act, nh, NU, emit)

            @block.vector
            def _(dve):
                dve.sem_inc(copied, 2)
                dve.sem_inc(summed, 2)
                dve.sem_inc(written, 2)

                def maxima(k, u, m, i, chain):
                    dve.wait_ge(scored, NU * k + i + 1)
                    chain.then(dve.tensor_reduce(stat[:, i % 3, 0:1], score[:, slot(u, i), 0:P * len(blocks[i])], AX.X, ALU.max))
                    dve.tensor_scalar(stat[:, i % 3, 1:2], stat[:, i % 3, 0:1], -1.0, None, ALU.mult).then_inc(maxed, 1)

                def copies(k, u, m, i, chain):
                    dve.wait_ge(summed, NU * k + i + 1)
                    for cc in range(chunks[i]):
                        n = min(4, len(blocks[i]) - 4 * cc)
                        dve.wait_ge(turned, NCH * k + NCH + before[i] + cc + 1)
                        dve.tensor_copy(probT[:, slot(u, i), 4 * cc:4 * cc + n, :].rearrange("p j n -> p (j n)"),
                                        tp[:, (before[i] + cc) % 2, 0:P * n]).then_inc(copied, 1)

                def write(k, u, m, i, chain):
                    s = slot(u, i)
                    if i == NU - 1:
                        dve.wait_ge(oT_done, k + 1)
                        dve.tensor_copy(oT[:, :], op[0:HD, s, 0:P]).then_inc(oT_copied, 1)
                    dve.wait_ge(summed, NU * k + i + 1 + 2)
                    if i == NU - 1:
                        dve.nop().then_inc(head_free, 1)
                    chain.then(dve.reciprocal(stat[:, i % 3, 3:4], stat[:, i % 3, 2:3]))
                    tile = QT if i == NU - 1 else QT - 1 - i
                    col = P if i == NU - 1 else 0
                    dve.tensor_scalar(merged[:, tile, ds(HD * (h0 + k), HD)], op[:, s, col:col + HD],
                                      stat[:, i % 3, 3:4], None, ALU.mult).then_inc(written, 1)

                def emit(steps):
                    chain = Steps(dve, dve_chain, 2 * NU * steps[0][0])
                    maxima(*steps[0], chain)
                    for x, st in enumerate(steps):
                        if x + 1 < len(steps):
                            maxima(*steps[x + 1], chain)
                        copies(*st, chain)
                        if x:
                            write(*steps[x - 1], chain)
                    write(*steps[-1], chain)
                    assert chain.n == 2 * len(steps)
                over_units(dve, nh, NU, emit)


def sticks(nc, c, a, dram, merged):
    h0, nh = GROUPS[2]
    name = "stick_"
    with ExitStack() as ctx:
        sb = lambda n, s, d=F32: ctx.enter_context(nc.sbuf_tensor(name + n, s, d))
        ps = lambda n, s: ctx.enter_context(nc.psum_tensor(name + n, s, F32))
        sem = lambda n: ctx.enter_context(nc.semaphore(name + n))
        two = range(2)
        qT = [sb(f"qT{u}", [HD, TOK]) for u in two]
        kT = [sb(f"kT{u}", [HD, TOK]) for u in two]
        v = [sb(f"v{u}", [P, NT, HD]) for u in two]
        ckT = [sb(f"ckT{u}", [P, NB // 2, PAST]) for u in two]
        cv = [sb(f"cv{u}", [P, NB, PT, HD]) for u in two]
        q2 = [sb(f"q2{u}", [P, NB * TS]) for u in two]
        qm = [sb(f"qm{u}", [P, NB * TS]) for u in two]
        W = 512
        WS = P * (PT + 1)
        logs = sb("logs", [P, 2, W])
        soft = sb("soft", [P, 2, W])
        later = sb("later", [P, 2, W])
        wgt = sb("wgt", [P, 2, W])
        logs_s = sb("logs_s", [P, WS])
        soft_s = sb("soft_s", [P, WS])
        later_s = sb("later_s", [P, PT, P])
        wgt_s = sb("wgt_s", [P, WS])
        oT = sb("oT", [HD, P])
        zp = ps("z", [P, 4, W])
        zs = ps("zs", [P, 2 * W])
        op = ps("out", [P, 2, 512])
        S0 = 2 * W - WS

        units = [(4, j) for j in reversed(range(QT))] + [(0, j) for j in reversed(range(4))] + [None]
        NU = len(units)
        lo = [P * max(0, x[1] - x[0]) if x else 0 for x in units]
        diag = [x is not None and x[1] >= x[0] for x in units]
        first = [x is not None and x[1] == x[0] + 3 for x in units]
        last = [x is not None and x[1] == 0 for x in units]

        own, pe_turns, pool_turns = sem("sp_turns"), sem("pe_turns"), sem("pool_turns")
        once = sem("once")
        ready = sem("ready")
        loaded = [sem(f"loaded{u}") for u in two]
        head_free = sem("head_free")
        masked = sem("masked")
        scored = sem("scored")
        logged = sem("logged")
        softened = sem("softened")
        carried = sem("carried")
        tailed = sem("tailed")
        weighed = sem("weighed")
        summed = sem("summed")
        written = sem("written")
        oT_done = sem("oT_done")
        oT_copied = sem("oT_copied")
        act_chain = sem("act_chain")
        dve_chain = sem("dve_chain")
        pool_chain = sem("pool_chain")
        NL = 7
        at = lambda k, i: NU * k + i

        with nc.Block() as block:
            @block.sync
            def _(sp):
                sp.sem_inc(head_free, 2)

                def head(k, u, m):
                    load_head(sp, own, a, dram, h0 + k, k, loaded[u], head_free, qT[u], kT[u], v[u], ckT[u], cv[u], q2[u])
                over_heads(sp, nh, head)

            @block.gpsimd
            def _(pool):
                pool.sem_inc(carried, 2)
                s = Steps(pool, once, 0)
                for u in two:
                    s.then(pool.memset(qm[u][:, :], 0.0))

                def queries(k, u, m):
                    wait(pool, loaded[u], 16 * NL * (m + 1), pool_turns)
                    for half in two:
                        view = lambda t: t[u][HD * half:HD * half + HD, :].rearrange("p (j c) -> p j c", c=2 * TS)[
                            :, :, TS * half:TS * half + TS]
                        ins = pool.tensor_copy(view(qm), view(q2))
                    ins.then_inc(masked, 1)
                    wait(pool, masked, k + 1, pool_turns)

                def carry(k, u, m, i, chain):
                    wait(pool, softened, at(k, i) + 1 + 2, pool_turns)
                    if units[i] is None:
                        chain.then(pool.tensor_copy(later_s[:, 0, :], soft_s[:, 0:P]))
                        for b in range(1, PT):
                            ins = pool.tensor_tensor(later_s[:, b, :], later_s[:, b - 1, :], soft_s[:, P * b:P * b + P], ALU.add)
                            if b < PT - 1:
                                chain.then(ins)
                        ins.then_inc(carried, 1)
                        wait(pool, carried, at(k, i) + 1 + 2, pool_turns)
                        return
                    wait(pool, tailed, at(k, i) + 2, pool_turns)
                    wait(pool, carried, at(k, i) + 2, pool_turns)
                    old, new, s_ = later[:, i % 2], later[:, (i + 1) % 2], soft[:, i % 2]
                    seen = W if first[i] else lo[i - 1]
                    if lo[i] < seen:
                        ins = pool.tensor_copy(new[:, lo[i]:seen], s_[:, lo[i]:seen])
                    if seen < W:
                        ins = pool.tensor_tensor(new[:, seen:W], old[:, seen:W], s_[:, seen:W], ALU.add)
                    ins.then_inc(carried, 1)

                def emit(steps):
                    chain = Steps(pool, pool_chain, (PT - 1) * steps[0][0], pool_turns)
                    for k, u, m, i in steps:
                        if i == 0:
                            queries(k, u, m)
                        carry(k, u, m, i, chain)
                    assert chain.n == (PT - 1) * (len(steps) // NU)
                over_units(pool, nh, NU, emit)

            @block.tensor
            def _(pe):
                pe.sem_inc(tailed, 2)
                pe.sem_inc(summed, 2)

                def scores(k, u, m, i):
                    if i == 0:
                        pe.wait_ge(loaded[u], 16 * NL * (m + 1))
                        pe.wait_ge(masked, k + 1)
                    pe.wait_ge(weighed, at(k, i) + 1)
                    if units[i] is None:
                        pe.matmul(zs[:, S0:W], kT[u][:, SEQ:TOK], qT[u][:, SEQ:TOK], start=True, stop=True,
                                  skip_group_check=True)
                        for b in range(PT):
                            for j in range(NB // 2):
                                mm = pe.matmul(zs[:, W + P * b + 2 * TS * j:W + P * b + 2 * TS * (j + 1)],
                                               ckT[u][:, j, P * (PT - 1 - b):P * (PT - b)], qm[u][:, 2 * TS * j:2 * TS * (j + 1)],
                                               start=(b == 0 and j == 0), stop=True, skip_group_check=True)
                    else:
                        q0, j = units[i]
                        mm = pe.matmul(zp[:, i % 4, lo[i]:W], kT[u][:, P * j:P * j + P], qT[u][:, P * q0 + lo[i]:P * q0 + W],
                                       start=True, stop=True, skip_group_check=True)
                    mm.then_inc(scored, 1)

                def add(region, lhsT, rhs):
                    return pe.matmul(region, lhsT, rhs, start=False, stop=True, skip_group_check=True)

                def tails(k, u, m, i):
                    pe.wait_ge(softened, at(k, i) + 1 + 2)
                    if units[i] is None:
                        add(zs[:, S0:W], c["identb"][:, :], c["stick_s"][:, :])
                        add(zs[:, S0:W], c["negtri"][:, :], soft_s[:, 0:P])
                        add(zs[:, W:2 * W], c["negtri"][:, :], soft_s[:, P:WS])
                        pe.wait_ge(carried, at(k, i) + 1 + 2)
                        mm = add(zs[:, W:2 * W], c["negones"][:, :], later_s[:, :, :].rearrange("p b n -> p (b n)"))
                    else:
                        z = zp[:, i % 4, :]
                        if diag[i]:
                            add(z[:, lo[i]:lo[i] + P], c["identb"][:, :], c["stick"][:, :])
                        mm = add(z[:, lo[i]:W], c["negtri"][:, :], soft[:, i % 2, lo[i]:W])
                        if not first[i]:
                            pe.wait_ge(carried, at(k, i) + 2)
                            mm = add(z[:, lo[i - 1]:W], c["negones"][:, :], later[:, i % 2, lo[i - 1]:W])
                    mm.then_inc(tailed, 1)

                def values(k, u, m, i):
                    pe.wait_ge(weighed, at(k, i) + 1 + 4)
                    if units[i] is None:
                        pe.wait_ge(written, 3 * k + 1 + 1)
                        mm = sample_values(pe, c, op[:, 0, :], 0, P, None, wgt_s[:, 0:P],
                                           lambda kt, b: wgt_s[:, P * (PT - kt) + TS * b:P * (PT - kt) + TS * b + TS],
                                           v[u], cv[u], oT, oT_done, oT_copied, k, pe_turns)
                    else:
                        q0, j = units[i]
                        if first[i]:
                            pe.wait_ge(written, 3 * k + 1)
                        for t in range(max(j - q0, 0), 4):
                            mm = pe.matmul(op[:, 1 if q0 == 0 else 0, HD * t:HD * t + HD], wgt[:, i % 2, P * t:P * t + P],
                                           v[u][:, j, :], start=first[i], stop=last[i], skip_group_check=True)
                    mm.then_inc(summed, 1)

                def emit(steps):
                    n = len(steps)
                    scores(*steps[0])
                    scores(*steps[1])
                    for x in range(n):
                        if x + 2 < n:
                            scores(*steps[x + 2])
                        tails(*steps[x])
                        if x:
                            values(*steps[x - 1])
                    values(*steps[-1])
                over_units(pe, nh, NU, emit)

            @block.scalar
            def _(act):
                act.sem_inc(weighed, 4)

                def parts(i, t, ts):
                    return ts[:, :] if units[i] is None else t[:, i % 2, lo[i]:W]

                def z_of(i):
                    return zs[:, S0:2 * W] if units[i] is None else zp[:, i % 4, lo[i]:W]

                def logarithms(k, u, m, i, chain):
                    act.wait_ge(scored, at(k, i) + 1)
                    act.wait_ge(softened, at(k, i) + 1)
                    t = parts(i, logs, logs_s)
                    chain.then(act.activation(t, z_of(i), ACT.Abs))
                    chain.then(act.activation(t, t, ACT.Exp, scale=-1.0))
                    act.activation(t, t, ACT.Ln, bias=c["one"][:, :]).then_inc(logged, 1)

                def weights(k, u, m, i):
                    act.wait_ge(tailed, at(k, i) + 1 + 2)
                    act.wait_ge(summed, at(k, i) + 1)
                    act.activation(parts(i, wgt, wgt_s), z_of(i), ACT.Exp).then_inc(weighed, 1)

                def emit(steps):
                    chain = Steps(act, act_chain, 2 * NU * steps[0][0])
                    logarithms(*steps[0], chain)
                    for x, st in enumerate(steps):
                        if x + 1 < len(steps):
                            logarithms(*steps[x + 1], chain)
                        weights(*st)
                    assert chain.n == 2 * len(steps)
                over_units(act, nh, NU, emit)

            @block.vector
            def _(dve):
                dve.sem_inc(softened, 2)
                dve.sem_inc(written, 1)

                def soften(k, u, m, i, chain):
                    dve.wait_ge(logged, at(k, i) + 1)
                    dve.wait_ge(tailed, at(k, i) + 1)
                    dve.wait_ge(carried, at(k, i) + 1)
                    if units[i] is None:
                        z, t, s_, keep = zs[:, S0:2 * W], logs_s[:, :], soft_s[:, :], "keep_stick_s"
                    else:
                        z, t, s_, keep = zp[:, i % 4, lo[i]:W], logs[:, i % 2, lo[i]:W], soft[:, i % 2, lo[i]:W], "keep_stick"
                    ins = dve.scalar_tensor_tensor(out=s_, in0=z, scalar=0.0, in1=t, op0=ALU.max, op1=ALU.add)
                    if units[i] is None or diag[i]:
                        chain.then(ins)
                        ins = dve.tensor_tensor(s_[:, 0:P], s_[:, 0:P], c[keep][:, :], ALU.mult)
                    ins.then_inc(softened, 1)

                def write(k, u, m, i):
                    if units[i] is None:
                        dve.wait_ge(oT_done, k + 1)
                        dve.tensor_copy(oT[:, :], op[0:HD, 0, 0:P]).then_inc(oT_copied, 1)
                    elif not last[i]:
                        return
                    dve.wait_ge(summed, at(k, i) + 1 + 2)
                    cols = ds(HD * (h0 + k), HD)
                    if units[i] is None:
                        dve.nop().then_inc(head_free, 1)
                        ins = dve.tensor_copy(merged[:, QT, cols], op[:, 0, P:P + HD])
                    else:
                        q0 = units[i][0]
                        ins = dve.tensor_copy(merged[:, q0:q0 + 4, cols],
                                              op[:, 1 if q0 == 0 else 0, 0:4 * HD].rearrange("p (t d) -> p t d", d=HD))
                    ins.then_inc(written, 1)

                ND = sum(diag) + 1

                def emit(steps):
                    chain = Steps(dve, dve_chain, ND * steps[0][0])
                    soften(*steps[0], chain)
                    for x in range(len(steps)):
                        if x + 1 < len(steps):
                            soften(*steps[x + 1], chain)
                        if x:
                            write(*steps[x - 1])
                    write(*steps[-1])
                    assert chain.n == ND * (len(steps) // NU)
                over_units(dve, nh, NU, emit)


BLOCKS = (2 * TOK - NE) // P + NE
PAIRS = (BLOCKS + 1) // 2
LEAST_PAIRS = TOK // P
SLOTBLOCKS = 2 * PAIRS + 2
assert SLOTBLOCKS == 4 * NT


def shift(n, u, m, d):
    if d < 0:
        return (n - 1, 0, m) if u else (n - 1, 1, m - 1)
    return (n + 1, 0, m + 1) if u else (n + 1, 1, m)


def over_tile_steps(e, step):
    step(0, 0, 0)
    step(1, 1, 0)
    with e.Fori(1, NT // 2) as m:
        step(2 * m, 0, m)
        step(2 * m + 1, 1, m)
    step(NT - 1, 0, NT // 2)
    step(NT, 1, NT // 2)


def among(x):
    return not isinstance(x, int) or 0 <= x < NT


def mixing(nc, c, a, dram, merged, h, xn, logits, released):
    with ExitStack() as ctx:
        sb = lambda n, s, d=F32: ctx.enter_context(nc.sbuf_tensor("mix_" + n, s, d))
        ps = lambda n, s: ctx.enter_context(nc.psum_tensor("mix_" + n, s, F32))
        sem = lambda n: ctx.enter_context(nc.semaphore("mix_" + n))
        two = range(2)
        w_out = sb("w_out", [P, KD, D])
        w_r = sb("w_r", [P, KD, NG + NE])
        b_r = sb("b_r", [P, NG + NE])
        gmo = sb("gmo", [P, D])
        gff = sb("gff", [P, D])
        xr = sb("xr", [P, 2, D])
        m2 = sb("m2", [P, D])
        mT = [sb(f"mT{u}", [P, KD, P]) for u in two]
        xT = sb("xT", [P, KD, P])
        sq = sb("sq", [P, D])
        sm = sb("sm", [P, 2, 3])
        sh = sb("sh", [P, 2])
        tm = ps("tm", [P, 2, 512])
        tx = ps("tx", [P, 2, 512])
        om = ps("om", [P, 2, 512])
        lg = ps("lg", [P, 512])

        own = sem("sp_turns")
        small = sem("small")
        w_loaded = [sem(f"w_loaded{i}") for i in two]
        x_loaded = [sem(f"x_loaded{u}") for u in two]
        act_chain = sem("act_chain")
        m_scale = sem("m_scale")
        m_normed = sem("m_normed")
        m_turned = sem("m_turned")
        m_copied = sem("m_copied")
        mixed = sem("mixed")
        h_ready = sem("h_ready")
        h_scale = sem("h_scale")
        x_normed = sem("x_normed")
        x_turned = sem("x_turned")
        x_copied = sem("x_copied")
        routed = sem("routed")
        logits_ready = sem("logits_ready")
        xs = sb("xs", [P, D])
        x_staged = sem("x_staged")
        row_chain = sem("row_chain")

        with nc.Block() as block:
            @block.sync
            def _(sp):
                wv = a["w_out"].rearrange("(k p) n -> p k n", p=P)
                for i in two:
                    sp.dma_start(w_out[:, :, 512 * i:512 * i + 512], wv[:, :, 512 * i:512 * i + 512]).then_inc(w_loaded[i], 16)
                sp.dma_start(gmo[:, :], a["g_mix_out"].partition_broadcast(P)).then_inc(small, 16)
                sp.dma_start(gff[:, :], a["norm_ffn"].partition_broadcast(P)).then_inc(small, 16)
                sp.dma_start(w_r[:, :, :], a["w_router"].rearrange("(k p) n -> p k n", p=P)).then_inc(small, 16)
                sp.dma_start(b_r[:, :], a["b_router"].partition_broadcast(P)).then_inc(small, 16)

                def load(n, u, m):
                    wait(sp, h_ready, n - 1, own)
                    sp.dma_start(xr[:, u, :], a["x"][ds(n * P, P), :]).then_inc(x_loaded[u], 16)
                over_tiles(sp, load)

            @block.tensor
            def _(pe):
                def turn(src, dst, ready, copied, n, done):
                    pe.wait_ge(ready, n + 1)
                    for half in two:
                        wait(pe, copied, 2 * (n - 1) + half + 1)
                        for j in range(4 * half, 4 * half + 4):
                            mm = pe.transpose(dst[:, half, P * (j % 4):P * (j % 4) + P], src(j), c["ident"][:, :])
                        mm.then_inc(done, 1)

                def mix(n, u, m):
                    for half in two:
                        pe.wait_ge(m_copied, 2 * n + 2)
                        wait(pe, h_ready, n)
                        pe.wait_ge(w_loaded[half], 16)
                        for k in range(KD):
                            mm = pe.matmul(om[:, half, :], mT[u][:, k, :], w_out[:, k, 512 * half:512 * half + 512],
                                           start=(k == 0), stop=(k == KD - 1))
                    mm.then_inc(mixed, 1)

                def route(n):
                    pe.wait_ge(x_copied, 2 * n + 2)
                    wait(pe, logits_ready, n)
                    for k in range(KD):
                        mm = pe.matmul(lg[:, 0:NG + NE], xT[:, k, :], w_r[:, k, :], start=(k == 0), stop=(k == KD - 1))
                    mm.then_inc(routed, 1)

                def step(n, u, m):
                    if among(n):
                        mix(n, u, m)
                    if among(n - 1):
                        turn(lambda j: xs[:, P * j:P * j + P], tx, x_staged, x_copied, n - 1, x_turned)
                    if among(n + 1):
                        turn(lambda j: m2[:, P * j:P * j + P], tm, m_normed, m_copied, n + 1, m_turned)
                    if among(n - 1):
                        route(n - 1)
                pe.wait_ge(small, 64)
                turn(lambda j: m2[:, P * j:P * j + P], tm, m_normed, m_copied, 0, m_turned)
                over_tile_steps(pe, step)

            @block.scalar
            def _(act):
                PER = 6

                def group_scale(n, u, m):
                    s = Steps(act, act_chain, PER * n)
                    wait(act, m_normed, n - 1)
                    for g, (h0, nh) in enumerate(GROUPS):
                        s.then(act.activation(sq[:, 0:HD * nh], merged[:, ds(n, 1), HD * h0:HD * (h0 + nh)]
                                              .rearrange("p a w -> p (a w)"), ACT.Square, accum_out=sm[:, u, g:g + 1]))
                    s.then(act.activation(sm[:, u, 0:1], sm[:, u, 0:1], ACT.Ln, bias=c["eps"][:, :], scale=1.0 / (HD * HA)))
                    s.then(act.activation(sm[:, u, 1:3], sm[:, u, 1:3], ACT.Ln, bias=c["eps"][:, :], scale=1.0 / (HD * HB)))
                    s.then(act.activation(sm[:, u, :], sm[:, u, :], ACT.Exp, scale=-0.5))
                    act.sem_inc(m_scale, 1)
                    assert s.n == PER

                def row_scale(n, u, m):
                    s = Steps(act, row_chain, 2 * n)
                    act.wait_ge(h_ready, n + 1)
                    wait(act, x_normed, n - 1)
                    s.then(act.activation(sq[:, :], h[:, ds(n, 1), :].rearrange("p a w -> p (a w)"), ACT.Square,
                                          accum_out=sh[:, u:u + 1]))
                    s.then(act.activation(sh[:, u:u + 1], sh[:, u:u + 1], ACT.Ln, bias=c["eps"][:, :], scale=1.0 / D))
                    act.activation(sh[:, u:u + 1], sh[:, u:u + 1], ACT.Exp, scale=-0.5).then_inc(h_scale, 1)

                def copies(src, dst, turned, free, count, n, done):
                    for half in two:
                        act.wait_ge(turned, 2 * n + half + 1)
                        wait(act, free, count)
                        act.activation(dst[:, 4 * half:4 * half + 4, :].rearrange("p j n -> p (j n)"), src[:, half, :],
                                       ACT.Copy).then_inc(done, 1)

                def stage(n, u, m):
                    act.wait_ge(x_normed, n + 1)
                    wait(act, x_turned, 2 * n)
                    act.activation(xs[:, :], xn[:, ds(n, 1), :].rearrange("p a w -> p (a w)"), ACT.Copy).then_inc(x_staged, 1)

                def step(n, u, m):
                    if among(n - 1):
                        row_scale(*shift(n, u, m, -1))
                    if among(n + 1):
                        group_scale(*shift(n, u, m, 1))
                    if among(n - 1):
                        stage(*shift(n, u, m, -1))
                        copies(tx, xT, x_turned, routed, n - 1, n - 1, x_copied)
                    if among(n + 1):
                        copies(tm, mT[1 - u], m_turned, mixed, n, n + 1, m_copied)
                group_scale(0, 0, 0)
                copies(tm, mT[0], m_turned, mixed, 0, 0, m_copied)
                over_tile_steps(act, step)

            @block.vector
            def _(dve):
                dve.wait_ge(small, 64)

                def norm_heads(n, u, m):
                    dve.wait_ge(m_scale, n + 1)
                    wait(dve, m_turned, 2 * n)
                    for g, (h0, nh) in enumerate(GROUPS):
                        cols = slice(HD * h0, HD * (h0 + nh))
                        ins = dve.scalar_tensor_tensor(out=m2[:, cols], in0=merged[:, ds(n, 1), cols].rearrange("p a w -> p (a w)"),
                                                       scalar=sm[:, u, g:g + 1], in1=gmo[:, cols], op0=ALU.mult, op1=ALU.mult)
                    ins.then_inc(m_normed, 1)

                def norm_rows(n, u, m):
                    dve.wait_ge(h_scale, n + 1)
                    row = lambda t: t[:, ds(n, 1), :].rearrange("p a w -> p (a w)")
                    dve.scalar_tensor_tensor(out=row(xn), in0=row(h), scalar=sh[:, u:u + 1], in1=gff[:, :],
                                             op0=ALU.mult, op1=ALU.mult).then_inc(x_normed, 1)

                def residual(n, u, m):
                    dve.wait_ge(x_loaded[u], 16 * (m + 1))
                    dve.wait_ge(mixed, n + 1)
                    dve.tensor_tensor(h[:, ds(n, 1), :].rearrange("p a w -> p (a w)"), om[:, :, :].rearrange("p a w -> p (a w)"),
                                      xr[:, u, :], ALU.add).then_inc(h_ready, 1)

                def take_logits(n):
                    dve.wait_ge(routed, n + 1)
                    dve.tensor_tensor(logits[:, ds(n, 1), :].rearrange("p a w -> p (a w)"), lg[:, 0:NG + NE], b_r[:, :],
                                      ALU.add).then_inc(logits_ready, 1)

                def step(n, u, m):
                    if among(n - 1):
                        norm_rows(*shift(n, u, m, -1))
                    if among(n + 1):
                        norm_heads(*shift(n, u, m, 1))
                    if among(n):
                        residual(n, u, m)
                    if among(n - 1):
                        take_logits(n - 1)
                norm_heads(0, 0, 0)
                over_tile_steps(dve, step)

            @block.gpsimd
            def _(pool):
                for s in released:
                    pool.sem_clear(s)


def routing(nc, c, a, dram, xn, logits, gates, slots, owner):
    with ExitStack() as ctx:
        sb = lambda n, s, d=F32: ctx.enter_context(nc.sbuf_tensor("route_" + n, s, d))
        ps = lambda n, s: ctx.enter_context(nc.psum_tensor("route_" + n, s, F32))
        sem = lambda n: ctx.enter_context(nc.semaphore("route_" + n))
        I32 = mybir.dt.int32
        ge, gs, es, t4, gh, le, l2, oh1, oh2 = (sb(n, [P, NT, 4]) for n in
                                               ("ge", "gs", "es", "t4", "gh", "le", "l2", "oh1", "oh2"))
        m1, m2, pg, w1, den = (sb(n, [P, NT]) for n in ("m1", "m2", "pg", "w1", "den"))
        t16 = sb("t16", [P, NT, NG, EG])
        M1 = sb("M1", [P, NT, NG, EG])
        M2 = sb("M2", [P, NT, NG, EG])
        M = sb("M", [P, NT, NE])
        S = sb("S", [P, NT + 1, NE])
        pos = sb("pos", [P, NT, NE])
        cnt = sb("cnt", [P, NE])
        cmp = sb("cmp", [P, NE, NT])
        nb = sb("nb", [P, NE])
        cum = sb("cum", [P, NE])
        ones16 = sb("ones16", [P, NE])
        bcmp = sb("bcmp", [P, SLOTBLOCKS, NE])
        bown = sb("bown", [P, SLOTBLOCKS])
        half = sb("half", [P, 1])
        slotf = sb("slotf", [P, 2, NT])
        desc_i = sb("desc_i", [P, 4], I32)
        desc = sb("desc", [P, 4])
        step_i = sb("step_i", [P, NT], I32)
        steps_ = sb("steps", [P, NT])
        blk_i = sb("blk_i", [P, SLOTBLOCKS], I32)
        blk = sb("blk", [P, SLOTBLOCKS])
        rank = ps("rank", [P, 512])
        cp = ps("cp", [P, 512])
        iotas = sem("iotas")
        chain = sem("chain")
        to_act = sem("to_act")
        from_act = sem("from_act")
        counted = sem("counted")
        chosen = sem("chosen")
        placed = sem("placed")
        scattered = sem("scattered")

        with nc.Block() as block:
            @block.gpsimd
            def _(pool):
                pool.iota(desc_i[:, :], pattern=[[-1, 4]], base=4, channel_multiplier=0)
                pool.iota(step_i[:, :], pattern=[[P, NT]], base=0, channel_multiplier=0)
                pool.iota(blk_i[:, :], pattern=[[1, SLOTBLOCKS]], base=0, channel_multiplier=0).then_inc(iotas, 1)
                pool.wait_ge(placed, 1)
                for n in range(NT):
                    for k in range(2):
                        pool.indirect_dma_start(out=dram["grouped"],
                                                out_offset=bass.IndirectOffsetOnAxis(ap=slots[:, k, n:n + 1], axis=0),
                                                in_=xn[:, n, :], in_offset=None).then_inc(scattered, 16)
                pool.wait_ge(scattered, 16 * 2 * NT)

            @block.scalar
            def _(act):
                act.wait_ge(to_act, 1)
                act.activation(gs[:, :, :], ge[:, :, :], ACT.Exp).then_inc(from_act, 1)
                act.wait_ge(to_act, 2)
                act.activation(w1[:, :], m1[:, :], ACT.Exp).then_inc(from_act, 1)

            @block.tensor
            def _(pe):
                pe.wait_ge(chosen, 1)
                Mf = M[:, :, :].rearrange("p n e -> p (n e)")
                Sf = S[:, 0:NT, :].rearrange("p n e -> p (n e)")
                pe.matmul(rank[:, 0:NT * NE], c["keep_stick"][:, :], Mf, start=True, stop=False)
                pe.matmul(rank[:, 0:NT * NE], c["ones"][:, :], Sf, start=False, stop=True)
                pe.matmul(cp[:, 0:NE], c["ones"][:, :], S[:, NT, :], start=True, stop=True).then_inc(counted, 1)

            @block.vector
            def _(dve):
                s = Steps(dve, chain, 0)
                t = s.then
                bc = lambda x: x.unsqueeze(2).to_broadcast([P, NT, 4])
                G = logits[:, :, 0:NG]
                E4 = logits[:, :, NG:].rearrange("p n (g e) -> p n g e", e=EG)
                dve.wait_ge(iotas, 1)
                t(dve.tensor_copy(desc[:, :], desc_i[:, :]))
                t(dve.tensor_copy(steps_[:, :], step_i[:, :]))
                t(dve.tensor_copy(blk[:, :], blk_i[:, :]))
                desc_b = desc[:, :].unsqueeze(1).to_broadcast([P, NT, 4])

                def first_max(x, top, out):
                    t(dve.tensor_reduce(top[:, :], x, AX.X, ALU.max))
                    t(dve.tensor_tensor(t4[:, :, :], x, bc(top[:, :]), ALU.is_equal))
                    t(dve.tensor_tensor(t4[:, :, :], t4[:, :, :], desc_b, ALU.mult))
                    t(dve.tensor_reduce(den[:, :], t4[:, :, :], AX.X, ALU.max))
                    t(dve.tensor_tensor(out[:, :, :], t4[:, :, :], bc(den[:, :]), ALU.is_equal))

                first_max(G, m1, gh)
                t(dve.tensor_tensor(ge[:, :, :], G, bc(m1[:, :]), ALU.subtract))
                dve.sem_inc(to_act, 1)
                dve.wait_ge(from_act, 1)
                t(dve.tensor_reduce(pg[:, :], gs[:, :, :], AX.X, ALU.add))
                t(dve.reciprocal(pg[:, :], pg[:, :]))
                t(dve.tensor_tensor(t16[:, :, :, :], E4, gh[:, :, :].unsqueeze(3).to_broadcast([P, NT, NG, EG]), ALU.mult))
                t(dve.tensor_reduce(le[:, :, :], t16[:, :, :, :].rearrange("p n g e -> p n e g"), AX.X, ALU.add))
                first_max(le[:, :, :], m1, oh1)
                t(dve.scalar_tensor_tensor(out=l2[:, :, :].rearrange("p n e -> p (n e)"), in0=oh1[:, :, :].rearrange("p n e -> p (n e)"),
                                           scalar=NEG, in1=le[:, :, :].rearrange("p n e -> p (n e)"), op0=ALU.mult, op1=ALU.add))
                first_max(l2[:, :, :], m2, oh2)
                t(dve.tensor_tensor(m1[:, :], m2[:, :], m1[:, :], ALU.subtract))
                dve.sem_inc(to_act, 1)
                dve.wait_ge(from_act, 2)
                t(dve.tensor_scalar(den[:, :], w1[:, :], 1.0, None, ALU.add))
                t(dve.reciprocal(den[:, :], den[:, :]))
                t(dve.tensor_tensor(gates[:, 0, :], den[:, :], pg[:, :], ALU.mult))
                t(dve.tensor_tensor(gates[:, 1, :], gates[:, 0, :], w1[:, :], ALU.mult))
                for Mk, oh in ((M1, oh1), (M2, oh2)):
                    t(dve.tensor_tensor(Mk[:, :, :, :], gh[:, :, :].unsqueeze(3).to_broadcast([P, NT, NG, EG]),
                                        oh[:, :, :].unsqueeze(2).to_broadcast([P, NT, NG, EG]), ALU.mult))
                f = lambda x: x[:, :, :, :].rearrange("p n g e -> p n (g e)")
                t(dve.tensor_tensor(M[:, :, :], f(M1), f(M2), ALU.add))
                t(dve.memset(S[:, 0, :], 0.0))
                for n in range(NT):
                    t(dve.tensor_tensor(S[:, n + 1, :], S[:, n, :], M[:, n, :], ALU.add))
                dve.sem_inc(chosen, 1)
                dve.wait_ge(counted, 1)
                t(dve.tensor_copy(cnt[:, :], cp[:, 0:NE]))
                t(dve.memset(ones16[:, :], 1.0))
                t(dve.tensor_tensor(cmp[:, :, :], cnt[:, :].unsqueeze(2).to_broadcast([P, NE, NT]),
                                    steps_[:, :].unsqueeze(1).to_broadcast([P, NE, NT]), ALU.is_gt))
                t(dve.tensor_reduce(nb[:, :], cmp[:, :, :], AX.X, ALU.add))
                t(dve.tensor_tensor_scan(cum[:, :], ones16[:, :], nb[:, :], 0.0, ALU.mult, ALU.add))
                t(dve.tensor_tensor(bcmp[:, :, :], blk[:, :].unsqueeze(2).to_broadcast([P, SLOTBLOCKS, NE]),
                                    cum[:, :].unsqueeze(1).to_broadcast([P, SLOTBLOCKS, NE]), ALU.is_ge))
                t(dve.tensor_reduce(bown[:, :], bcmp[:, :, :], AX.X, ALU.add))
                t(dve.tensor_scalar(bown[:, :], bown[:, :], float(NE - 1), None, ALU.min))
                t(dve.tensor_copy(owner[:, 0:SLOTBLOCKS], bown[0:1, :]))
                t(dve.tensor_scalar(half[:, :], cum[:, NE - 1:NE], 0.5, 0.25 - LEAST_PAIRS, ALU.mult, ALU.add))
                t(dve.tensor_copy(owner[:, SLOTBLOCKS:SLOTBLOCKS + 1], half[0:1, :]))
                t(dve.tensor_tensor(cum[:, :], cum[:, :], nb[:, :], ALU.subtract))
                t(dve.tensor_scalar(cum[:, :], cum[:, :], float(P), None, ALU.mult))
                t(dve.tensor_tensor(pos[:, :, :], rank[:, 0:NT * NE].rearrange("p (n e) -> p n e", e=NE),
                                    cum[:, :].unsqueeze(1).to_broadcast([P, NT, NE]), ALU.add))
                for k, Mk in enumerate((M1, M2)):
                    t(dve.tensor_tensor(M[:, :, :], f(Mk), pos[:, :, :], ALU.mult))
                    t(dve.tensor_reduce(slotf[:, k, :], M[:, :, :], AX.X, ALU.add))
                    t(dve.tensor_copy(slots[:, k, :], slotf[:, k, :]))
                dve.sem_inc(placed, 1)


def log_sigmoid_parts(act, x, t, chain, done, one):
    chain.then(act.activation(t, x, ACT.Abs))
    chain.then(act.activation(t, t, ACT.Exp, scale=-1.0))
    act.activation(t, t, ACT.Ln, bias=one).then_inc(done, 1)


def experts(nc, c, a, dram, owner, wg):
    with ExitStack() as ctx:
        sb = lambda n, s, d=F32: ctx.enter_context(nc.sbuf_tensor("exp_" + n, s, d))
        ps = lambda n, s: ctx.enter_context(nc.psum_tensor("exp_" + n, s, F32))
        sem = lambda n: ctx.enter_context(nc.semaphore("exp_" + n))
        two = range(2)
        FT = DE // P
        wgu = [sb(f"wgu{u}", [P, KD, 2 * DE]) for u in two]
        wd = [sb(f"wd{u}", [P, FT, D]) for u in two]
        xg = [sb(f"xg{u}", [P, D]) for u in two]
        xT = [sb(f"xT{u}", [P, KD, P]) for u in two]
        logs = sb("logs", [P, DE])
        sig = sb("sig", [P, DE])
        sil = sb("sil", [P, DE])
        hid = [sb(f"hid{u}", [P, DE]) for u in two]
        hT = sb("hT", [P, FT, P])
        y = sb("y", [P, 2, D])
        tp = ps("tp", [P, 2, 512])
        gu = ps("gu", [P, 2, 512])
        th = ps("th", [P, 512])
        yp = ps("yp", [P, 2, 512])

        own, pool_turns = sem("sp_turns"), sem("pool_turns")
        up_loaded = [sem(f"up_loaded{u}") for u in two]
        down_loaded = [sem(f"down_loaded{u}") for u in two]
        x_loaded = [sem(f"x_loaded{u}") for u in two]
        turned = sem("turned")
        copied = sem("copied")
        upped = sem("upped")
        logged = sem("logged")
        summed = sem("summed")
        expd = sem("expd")
        hidden = sem("hidden")
        h_turned = sem("h_turned")
        h_copied = sem("h_copied")
        downed = sem("downed")
        y_taken = sem("y_taken")
        y_stored = [sem(f"y_stored{u}") for u in two]
        act_chain = sem("act_chain")
        dve_chain = sem("dve_chain")
        wg_loaded = sem("wg_loaded")

        def over_blocks(e, step):
            pairs = e.value_load(owner[0:1, SLOTBLOCKS:SLOTBLOCKS + 1], min_val=0, max_val=PAIRS - LEAST_PAIRS) + LEAST_PAIRS
            step(0, 0, 0, None)
            step(1, 1, 0, None)
            with e.Fori(1, pairs) as m:
                step(2 * m, 0, m, None)
                step(2 * m + 1, 1, m, None)
            step(2 * pairs, 0, pairs, "last")
            return pairs

        def behind(b):
            return not (isinstance(b, int) and b == 0)

        with nc.Block() as block:
            @block.sync
            def _(sp):
                wv = a["w_ple_gate"].rearrange("(k p) n -> p k n", p=P)

                def step(b, u, m, last):
                    if last is None:
                        e = sp.value_load(owner[0:1, ds(b, 1)], min_val=0, max_val=NE - 1)
                        wait(sp, upped, b - 1, own)
                        sp.dma_start(wgu[u][:, :, :], a["w_gu"][ds(e, 1)].rearrange("a p k f -> (a p) k f"))\
                          .then_inc(up_loaded[u], 16)
                        bb, uu, _ = shift(b, u, m, 1)
                        wait(sp, turned, 2 * b, own)
                        sp.dma_start(xg[uu][:, :], dram["grouped"][ds(bb * P, P), :]).then_inc(x_loaded[uu], 16)
                    if isinstance(b, int) and b < 2:
                        sp.dma_start(wg[:, :, 512 * b:512 * b + 512], wv[:, :, 512 * b:512 * b + 512]).then_inc(wg_loaded, 16)
                    if not (isinstance(b, int) and b < 2):
                        bb, uu, _ = b - 2, u, m - 1
                        wait(sp, y_taken, bb + 1, own)
                        sp.dma_start(dram["grouped"][ds(bb * P, P), :], y[:, uu, :]).then_inc(y_stored[uu], 16)
                    if last:
                        wait(sp, y_taken, b, own)
                        sp.dma_start(dram["grouped"][ds((b - 1) * P, P), :], y[:, 1, :]).then_inc(y_stored[1], 16)
                sp.dma_start(xg[0][:, :], dram["grouped"][0:P, :]).then_inc(x_loaded[0], 16)
                pairs = over_blocks(sp, step)
                for u in two:
                    wait(sp, y_stored[u], 16 * pairs, own)
                    wait(sp, x_loaded[u], 16 * (pairs + 1 - u), own)
                sp.wait_ge(wg_loaded, 32)

            @block.gpsimd
            def _(pool):
                def step(b, u, m, last):
                    if last is None:
                        e = pool.value_load(owner[0:1, ds(b, 1)], min_val=0, max_val=NE - 1)
                        wait(pool, downed, b - 1, pool_turns)
                        pool.dma_start(wd[u][:, :, :], a["w_ed"][ds(e, 1)].rearrange("a (f p) n -> p (a f) n", p=P))\
                            .then_inc(down_loaded[u], 16)
                over_blocks(pool, step)

            @block.tensor
            def _(pe):
                def turn(b, u, m):
                    pe.wait_ge(x_loaded[u], 16 * (m + 1))
                    for half in two:
                        wait(pe, copied, 2 * (b - 1) + half + 1)
                        for j in range(4 * half, 4 * half + 4):
                            mm = pe.transpose(tp[:, half, P * (j % 4):P * (j % 4) + P], xg[u][:, P * j:P * j + P], c["ident"][:, :])
                        mm.then_inc(turned, 1)

                def up(b, u, ks):
                    for k in ks:
                        mm = pe.matmul(gu[:, u, :], xT[u][:, k, :], wgu[u][:, k, :], start=(k == 0), stop=(k == KD - 1),
                                       skip_group_check=True)
                    return mm

                def step(b, u, m, last):
                    if last is None:
                        pe.wait_ge(copied, 2 * b + 2)
                        pe.wait_ge(up_loaded[u], 16 * (m + 1))
                        wait(pe, hidden, b - 1)
                        up(b, u, range(4))
                        turn(*shift(b, u, m, 1))
                        up(b, u, range(4, 6))
                    if behind(b):
                        bb, uu, m1 = shift(b, u, m, -1)
                        pe.wait_ge(hidden, bb + 1)
                        wait(pe, h_copied, bb)
                        for f in range(FT):
                            mm = pe.transpose(th[:, P * f:P * f + P], hid[uu][:, P * f:P * f + P], c["ident"][:, :])
                        mm.then_inc(h_turned, 1)
                    if last is None:
                        up(b, u, range(6, KD)).then_inc(upped, 1)
                    if behind(b):
                        pe.wait_ge(h_copied, bb + 1)
                        pe.wait_ge(down_loaded[uu], 16 * (m1 + 1))
                        wait(pe, y_taken, bb)
                        for half in two:
                            for f in range(FT):
                                mm = pe.matmul(yp[:, half, :], hT[:, f, :], wd[uu][:, f, 512 * half:512 * half + 512],
                                               start=(f == 0), stop=(f == FT - 1))
                        mm.then_inc(downed, 1)
                turn(0, 0, 0)
                over_blocks(pe, step)

            @block.scalar
            def _(act):
                def copies(b, u):
                    for half in two:
                        act.wait_ge(turned, 2 * b + half + 1)
                        wait(act, upped, b - 1)
                        act.activation(xT[u][:, 4 * half:4 * half + 4, :].rearrange("p j n -> p (j n)"), tp[:, half, :],
                                       ACT.Copy).then_inc(copied, 1)

                def step(b, u, m, last):
                    if behind(b):
                        bb, uu, _ = shift(b, u, m, -1)
                        s = Steps(act, act_chain, 2 * bb)
                        act.wait_ge(upped, bb + 1)
                        log_sigmoid_parts(act, gu[:, uu, 0:DE], logs[:, :], s, logged, c["one"][:, :])
                        act.wait_ge(summed, bb + 1)
                        act.activation(sig[:, :], logs[:, :], ACT.Exp).then_inc(expd, 1)
                    if last is None:
                        copies(b + 1, 1 - u)
                    if behind(b):
                        act.wait_ge(h_turned, bb + 1)
                        wait(act, downed, bb)
                        act.activation(hT[:, :, :].rearrange("p f n -> p (f n)"), th[:, 0:DE], ACT.Copy).then_inc(h_copied, 1)
                copies(0, 0)
                over_blocks(act, step)

            @block.vector
            def _(dve):
                def step(b, u, m, last):
                    if not behind(b):
                        return
                    bb, uu, m1 = shift(b, u, m, -1)
                    s = Steps(dve, dve_chain, bb)
                    dve.wait_ge(logged, bb + 1)
                    dve.scalar_tensor_tensor(out=logs[:, :], in0=gu[:, uu, 0:DE], scalar=0.0, in1=logs[:, :],
                                             op0=ALU.min, op1=ALU.subtract).then_inc(summed, 1)
                    dve.wait_ge(expd, bb + 1)
                    s.then(dve.tensor_tensor(sil[:, :], gu[:, uu, 0:DE], sig[:, :], ALU.mult))
                    wait(dve, h_turned, bb - 1)
                    dve.tensor_tensor(hid[uu][:, :], sil[:, :], gu[:, uu, DE:2 * DE], ALU.mult).then_inc(hidden, 1)
                    dve.wait_ge(downed, bb + 1)
                    wait(dve, y_stored[uu], 16 * m1)
                    dve.tensor_copy(y[:, uu, :], yp[:, :, :].rearrange("p a n -> p (a n)")).then_inc(y_taken, 1)
                over_blocks(dve, step)


def embedding(nc, c, a, dram, h, gates, slots, wg):
    with ExitStack() as ctx:
        sb = lambda n, s, d=F32: ctx.enter_context(nc.sbuf_tensor("ple_" + n, s, d))
        ps = lambda n, s: ctx.enter_context(nc.psum_tensor("ple_" + n, s, F32))
        sem = lambda n: ctx.enter_context(nc.semaphore("ple_" + n))
        two = range(2)
        KP = DP // P
        wp = sb("wp", [P, KP, D])
        gpl = sb("gpl", [P, D])
        pT = [sb(f"pT{u}", [P, KP, P]) for u in two]
        rows = [sb(f"rows{u}", [P, 2, D]) for u in two]
        hn = sb("hn", [P, D])
        hT = [sb(f"hT{u}", [P, KD, P]) for u in two]
        sq = sb("sq", [P, D])
        sh = sb("sh", [P, 2])
        eg = sb("eg", [P, D])
        t1 = sb("t1", [P, D])
        logs = sb("logs", [P, D])
        y = sb("y", [P, 2, D])
        tp = ps("tp", [P, 2, 512])
        gp = ps("gp", [P, 2, 2, 512])
        pp = ps("pp", [P, 2, 512])

        own = sem("sp_turns")
        small = sem("small")
        p_loaded = [sem(f"p_loaded{u}") for u in two]
        gathered = [sem(f"gathered{u}") for u in two]
        added = sem("added")
        scaled = sem("scaled")
        normed = sem("normed")
        turned = sem("turned")
        copied = sem("copied")
        gated = sem("gated")
        pled = sem("pled")
        logged = sem("logged")
        summed = sem("summed")
        expd = sem("expd")
        y_ready = sem("y_ready")
        y_stored = [sem(f"y_stored{u}") for u in two]
        chain = sem("chain")
        act_chain = sem("act_chain")
        add_chain = sem("add_chain")
        log_chain = sem("log_chain")

        with nc.Block() as block:
            @block.sync
            def _(sp):
                sp.dma_start(gpl[:, :], a["norm_ple"].partition_broadcast(P)).then_inc(small, 16)
                sp.dma_start(wp[:, :, :], a["w_ple"].rearrange("(k p) n -> p k n", p=P)).then_inc(small, 16)

                def step(n, u, m):
                    if among(n):
                        wait(sp, pled, n - 1, own)
                        sp.dma_start(pT[u][:, :, :], a["pT"][ds(n, 1)].rearrange("a p k n -> p (a k) n")).then_inc(p_loaded[u], 16)
                    if among(n - 1):
                        bb, uu, mm = shift(n, u, m, -1)
                        wait(sp, y_ready, bb + 1, own)
                        sp.dma_start(a["y"][ds(bb * P, P), :], y[:, uu, :]).then_inc(y_stored[uu], 16)
                over_tile_steps(sp, step)
                for u in two:
                    sp.wait_ge(y_stored[u], 16 * ((NT + 1 - u) // 2))

            @block.gpsimd
            def _(pool):
                for n in range(NT):
                    wait(pool, added, n - 1)
                    for k in two:
                        pool.indirect_dma_start(out=rows[n % 2][:, k, :], out_offset=None, in_=dram["grouped"],
                                                in_offset=bass.IndirectOffsetOnAxis(ap=slots[:, k, n:n + 1], axis=0))\
                            .then_inc(gathered[n % 2], 16)

            @block.tensor
            def _(pe):
                pe.wait_ge(small, 32)

                def turn(n):
                    pe.wait_ge(normed, n + 1)
                    for half in two:
                        wait(pe, copied, 2 * (n - 1) + half + 1)
                        for j in range(4 * half, 4 * half + 4):
                            mm = pe.transpose(tp[:, half, P * (j % 4):P * (j % 4) + P], hn[:, P * j:P * j + P], c["ident"][:, :])
                        mm.then_inc(turned, 1)

                def gate(u, half, n):
                    cols = slice(512 * half, 512 * half + 512)
                    for k in range(KD):
                        mm = pe.matmul(gp[:, u, half, :], hT[u][:, k, :], wg[:, k, cols], start=(k == 0), stop=(k == KD - 1))
                    return mm

                def step(n, u, m):
                    if among(n):
                        pe.wait_ge(copied, 2 * n + 2)
                        wait(pe, y_ready, n - 1)
                        gate(u, 0, n)
                    if among(n + 1):
                        turn(n + 1)
                    if among(n):
                        gate(u, 1, n).then_inc(gated, 1)
                        pe.wait_ge(p_loaded[u], 16 * (m + 1))
                        wait(pe, y_ready, n)
                        for half in two:
                            cols = slice(512 * half, 512 * half + 512)
                            for k in range(KP):
                                mm = pe.matmul(pp[:, half, :], pT[u][:, k, :], wp[:, k, cols], start=(k == 0), stop=(k == KP - 1))
                        mm.then_inc(pled, 1)
                turn(0)
                over_tile_steps(pe, step)

            @block.scalar
            def _(act):
                def scale(n, u, m):
                    s = Steps(act, act_chain, 2 * n)
                    act.wait_ge(added, n + 1)
                    wait(act, normed, n - 1)
                    s.then(act.activation(sq[:, :], h[:, ds(n, 1), :].rearrange("p a w -> p (a w)"), ACT.Square, accum_out=sh[:, u:u + 1]))
                    s.then(act.activation(sh[:, u:u + 1], sh[:, u:u + 1], ACT.Ln, bias=c["eps"][:, :], scale=1.0 / D))
                    act.activation(sh[:, u:u + 1], sh[:, u:u + 1], ACT.Exp, scale=-0.5).then_inc(scaled, 1)

                def copies(n, u):
                    for half in two:
                        act.wait_ge(turned, 2 * n + half + 1)
                        wait(act, gated, n - 1)
                        act.activation(hT[u][:, 4 * half:4 * half + 4, :].rearrange("p j n -> p (j n)"), tp[:, half, :],
                                       ACT.Copy).then_inc(copied, 1)

                def step(n, u, m):
                    if among(n + 1):
                        scale(*shift(n, u, m, 1))
                    if among(n - 1):
                        bb, uu, _ = shift(n, u, m, -1)
                        s = Steps(act, log_chain, 2 * bb)
                        act.wait_ge(gated, bb + 1)
                        wait(act, y_ready, bb)
                        log_sigmoid_parts(act, gp[:, uu, :, :].rearrange("p a n -> p (a n)"), logs[:, :], s, logged,
                                          c["one"][:, :])
                    if among(n + 1):
                        copies(n + 1, 1 - u)
                    if among(n - 1):
                        act.wait_ge(summed, bb + 1)
                        act.activation(eg[:, :], logs[:, :], ACT.Exp).then_inc(expd, 1)
                scale(0, 0, 0)
                copies(0, 0)
                over_tile_steps(act, step)

            @block.vector
            def _(dve):
                dve.wait_ge(small, 32)

                def add(n, u, m):
                    s = Steps(dve, add_chain, n)
                    dve.wait_ge(gathered[u], 32 * (m + 1))
                    row = h[:, ds(n, 1), :].rearrange("p a w -> p (a w)")
                    s.then(dve.scalar_tensor_tensor(out=row, in0=rows[u][:, 0, :], scalar=gates[:, 0, ds(n, 1)],
                                                    in1=row, op0=ALU.mult, op1=ALU.add))
                    dve.scalar_tensor_tensor(out=row, in0=rows[u][:, 1, :], scalar=gates[:, 1, ds(n, 1)],
                                             in1=row, op0=ALU.mult, op1=ALU.add).then_inc(added, 1)

                def norm(n, u, m):
                    dve.wait_ge(scaled, n + 1)
                    wait(dve, turned, 2 * n)
                    dve.scalar_tensor_tensor(out=hn[:, :], in0=h[:, ds(n, 1), :].rearrange("p a w -> p (a w)"), scalar=sh[:, u:u + 1], in1=gpl[:, :],
                                             op0=ALU.mult, op1=ALU.mult).then_inc(normed, 1)

                def log_sigmoid(n, u):
                    dve.wait_ge(logged, n + 1)
                    dve.scalar_tensor_tensor(out=logs[:, :], in0=gp[:, u, :, :].rearrange("p a n -> p (a n)"), scalar=0.0,
                                             in1=logs[:, :], op0=ALU.min, op1=ALU.subtract).then_inc(summed, 1)

                def finish(n, u, m):
                    s = Steps(dve, chain, n)
                    dve.wait_ge(pled, n + 1)
                    dve.wait_ge(expd, n + 1)
                    s.then(dve.tensor_tensor(t1[:, :], pp[:, :, :].rearrange("p a n -> p (a n)"), eg[:, :], ALU.mult))
                    wait(dve, y_stored[u], 16 * m)
                    dve.tensor_tensor(y[:, u, :], t1[:, :], h[:, ds(n, 1), :].rearrange("p a w -> p (a w)"), ALU.add)\
                        .then_inc(y_ready, 1)

                def step(n, u, m):
                    if among(n + 1):
                        add(*shift(n, u, m, 1))
                        norm(*shift(n, u, m, 1))
                    if among(n - 1):
                        bb, uu, mm = shift(n, u, m, -1)
                        log_sigmoid(bb, uu)
                        finish(bb, uu, mm)
                add(0, 0, 0)
                norm(0, 0, 0)
                over_tile_steps(dve, step)


def program(nc, a, dram):
    with ExitStack() as ctx:
        sb = lambda n, s, d=F32: ctx.enter_context(nc.sbuf_tensor(n, s, d))
        sem = lambda n: ctx.enter_context(nc.semaphore(n))
        dram["q_heads"] = dram["qkT"][0:KD].rearrange("j (r d) n -> (j r) d n", d=HD)
        dram["k_heads"] = dram["qkT"][KD:2 * KD].rearrange("j (r d) n -> (j r) d n", d=HD)
        c = constants(nc, sb, sem)
        zeroed = sem("zeroed")
        released = projection(nc, c, a, dram, zeroed)
        h = sb("h", [P, NT, D])
        logits = sb("logits", [P, NT, NG + NE])
        gates = sb("gates", [P, 2, NT])
        slots = sb("slots", [P, 2, NT], mybir.dt.uint32)
        owner = sb("owner", [1, SLOTBLOCKS + 1], mybir.dt.int32)
        with nc.sbuf_tensor("merged", [P, NT, D], F32) as merged:
            attention(nc, c, a, dram, merged, band=False)
            attention(nc, c, a, dram, merged, band=True)
            sticks(nc, c, a, dram, merged)
            with nc.sbuf_tensor("xn", [P, NT, D], F32) as xn:
                mixing(nc, c, a, dram, merged, h, xn, logits, released)
                routing(nc, c, a, dram, xn, logits, gates, slots, owner)
        wg = sb("w_ple_gate", [P, KD, D])
        experts(nc, c, a, dram, owner, wg)
        embedding(nc, c, a, dram, h, gates, slots, wg)


def kernel(**inputs):
    import numpy as np
    import concourse.bacc as bacc
    from concourse.bass_utils import run_bass_kernel_spmd

    i = {k: np.asarray(v) for k, v in inputs.items()}
    x = np.concatenate([i["x_prompt"][0], i["x_sample"].reshape(NB * TS, D)])
    p = np.concatenate([i["p_prompt"][0, 0], i["p_sample"][0].reshape(NB * TS, DP)])
    kc = np.concatenate([i["cache_a_k"][0], i["cache_b_k"][0], i["cache_c_k"][0]], axis=2)
    vc = np.concatenate([i["cache_a_v"][0], i["cache_b_v"][0], i["cache_c_v"][0]], axis=2)
    cols = lambda v: v[0].reshape(-1, P).T
    host = {
        "x": x,
        "xT": x.reshape(NT, P, KD, P).transpose(0, 3, 2, 1),
        "pT": p.reshape(NT, P, DP // P, P).transpose(0, 3, 2, 1),
        "cache_kT": kc.transpose(2, 0, 3, 1).reshape(H, NB // 2, P, PAST).transpose(0, 2, 1, 3),
        "cache_v": vc.transpose(2, 0, 1, 3).reshape(H, NB, PT, P, HD).transpose(0, 3, 1, 2, 4),
        "cache_logf": i["cache_a_logf"][0].transpose(2, 0, 1).reshape(HA * NB, PAST),
        "norm_mix": cols(i["norm_mix"]), "g_mix_out": i["g_mix_out"][0],
        "norm_ffn": i["norm_ffn"][0], "norm_ple": i["norm_ple"][0],
        "w_in": i["w_in"][0], "b_f": i["b_f"][0], "g_qa": i["g_qa"][0], "g_ka": i["g_ka"][0],
        "g_qb": i["g_qb"][0], "g_kb": i["g_kb"][0], "rel_bias": i["rel_bias"][0], "w_out": i["w_out"][0],
        "w_router": np.concatenate([i["w_router_group"][0], i["w_router_expert"][0]], axis=1),
        "b_router": np.concatenate([i["b_router_group"][0], i["b_router_expert"][0]]),
        "w_gu": np.concatenate([i[n][0].reshape(NE, KD, P, DE) for n in ("w_exp_gate", "w_exp_up")], axis=3)
                  .transpose(0, 2, 1, 3),
        "w_ed": i["w_exp_down"][0],
        "w_ple": i["w_ple"][0], "w_ple_gate": i["w_ple_gate"][0],
    }
    outs = {"y": (TOK, D), "k_all": (TOK, D), "v_all": (TOK, D), "logf_all": (TOK, HA)}
    scratch = {"qkT": (2 * KD, P, TOK), "lfs": (HA, NB * TS), "c": (2, HA, TOK), "c_past": (HA, NB, PAST),
               "bias": (HB, EXT), "bias_hankel": (HB, P, 3 * P), "grouped": (SLOTBLOCKS * P, D)}

    nc = bacc.Bacc("TRN2", target_bir_lowering=False, num_devices=1)
    arrays, a, dram = {}, {}, {}
    for name, v in host.items():
        arrays["in_" + name] = np.ascontiguousarray(v)
        a[name] = nc.dram_tensor("in_" + name, v.shape, F32, kind="ExternalInput").ap()
    for name, shape in outs.items():
        a[name] = nc.dram_tensor("out_" + name, shape, F32, kind="ExternalOutput").ap()
    for name, shape in scratch.items():
        dram[name] = nc.dram_tensor("scratch_" + name, shape, F32, kind="Internal").ap()
    program(nc, a, dram)
    r = run_bass_kernel_spmd(nc, [arrays], core_ids=[0]).results[0]

    y, k, v, f = (r["out_" + n] for n in ("y", "k_all", "v_all", "logf_all"))

    def rows(t, lo, n, prompt, keep=0):
        t = t.reshape(TOK, -1, HD)[:, lo:lo + n]
        return t[keep:SEQ].reshape(1, 1, SEQ - keep, n, HD) if prompt else t[SEQ:].reshape(1, NB, TS, n, HD)

    res = [y[:SEQ].reshape(1, SEQ, D), y[SEQ:].reshape(NB, TS, D)]
    for prompt in (True, False):
        res += [rows(k, 0, HA, prompt), rows(v, 0, HA, prompt),
                f[:SEQ].reshape(1, 1, SEQ, HA) if prompt else f[SEQ:].reshape(1, NB, TS, HA),
                rows(k, HA, HB, prompt, SEQ - PAST), rows(v, HA, HB, prompt, SEQ - PAST),
                rows(k, HA + HB, HC, prompt), rows(v, HA + HB, HC, prompt)]
    return tuple(np.ascontiguousarray(t) for t in res)
```

```python
from contextlib import ExitStack

import concourse.bass as bass
from concourse import mybir

F32 = mybir.dt.float32
F32R = mybir.dt.float32r
BF16 = mybir.dt.bfloat16
ACT = mybir.ActivationFunctionType
ALU = mybir.AluOpType
AX = mybir.AxisListType
ds = bass.ds

P = 128
D = 1024
KD = D // P
SEQ = 1024
NB, TS = 8, 16
PAST = 512
TOK = SEQ + NB * TS
NT = TOK // P
QT = SEQ // P
H, HD = 16, 64
HA, HB, HC = 6, 5, 5
GROUPS = ((0, HA), (HA, HB), (HA + HB, HC))
DIN = 3 * D + HA
REL = 257
EXT = 1792
PT = PAST // P
NE, NG, EG, DE = 16, 4, 4, 256
DP = 256
ROWS = 104
BS = 2 * ROWS
BLOCKS = (2 * TOK - NE) // BS + NE
PAIRS = (BLOCKS + 1) // 2
LEAST_PAIRS = ((2 * TOK + BS - 1) // BS + 1) // 2
SLOTBLOCKS = 2 * PAIRS + 2
FILLS = -(-2 * SLOTBLOCKS // NT)
EPS = 1e-6
NEG = -1e30
SCALE = HD ** -0.5


def wait(e, sem, count, own=None):
    if isinstance(count, int) and count <= 0:
        return
    e.wait_ge(sem, count)
    if own is not None and not isinstance(count, int):
        e.sem_inc(own, 1)


class Steps:

    def __init__(self, e, sem, base, own=None):
        self.e, self.sem, self.base, self.n, self.own = e, sem, base, 0, own

    def then(self, ins):
        self.n += 1
        ins.then_inc(self.sem, 1)
        wait(self.e, self.sem, self.base + self.n, self.own)


def over_tiles(e, body):
    body(0, 0, 0)
    body(1, 1, 0)
    with e.Fori(1, NT // 2) as m:
        body(2 * m, 0, m)
        body(2 * m + 1, 1, m)
    body(NT - 1, 0, NT // 2)


def over_heads(e, n, body):
    with e.Fori(0, n // 2) as m:
        body(2 * m, 0, m)
        body(2 * m + 1, 1, m)
    if n % 2:
        body(n - 1, 0, n // 2)


def constants(sb):
    c = {}
    c["ident"] = sb("ident", [P, P], F32)
    c["identb"] = sb("identb", [P, P], BF16)
    c["flip"] = sb("flip", [P, P], F32)
    c["negtri"] = sb("negtri", [P, P], F32)
    c["negones"] = sb("negones", [P, P], F32)
    c["ones"] = sb("ones", [P, P], F32)
    c["keep_stick"] = sb("keep_stick", [P, P], F32)
    c["keep_stick_s"] = sb("keep_stick_s", [P, P], F32)
    for name in ("causal", "band_diag", "band_far", "causal_s", "same_s", "stick", "stick_s"):
        c[name] = sb("mask_" + name, [P, P], BF16)
    c["eps"] = sb("eps", [P, 1], F32)
    c["zero"] = sb("zero", [P, 1], F32)
    c["one"] = sb("one", [P, 1], F32)
    return c


def fill_columns(pool, c, s):
    for name, v in (("eps", EPS), ("zero", 0.0), ("one", 1.0)):
        s.then(pool.memset(c[name][:, :], v))


def fill_matrices(pool, c, s):
    def select(t, value, base, pattern, mult, op, fill):
        v = t[:, :]
        if len(pattern) == 2:
            v = v.rearrange("p (b t) -> p b t", t=pattern[1][1])
        s.then(pool.affine_select(out=v, in_=v, compare_op=op, fill=fill, base=base,
                                  pattern=pattern, channel_multiplier=mult))

    def same_sample(t, fill):
        select(t, None, 0, [[-TS, NB], [0, TS]], 1, ALU.is_ge, fill)
        select(t, None, TS - 1, [[TS, NB], [0, TS]], -1, ALU.is_ge, fill)

    for name, v in (("ident", 0.0), ("identb", 0.0), ("flip", 0.0), ("negtri", -1.0), ("negones", -1.0), ("ones", 1.0),
                    ("keep_stick", 1.0), ("keep_stick_s", 1.0), ("causal", 0.0),
                    ("causal_s", 0.0), ("same_s", 0.0), ("stick", 0.0), ("stick_s", 0.0),
                    ("band_diag", 0.0), ("band_far", 0.0)):
        s.then(pool.memset(c[name][:, :], v))
    for name in ("ident", "identb"):
        select(c[name], None, 0, [[-1, P]], 1, ALU.not_equal, 1.0)
    select(c["flip"], None, -(P - 1), [[1, P]], 1, ALU.not_equal, 1.0)
    select(c["negtri"], None, 0, [[-1, P]], 1, ALU.is_ge, 0.0)
    for name, fill in (("keep_stick", 0.0), ("stick", NEG), ("keep_stick_s", 0.0), ("stick_s", NEG)):
        select(c[name], None, -1, [[1, P]], -1, ALU.is_ge, fill)
    for name in ("causal", "causal_s"):
        select(c[name], None, 0, [[-1, P]], 1, ALU.is_ge, NEG)
    for name, fill in (("keep_stick_s", 0.0), ("stick_s", NEG), ("causal_s", NEG), ("same_s", NEG)):
        same_sample(c[name], fill)
    s.then(pool.memset(c["band_diag"][0:HD, HD:P], NEG))
    s.then(pool.memset(c["band_far"][HD:P, 0:HD], NEG))


def projection(nc, c, a, dram, zeroed):
    with ExitStack() as ctx:
        sb = lambda n, s, d=F32: ctx.enter_context(nc.sbuf_tensor(n, s, d))
        ps = lambda n, s: ctx.enter_context(nc.psum_tensor(n, s, F32))
        used = []

        def sem(n):
            used.append(ctx.enter_context(nc.semaphore(n)))
            return used[-1]
        NGRP = 7
        WG = [512] * 6 + [HA]
        BANK = [0, 1, 2, 0, 1, 2, 1]
        FREE = [-3, 0, -1, 1, 2, 3, 5]
        w_in = sb("w_in", [P, KD, DIN])
        xT = sb("xT", [P, 2, KD, P])
        xr = sb("xr", [P, 2, D])
        sqx = sb("sqx", [P, D])
        gmix = sb("gmix", [P, KD])
        grow = sb("grow", [P, 2, D])
        bf = sb("bf", [P, HA])
        z = sb("z", [P, 2, DIN])
        sq = sb("sq", [P, 2, (HA + HB) * HD])
        ssx = sb("ssx", [P, 2, 2])
        hss = sb("hss", [P, 2, 22])
        lft = sb("lft", [P, 3, HA])
        logf = sb("logf", [P, 2, HA])
        qkT = sb("qkT", [P, 16, P])
        lfT = sb("lfT", [HA, TOK])
        biasx = sb("biasx", [HB, EXT])
        zp = ps("zp", [P, 3, 512])
        tp = ps("tp", [P, 4, 512])
        lp = ps("lp", [P, 512])
        ones = sb("ones_row", [P, SEQ])
        cp = sb("cp", [HA, 2, SEQ])
        lc = sb("lc", [HA * NB, PAST + TS])
        cs = sb("cs", [HA * NB, 2, PAST + TS])

        w_loaded = [sem(f"w_loaded{g}") for g in range(NGRP)]
        small_loaded = sem("small_loaded")
        sp_turns = sem("sp_turns")
        x_loaded = [sem(f"x_loaded{u}") for u in range(2)]
        z_stored = [sem(f"z_stored{u}") for u in range(2)]
        qkT_stored = sem("qkT_stored")
        xT_scaled = sem("xT_scaled")
        act_chain = sem("act_chain")
        dve_chain = sem("dve_chain")
        group_done = sem("group_done")
        group_taken = sem("group_taken")
        squares_ready = sem("squares_ready")
        heads_scaled = sem("heads_scaled")
        gates_in = sem("gates_in")
        gates_log = sem("gates_log")
        z_ready = sem("z_ready")
        turned = sem("turned")
        turned_taken = sem("turned_taken")
        grow_ready = sem("grow_ready")
        sums_ready = sem("sums_ready")
        late_stored = sem("late_stored")
        gmix_loaded = sem("gmix_loaded")
        made = sem("constants_made")
        matrices_made = sem("matrices_made")
        zeros = sb("zeros", [ROWS, D])
        zero_made = sem("zero_made")
        bias_loaded = sem("bias_loaded")
        bias_ready = sem("bias_ready")
        lc_loaded = sem("lc_loaded")
        lc_back = sem("lc_back")

        with nc.Block() as block:
            @block.sync
            def _(sp):
                sp.dma_start(xT[:, 0], a["xT"][0]).then_inc(x_loaded[0], 16)
                sp.dma_start(xr[:, 0, :], a["x"][0:P, :]).then_inc(x_loaded[0], 16)
                sp.dma_start(gmix[:, :], a["norm_mix"]).then_inc(gmix_loaded, 16)
                wv = a["w_in"].rearrange("(k p) n -> p k n", p=P)

                def load_weights(g):
                    sp.dma_start(w_in[:, :, 512 * g:512 * g + WG[g]], wv[:, :, 512 * g:512 * g + WG[g]])\
                      .then_inc(w_loaded[g], 16)
                load_weights(0)
                sp.dma_start(bf[:, :], a["b_f"].partition_broadcast(P)).then_inc(small_loaded, 16)
                for i, (src, lo, n) in enumerate((("g_qa", 0, HA), ("g_qb", HA, HB))):
                    sp.dma_start(grow[:, 0, HD * lo:HD * lo + HD], a[src].partition_broadcast(P))\
                      .then_inc(small_loaded, 16)
                for i, (src, lo, n) in enumerate((("g_ka", 0, HA), ("g_kb", HA, HB))):
                    sp.dma_start(grow[:, 1, HD * lo:HD * lo + HD], a[src].partition_broadcast(P))\
                      .then_inc(small_loaded, 16)
                sp.dma_start(lc[:, 0:PAST], a["cache_logf"]).then_inc(lc_loaded, 16)
                sp.dma_start(biasx[:, 0:REL], a["rel_bias"]).then_inc(bias_loaded, 16)

                for g in range(1, NGRP):
                    load_weights(g)

                def load(n, u, m):
                    wait(sp, group_taken, 7 * (n - 1), sp_turns)
                    sp.dma_start(xT[:, u], a["xT"][ds(n, 1)].rearrange("a p k n -> p (a k) n")).then_inc(x_loaded[u], 16)
                    sp.dma_start(xr[:, u, :], a["x"][ds(n * P, P), :]).then_inc(x_loaded[u], 16)

                def store(n, u, m):
                    wait(sp, z_ready, n + 1, sp_turns)
                    sp.dma_start(a["k_all"][ds(n * P, P), :], z[:, u, D:2 * D]).then_inc(z_stored[u], 16)
                    sp.dma_start(a["v_all"][ds(n * P, P), :], z[:, u, 2 * D:3 * D]).then_inc(z_stored[u], 16)
                    sp.dma_start(a["logf_all"][ds(n * P, P), :], logf[:, u, :]).then_inc(z_stored[u], 16)

                def store_turned(n, u, m):
                    wait(sp, turned_taken, 4 * (n + 1), sp_turns)
                    sp.dma_start(dram["qkT"][:, :, ds(n * P, P)].rearrange("j p n -> p j n"), qkT[:, :, :])\
                      .then_inc(qkT_stored, 16)

                load(1, 1, 0)
                store(0, 0, 0)
                with sp.Fori(1, NT // 2) as m:
                    load(2 * m, 0, m)
                    store(2 * m - 1, 1, m - 1)
                    store_turned(2 * m - 2, 0, m - 1)
                    load(2 * m + 1, 1, m)
                    store(2 * m, 0, m)
                    store_turned(2 * m - 1, 1, m - 1)
                load(8, 0, 4)
                store(7, 1, 3)
                store_turned(6, 0, 3)
                sp.wait_ge(bias_ready, 2)
                sp.dma_start(dram["bias"], biasx[:, :]).then_inc(late_stored, 16)
                sp.wait_ge(late_stored, 16)
                for h in range(HB):
                    src = bass.AP(dram["bias"].tensor, EXT * h, [[1, P], [1, 3 * P]])
                    sp.dma_start(dram["bias_hankel"][h], src).then_inc(late_stored, 16)
                store(8, 0, 4)
                store_turned(7, 1, 3)
                store_turned(8, 0, 4)
                sp.wait_ge(turned_taken, 4 * NT)
                sp.dma_start(dram["lfs"], lfT[:, SEQ:TOK]).then_inc(late_stored, 16)
                sp.wait_ge(late_stored, 16 * 7)
                sp.dma_start(lc[:, PAST:PAST + TS], dram["lfs"].rearrange("h (b t) -> (h b) t", t=TS))\
                  .then_inc(lc_back, 16)
                sp.wait_ge(sums_ready, 1)
                sp.dma_start(dram["c"][0, :, 0:SEQ], cp[:, 0, :]).then_inc(late_stored, 16)
                sp.dma_start(dram["c"][1, :, 0:SEQ], cp[:, 1, :]).then_inc(late_stored, 16)
                sp.wait_ge(sums_ready, 2)
                for i in range(2):
                    sp.dma_start(dram["c"][i, :, SEQ:TOK].rearrange("h (b t) -> h b t", t=TS),
                                 cs[:, i, PAST:PAST + TS]).then_inc(late_stored, 16)
                sp.dma_start(dram["c_past"].rearrange("h b k -> (h b) k"), cs[:, 1, 0:PAST]).then_inc(late_stored, 16)
                sp.wait_ge(late_stored, 16 * 12)
                sp.wait_ge(qkT_stored, 16 * NT)
                for u in range(2):
                    sp.wait_ge(z_stored[u], 48 * ((NT - u + 1) // 2))

            @block.gpsimd
            def _(pool):
                constant_steps = Steps(pool, made, 0)
                fill_columns(pool, c, constant_steps)
                pool.memset(zeros[:, :], 0.0).then_inc(zero_made, 1)
                pool.wait_ge(gmix_loaded, 16)
                pool.wait_ge(zero_made, 1)

                def scale(n, u, m):
                    pool.wait_ge(x_loaded[u], 32 * (m + 1))
                    pool.tensor_tensor(xT[:, u], xT[:, u], gmix[:, :].unsqueeze(2).to_broadcast([P, KD, P]), ALU.mult)\
                        .then_inc(xT_scaled, 1)
                    if isinstance(n, int) and n == 0:
                        fill_matrices(pool, c, constant_steps)
                        pool.sem_inc(matrices_made, 1)
                    for j in range(FILLS):
                        pool.dma_start(dram["grouped"][ds((FILLS * n + j) * ROWS, ROWS), :], zeros[:, :]).then_inc(zeroed, 16)
                over_tiles(pool, scale)
                pool.wait_ge(bias_loaded, 16)
                pool.memset(biasx[:, REL:EXT], 0.0).then_inc(bias_ready, 1)
                pool.wait_ge(bias_ready, 1)
                pool.tensor_scalar(biasx[:, REL:EXT], biasx[:, REL:EXT], biasx[:, REL - 1:REL], None, ALU.add)\
                    .then_inc(bias_ready, 1)
                pool.wait_ge(zeroed, 16 * FILLS * NT)

            @block.tensor
            def _(pe):
                def groups(n, u, m):
                    pe.wait_ge(xT_scaled, n + 1)
                    for g in range(NGRP):
                        wait(pe, group_taken, 7 * n + FREE[g])
                        pe.wait_ge(w_loaded[g], 16)
                        for k in range(KD):
                            mm = pe.matmul(zp[:, BANK[g], 0:WG[g]], xT[:, u, k, :],
                                           w_in[:, k, 512 * g:512 * g + WG[g]], start=(k == 0), stop=(k == KD - 1))
                        mm.then_inc(group_done, 1)

                def turn(n, u, m):
                    pe.wait_ge(z_ready, n + 1)
                    wait(pe, turned_taken, 4 * n)
                    for b in range(4):
                        for j in range(4):
                            col = D * (b // 2) + 512 * (b % 2) + P * j
                            mm = pe.transpose(tp[:, b, P * j:P * j + P], z[:, u, col:col + P], c["ident"][:, :])
                        if b == 3:
                            mm = pe.transpose(lp[0:HA, 0:P], logf[:, u, :], c["ident"][:, :])
                        mm.then_inc(turned, 1)

                groups(0, 0, 0)
                groups(1, 1, 0)
                pe.wait_ge(matrices_made, 1)
                turn(0, 0, 0)
                with pe.Fori(1, NT // 2) as m:
                    groups(2 * m, 0, m)
                    turn(2 * m - 1, 1, m - 1)
                    groups(2 * m + 1, 1, m)
                    turn(2 * m, 0, m)
                groups(8, 0, 4)
                turn(7, 1, 3)
                turn(8, 0, 4)

            @block.scalar
            def _(act):
                act.preload_act_table_set("natural_log_exp_and_others")
                PER = 6
                act.wait_ge(made, 3)

                def tile(n, u, m):
                    s = Steps(act, act_chain, PER * n)
                    act.wait_ge(x_loaded[u], 32 * (m + 1))
                    s.then(act.activation(sqx[:, :], xr[:, u, :], ACT.Square, accum_out=ssx[:, u, 0:1]))
                    s.then(act.activation(ssx[:, u, 1:2], ssx[:, u, 0:1], ACT.Ln, bias=c["eps"][:, :], scale=1.0 / D))
                    s.then(act.activation(ssx[:, u, 0:1], ssx[:, u, 1:2], ACT.Exp, scale=-0.5))
                    wait(act, z_stored[u], 48 * m)
                    wait(act, turned, 4 * (n - 1))
                    for g in range(NGRP):
                        act.wait_ge(group_done, 7 * n + g + 1)
                        act.activation(z[:, u, 512 * g:512 * g + WG[g]], zp[:, BANK[g], 0:WG[g]], ACT.Copy,
                                       scale=ssx[:, u, 0:1]).then_inc(group_taken, 1)
                    act.wait_ge(squares_ready, n + 1)
                    s.then(act.activation(hss[:, 1, :], hss[:, 0, :], ACT.Ln, bias=c["eps"][:, :], scale=1.0 / HD))
                    act.activation(hss[:, 1, :], hss[:, 1, :], ACT.Exp, scale=-0.5).then_inc(heads_scaled, 1)
                    act.wait_ge(gates_in, n + 1)
                    s.then(act.activation(lft[:, 1, :], lft[:, 0, :], ACT.Abs))
                    s.then(act.activation(lft[:, 1, :], lft[:, 1, :], ACT.Exp, scale=-1.0))
                    act.activation(lft[:, 2, :], lft[:, 1, :], ACT.Ln, bias=c["one"][:, :]).then_inc(gates_log, 1)
                    assert s.n == PER
                over_tiles(act, tile)

            @block.vector
            def _(dve):
                dve.wait_ge(small_loaded, 16 * 5)
                first = Steps(dve, grow_ready, 0)
                for i in range(2):
                    for lo, n in GROUPS[:2]:
                        for h in range(1, n):
                            dve.tensor_copy(grow[:, i, HD * (lo + h):HD * (lo + h + 1)], grow[:, i, HD * lo:HD * lo + HD])
                first.then(dve.memset(grow[:, :, HD * (HA + HB):D], 1.0))
                first.then(dve.tensor_scalar(grow[:, 0, :], grow[:, 0, :], SCALE, None, ALU.mult))
                PER = 4
                NQ = (HA + HB) * HD

                def tile(n, u, m):
                    s = Steps(dve, dve_chain, PER * n)
                    zv = z[:, u, 0:2 * D].rearrange("p (a c) -> p a c", a=2)
                    act_groups = 7 * n + 7
                    dve.wait_ge(group_taken, act_groups)
                    s.then(dve.tensor_tensor(sq[:, :, :], zv[:, :, 0:NQ], zv[:, :, 0:NQ], ALU.mult))
                    dve.tensor_reduce(hss[:, 0, :], sq[:, :, :].rearrange("p a (h d) -> p (a h) d", d=HD),
                                      AX.X, ALU.add).then_inc(squares_ready, 1)
                    dve.tensor_tensor(lft[:, 0, :], z[:, u, 3 * D:DIN], bf[:, :], ALU.add).then_inc(gates_in, 1)
                    dve.wait_ge(heads_scaled, n + 1)
                    for i in range(2):
                        hv = zv[:, i, 0:NQ].rearrange("p (h d) -> p h d", d=HD)
                        ins = dve.tensor_tensor(hv, hv, hss[:, 1, 11 * i:11 * i + 11].unsqueeze(2).to_broadcast([P, 11, HD]),
                                                ALU.mult)
                        s.then(ins)
                    dve.tensor_tensor(zv, zv, grow[:, :, :], ALU.mult)
                    dve.wait_ge(gates_log, n + 1)
                    s.then(dve.tensor_scalar(lft[:, 0, :], lft[:, 0, :], 0.0, None, ALU.min))
                    wait(dve, z_stored[u], 48 * m)
                    dve.tensor_tensor(logf[:, u, :], lft[:, 0, :], lft[:, 2, :], ALU.subtract).then_inc(z_ready, 1)
                    assert s.n == PER

                def copies(n, u, m):
                    wait(dve, qkT_stored, 16 * n)
                    for b in range(4):
                        dve.wait_ge(turned, 4 * n + b + 1)
                        if b == 3:
                            dve.tensor_copy(lfT[:, ds(n * P, P)], lp[0:HA, 0:P])
                        dve.tensor_copy(qkT[:, 4 * b:4 * b + 4, :].rearrange("p j n -> p (j n)"), tp[:, b, :])\
                           .then_inc(turned_taken, 1)

                tile(0, 0, 0)
                tile(1, 1, 0)
                copies(0, 0, 0)
                with dve.Fori(1, NT // 2) as m:
                    tile(2 * m, 0, m)
                    copies(2 * m - 1, 1, m - 1)
                    tile(2 * m + 1, 1, m)
                    copies(2 * m, 0, m)
                tile(8, 0, 4)
                last = Steps(dve, dve_chain, PER * NT)
                last.then(dve.memset(ones[:, :], 1.0))
                copies(7, 1, 3)
                copies(8, 0, 4)
                dve.wait_ge(turned_taken, 4 * NT)
                last.then(dve.tensor_tensor_scan(cp[:, 0, :], ones[0:HA, :], lfT[:, 0:SEQ], 0.0, ALU.mult, ALU.add))
                dve.tensor_scalar(cp[:, 1, :], cp[:, 0, :], -1.0, None, ALU.mult).then_inc(sums_ready, 1)
                dve.wait_ge(lc_loaded, 16)
                dve.wait_ge(lc_back, 16)
                last.then(dve.tensor_tensor_scan(cs[:, 0, :], ones[0:HA * NB, 0:PAST + TS], lc[:, :], 0.0,
                                                 ALU.mult, ALU.add))
                dve.tensor_scalar(cs[:, 1, :], cs[:, 0, :], -1.0, None, ALU.mult).then_inc(sums_ready, 1)

    return used


def over_units(e, heads, count, emit):
    def steps(k, u, m):
        return [(k, u, m, i) for i in range(count)]

    with e.Fori(0, heads // 2) as m:
        emit(steps(2 * m, 0, m) + steps(2 * m + 1, 1, m))
    if heads % 2:
        emit(steps(heads - 1, 0, heads // 2))


def load_queries_keys(sp, dram, h, L, qT, kT):
    sp.dma_start(qT[0:HD, :], dram["q_heads"][ds(h, 1)].rearrange("a p n -> (a p) n")).then_inc(L, 16)
    sp.dma_start(kT[0:HD, :], dram["k_heads"][ds(h, 1)].rearrange("a p n -> (a p) n")).then_inc(L, 16)


def load_values_caches(sp, a, dram, h, L, v, ckT, cv, q2):
    sp.dma_start(v[:, :, :], a["v_all"].rearrange("(n p) w -> p n w", p=P)[:, :, ds(h * HD, HD)]).then_inc(L, 16)
    for half in range(2):
        sp.dma_start(q2[HD * half:HD * half + HD, :],
                     dram["q_heads"][ds(h, 1), :, SEQ:TOK].rearrange("a p n -> (a p) n")).then_inc(L, 16)
    sp.dma_start(ckT[:, :, :], a["cache_kT"][ds(h, 1)].rearrange("a p j n -> (a p) j n")).then_inc(L, 16)
    sp.dma_start(cv[:, :, :, :], a["cache_v"][ds(h, 1)].rearrange("a p b t d -> (a p) b t d")).then_inc(L, 16)


def sample_values(pe, c, out, outT_col, out_col, probT, pt_new, pt_past, v, cv, oT, oT_done, oT_copied, k, own):
    pe.matmul(out[0:HD, outT_col:outT_col + P], v[:, QT, :], pt_new, start=True, stop=False, skip_group_check=True)
    for kt in range(PT):
        for b in range(NB):
            mm = pe.matmul(out[0:HD, outT_col + TS * b:outT_col + TS * b + TS], cv[:, b, kt, :],
                           pt_past(kt, b), start=False, stop=(kt == PT - 1 and b == NB - 1), skip_group_check=True)
    mm.then_inc(oT_done, 1)
    wait(pe, oT_copied, k + 1, own)
    return pe.transpose(out[:, out_col:out_col + HD], oT[:, :], c["ident"][0:HD, 0:HD])


def attention(nc, c, a, dram, merged, band, released):
    h0, nh = GROUPS[1] if band else GROUPS[0]
    name = "band_" if band else "forget_"
    with ExitStack() as ctx:
        sb = lambda n, s, d=F32: ctx.enter_context(nc.sbuf_tensor(name + n, s, d))
        ps = lambda n, s: ctx.enter_context(nc.psum_tensor(name + n, s, F32))

        def sem(n):
            released.append(ctx.enter_context(nc.semaphore(name + n)))
            return released[-1]
        two = range(2)
        qT = [sb(f"qT{u}", [HD + 2, TOK]) for u in two]
        kT = [sb(f"kT{u}", [HD + 2, TOK]) for u in two]
        v = [sb(f"v{u}", [P, NT, HD]) for u in two]
        ckT = [sb(f"ckT{u}", [P, NB // 2, PAST]) for u in two]
        cv = [sb(f"cv{u}", [P, NB, PT, HD]) for u in two]
        q2 = [sb(f"q2{u}", [P, NB * TS]) for u in two]
        qm = [sb(f"qm{u}", [P, PT * 160]) for u in two]
        if band:
            near = [sb(f"near{u}", [P, 3, P]) for u in two]
            short1 = [sb(f"short1{u}", [TS, TS]) for u in two]
            short = [sb(f"short{u}", [TS, P]) for u in two]
            flip16 = sb("flip16", [TS, P])
        else:
            srow = [sb(f"srow{u}", [NB + 1, P]) for u in two]
            crow = [sb(f"crow{u}", [NB + 1, PAST]) for u in two]
        prob = sb("prob", [P, 2, SEQ])
        probT = sb("probT", [P, 2, QT, P])
        stat = sb("stat", [P, 3, 4])
        oT = sb("oT", [HD, P])
        score = ps("score", [P, 2, SEQ])
        tp = ps("turn", [P, 2, 512])
        op = ps("out", [P, 2, 512])

        order = [0, 7, 3, 6, 2, 5, 1, 4] if band else [7, 6, 5, 4, 0, 3, 1, 2]
        blocks = [list(range(max(0, q - PT) if band else 0, q + 1)) for q in order]
        blocks.append(list(range(PT + 1)))
        NU = len(blocks)
        chunks = [(len(b) + 3) // 4 for b in blocks]
        before = [sum(chunks[:i]) for i in range(NU)]
        NCH = sum(chunks)
        assert NCH % 2 == 0 and NU % 3 == 0

        own, pe_turns, pool_turns = sem("sp_turns"), sem("pe_turns"), sem("pool_turns")
        once = sem("once")
        ready = sem("ready")
        keys_loaded = [sem(f"keys_loaded{u}") for u in two]
        loaded = [sem(f"loaded{u}") for u in two]
        head_free = sem("head_free")
        masked = sem("masked")
        scored = sem("scored")
        maxed = sem("maxed")
        expd = sem("expd")
        turned = sem("turned")
        copied = sem("copied")
        summed = sem("summed")
        written = sem("written")
        oT_done = sem("oT_done")
        oT_copied = sem("oT_copied")
        dve_chain = sem("dve_chain")
        pool_chain = sem("pool_chain")
        NK, NL = 6, 5

        slot = lambda u, i: (u * NU + i) % 2

        with nc.Block() as block:
            @block.sync
            def _(sp):
                sp.sem_inc(head_free, 2)
                def head(k, u, m):
                    h = h0 + k
                    L, K = loaded[u], keys_loaded[u]
                    wait(sp, head_free, k + 1, own)
                    load_queries_keys(sp, dram, h, K, qT[u], kT[u])
                    sp.wait_ge(ready, 1)
                    if band:
                        sp.dma_start(kT[u][HD:HD + 1, :], dram["bias"][ds(k, 1), REL:REL + TOK]).then_inc(K, 16)
                        row = dram["bias_hankel"][ds(k, 1)].rearrange("a p n -> (a p) n")
                        for j in two:
                            sp.dma_start(near[u][:, j, :], row[:, 1 + P * j:1 + P * j + P]).then_inc(K, 16)
                        sp.dma_start(short1[u][:, :], row[0:TS, P - TS + 1:P + 1]).then_inc(K, 16)
                    else:
                        sp.dma_start(kT[u][HD:HD + 1, :], dram["c"][1, ds(h, 1), :]).then_inc(K, 16)
                        sp.dma_start(qT[u][HD + 1:HD + 2, :], dram["c"][0, ds(h, 1), :]).then_inc(K, 16)
                        sp.dma_start(crow[u][0:NB, :], dram["c_past"][ds(h, 1)].rearrange("a b n -> (a b) n")).then_inc(K, 16)
                        sp.dma_start(srow[u][NB:NB + 1, :], dram["c"][0, ds(h, 1), SEQ:TOK]).then_inc(K, 16)
                    load_values_caches(sp, a, dram, h, L, v[u], ckT[u], cv[u], q2[u])
                over_heads(sp, nh, head)

            @block.gpsimd
            def _(pool):
                s = Steps(pool, once, 0)
                for u in two:
                    s.then(pool.memset(qm[u][:, :], 0.0))
                    s.then(pool.memset(qT[u][HD:HD + 2, :], 1.0))
                    s.then(pool.memset(kT[u][HD:HD + 2, :], 1.0))
                    if not band:
                        s.then(pool.memset(crow[u][:, :], 1.0))
                        s.then(pool.memset(srow[u][:, :], 1.0))
                        sv = srow[u][0:NB, :].rearrange("p (b t) -> p b t", t=TS)
                        s.then(pool.affine_select(out=sv, in_=sv, compare_op=ALU.is_equal, fill=0.0, base=0,
                                                  pattern=[[-1, NB], [0, TS]], channel_multiplier=1))
                if band:
                    s.then(pool.memset(flip16[:, :], 1.0))
                    fv = flip16[:, :].rearrange("p (b t) -> p b t", t=TS)
                    s.then(pool.affine_select(out=fv, in_=fv, compare_op=ALU.is_equal, fill=0.0, base=-(TS - 1),
                                              pattern=[[0, NB], [1, TS]], channel_multiplier=1))
                pool.sem_inc(ready, 1)

                def head(k, u, m):
                    wait(pool, keys_loaded[u], 16 * NK * (m + 1), pool_turns)
                    wait(pool, loaded[u], 16 * NL * (m + 1), pool_turns)
                    if band:
                        chain = Steps(pool, pool_chain, 2 * k, pool_turns)
                        chain.then(pool.tensor_copy(near[u][:, 2, :].rearrange("p (b t) -> p b t", t=TS),
                                                    near[u][:, 1, 0:TS].unsqueeze(1).to_broadcast([P, NB, TS])))
                        chain.then(pool.tensor_copy(short[u][:, :].rearrange("p (b t) -> p b t", t=TS),
                                                    short1[u][:, :].unsqueeze(1).to_broadcast([TS, NB, TS])))
                    for half in two:
                        dst = qm[u][HD * half:HD * half + HD, :].rearrange("p (j c) -> p j c", c=160)
                        src = q2[u][HD * half:HD * half + HD, :].rearrange("p (j c) -> p j c", c=2 * TS)
                        ins = pool.tensor_copy(dst[:, :, TS * half:TS * half + TS], src[:, :, TS * half:TS * half + TS])
                    ins.then_inc(masked, 1)
                    wait(pool, masked, k + 1, pool_turns)
                over_heads(pool, nh, head)

            @block.tensor
            def _(pe):
                pe.wait_ge(ready, 1)
                pe.sem_inc(turned, NCH)

                def mask(region, m, stop=True):
                    return pe.matmul(region, c["identb"][:, :], c[m][:, :], start=False, stop=stop, skip_group_check=True)

                def scores(k, u, m, i):
                    s = slot(u, i)
                    if i == 0:
                        pe.wait_ge(keys_loaded[u], 16 * NK * (m + 1))
                    if i == NU - 1:
                        pe.wait_ge(loaded[u], 16 * NL * (m + 1))
                        pe.wait_ge(masked, k + 1)
                    pe.wait_ge(expd, NU * k + i + 1)
                    if i == NU - 1:
                        past = score[:, s, 0:PAST]
                        for j in range(NB // 2):
                            pe.matmul(past, qm[u][:, P * j:P * j + P], ckT[u][:, j, :], start=(j == 0), stop=False,
                                      skip_group_check=True)
                        new = score[:, s, PAST:PAST + P]
                        if band:
                            far = PAST - P
                            pe.matmul(past[:, 0:far], qT[u][HD:HD + 1, SEQ:TOK], kT[u][HD:HD + 1, 0:far], start=False,
                                      stop=False, skip_group_check=True)
                            pe.matmul(past[:, far:PAST], near[u][:, 2, :], c["flip"][:, :], start=False, stop=True,
                                      skip_group_check=True)
                            pe.matmul(new, qT[u][0:HD, SEQ:TOK], kT[u][0:HD, SEQ:TOK], start=True, stop=False,
                                      skip_group_check=True)
                            pe.matmul(new, short[u][:, :], flip16[:, :], start=False, stop=False, skip_group_check=True)
                        else:
                            pe.matmul(past, srow[u][:, :], crow[u][:, :], start=False, stop=True, skip_group_check=True)
                            pe.matmul(new, qT[u][:, SEQ:TOK], kT[u][:, SEQ:TOK], start=True, stop=False,
                                      skip_group_check=True)
                        mask(new, "same_s" if band else "causal_s").then_inc(scored, 1)
                        return
                    q = order[i]
                    j0 = blocks[i][0]
                    for cc in range(chunks[i]):
                        part = blocks[i][4 * cc:4 * cc + 4]
                        col = lambda j: P * (j - j0)
                        far = [j for j in part if j < q - 1] if band else part
                        close = [j for j in part if j not in far]
                        start = True
                        for js, rows in ((far, HD + 1 if band else HD + 2), (close, HD)):
                            if js:
                                mm = pe.matmul(score[:, s, col(js[0]):col(js[-1]) + P], qT[u][0:rows, P * q:P * q + P],
                                               kT[u][0:rows, P * js[0]:P * js[-1] + P], start=start, stop=True,
                                               skip_group_check=True)
                                start = False
                        for j in close:
                            mm = pe.matmul(score[:, s, col(j):col(j) + P], near[u][:, q - j, :], c["flip"][:, :],
                                           start=False, stop=True, skip_group_check=True)
                        for j in part:
                            if j == q:
                                mm = mask(score[:, s, col(j):col(j) + P], "band_diag" if band else "causal")
                            elif band and j == q - PT:
                                mm = mask(score[:, s, col(j):col(j) + P], "band_far")
                    mm.then_inc(scored, 1)

                def turn(k, u, m, i):
                    s = slot(u, i)
                    pe.wait_ge(expd, NU * k + i + 1 + 2)
                    for cc in range(chunks[i]):
                        pe.wait_ge(copied, NCH * k + before[i] + cc + 1)
                        for j in range(4 * cc, min(4 * cc + 4, len(blocks[i]))):
                            mm = pe.transpose(tp[:, (before[i] + cc) % 2, P * (j % 4):P * (j % 4) + P],
                                              prob[:, s, P * j:P * j + P], c["ident"][:, :])
                        mm.then_inc(turned, 1)

                def values(k, u, m, i):
                    s = slot(u, i)
                    pe.wait_ge(written, NU * k + i + 1)
                    pe.wait_ge(copied, NCH * k + before[i] + chunks[i] + 2)
                    if i == 0:
                        pe.wait_ge(loaded[u], 16 * NL * (m + 1))
                    n = len(blocks[i])
                    if i == NU - 1:
                        mm = sample_values(pe, c, op[:, s, :], 0, P, probT, probT[:, s, PT, :],
                                           lambda kt, b: probT[:, s, kt, TS * b:TS * b + TS], v[u], cv[u],
                                           oT, oT_done, oT_copied, k, pe_turns)
                    else:
                        for x, j in enumerate(blocks[i]):
                            mm = pe.matmul(op[:, s, 0:HD], probT[:, s, x, :], v[u][:, j, :], start=(x == 0), stop=(x == n - 1))
                    mm.then_inc(summed, 1)

                def emit(steps):
                    scores(*steps[0])
                    for x, st in enumerate(steps):
                        if x + 1 < len(steps):
                            scores(*steps[x + 1])
                        turn(*st)
                        if x:
                            values(*steps[x - 1])
                    values(*steps[-1])
                over_units(pe, nh, NU, emit)

            @block.scalar
            def _(act):
                act.sem_inc(expd, 2)

                def emit(steps):
                    for k, u, m, i in steps:
                        s = slot(u, i)
                        w = P * len(blocks[i])
                        act.wait_ge(maxed, NU * k + i + 1)
                        act.wait_ge(turned, NCH * k + NCH + (before[i - 1] if i else before[NU - 1] - NCH))
                        act.activation(prob[:, s, 0:w], score[:, s, 0:w], ACT.Exp, bias=stat[:, i % 3, 1:2],
                                       accum_out=stat[:, i % 3, 2:3]).then_inc(expd, 1)
                over_units(act, nh, NU, emit)

            @block.vector
            def _(dve):
                dve.sem_inc(copied, 2)
                dve.sem_inc(summed, 2)
                dve.sem_inc(written, 2)

                def maxima(k, u, m, i, chain):
                    dve.wait_ge(scored, NU * k + i + 1)
                    chain.then(dve.tensor_reduce(stat[:, i % 3, 0:1], score[:, slot(u, i), 0:P * len(blocks[i])], AX.X, ALU.max))
                    dve.tensor_scalar(stat[:, i % 3, 1:2], stat[:, i % 3, 0:1], -1.0, None, ALU.mult).then_inc(maxed, 1)

                def copies(k, u, m, i, chain):
                    dve.wait_ge(summed, NU * k + i + 1)
                    for cc in range(chunks[i]):
                        n = min(4, len(blocks[i]) - 4 * cc)
                        dve.wait_ge(turned, NCH * k + NCH + before[i] + cc + 1)
                        dve.tensor_copy(probT[:, slot(u, i), 4 * cc:4 * cc + n, :].rearrange("p j n -> p (j n)"),
                                        tp[:, (before[i] + cc) % 2, 0:P * n]).then_inc(copied, 1)

                def write(k, u, m, i, chain):
                    s = slot(u, i)
                    if i == NU - 1:
                        dve.wait_ge(oT_done, k + 1)
                        dve.tensor_copy(oT[:, :], op[0:HD, s, 0:P]).then_inc(oT_copied, 1)
                    dve.wait_ge(summed, NU * k + i + 1 + 2)
                    if i == NU - 1:
                        dve.nop().then_inc(head_free, 1)
                    chain.then(dve.reciprocal(stat[:, i % 3, 3:4], stat[:, i % 3, 2:3]))
                    tile = QT if i == NU - 1 else order[i]
                    col = P if i == NU - 1 else 0
                    dve.tensor_scalar(merged[:, tile, ds(HD * (h0 + k), HD)], op[:, s, col:col + HD],
                                      stat[:, i % 3, 3:4], None, ALU.mult).then_inc(written, 1)

                def emit(steps):
                    chain = Steps(dve, dve_chain, 2 * NU * steps[0][0])
                    maxima(*steps[0], chain)
                    for x, st in enumerate(steps):
                        if x + 1 < len(steps):
                            maxima(*steps[x + 1], chain)
                        copies(*st, chain)
                        if x:
                            write(*steps[x - 1], chain)
                    write(*steps[-1], chain)
                    assert chain.n == 2 * len(steps)
                over_units(dve, nh, NU, emit)


def sticks(nc, c, a, dram, merged, mixw):
    h0, nh = GROUPS[2]
    name = "stick_"
    with ExitStack() as ctx:
        sb = lambda n, s, d=F32: ctx.enter_context(nc.sbuf_tensor(name + n, s, d))
        ps = lambda n, s: ctx.enter_context(nc.psum_tensor(name + n, s, F32))
        sem = lambda n: ctx.enter_context(nc.semaphore(name + n))
        two = range(2)
        qT = [sb(f"qT{u}", [HD, TOK]) for u in two]
        kT = [sb(f"kT{u}", [HD, TOK]) for u in two]
        v = [sb(f"v{u}", [P, NT, HD]) for u in two]
        ckT = [sb(f"ckT{u}", [P, NB // 2, PAST]) for u in two]
        cv = [sb(f"cv{u}", [P, NB, PT, HD]) for u in two]
        q2 = [sb(f"q2{u}", [P, NB * TS]) for u in two]
        qm = [sb(f"qm{u}", [P, NB * TS]) for u in two]
        W = 512
        WS = P * (PT + 1)
        logs = sb("logs", [P, 2, W])
        soft = sb("soft", [P, 2, W])
        later = sb("later", [P, 2, W])
        wgt = sb("wgt", [P, 2, W])
        logs_s = sb("logs_s", [P, WS])
        soft_s = sb("soft_s", [P, WS])
        later_s = sb("later_s", [P, PT, P])
        wgt_s = sb("wgt_s", [P, WS])
        oT = sb("oT", [HD, P])
        zp = ps("z", [P, 4, W])
        zs = ps("zs", [P, 2 * W])
        op = ps("out", [P, 2, 512])
        S0 = 2 * W - WS

        units = [(4, j) for j in reversed(range(QT))] + [(0, j) for j in reversed(range(4))] + [None]
        NU = len(units)
        lo = [P * max(0, x[1] - x[0]) if x else 0 for x in units]
        diag = [x is not None and x[1] >= x[0] for x in units]
        first = [x is not None and x[1] == x[0] + 3 for x in units]
        last = [x is not None and x[1] == 0 for x in units]

        own, pe_turns, pool_turns = sem("sp_turns"), sem("pe_turns"), sem("pool_turns")
        once = sem("once")
        ready = sem("ready")
        keys_loaded = [sem(f"keys_loaded{u}") for u in two]
        loaded = [sem(f"loaded{u}") for u in two]
        head_free = sem("head_free")
        masked = sem("masked")
        scored = sem("scored")
        logged = sem("logged")
        softened = sem("softened")
        carried = sem("carried")
        tailed = sem("tailed")
        weighed = sem("weighed")
        summed = sem("summed")
        written = sem("written")
        oT_done = sem("oT_done")
        mix_loaded = sem("mix_loaded")
        oT_copied = sem("oT_copied")
        act_chain = sem("act_chain")
        dve_chain = sem("dve_chain")
        pool_chain = sem("pool_chain")
        NL = 5
        at = lambda k, i: NU * k + i

        with nc.Block() as block:
            @block.sync
            def _(sp):
                sp.sem_inc(head_free, 2)

                def head(k, u, m):
                    wait(sp, head_free, k + 1, own)
                    load_queries_keys(sp, dram, h0 + k, keys_loaded[u], qT[u], kT[u])
                    load_values_caches(sp, a, dram, h0 + k, loaded[u], v[u], ckT[u], cv[u], q2[u])
                over_heads(sp, nh, head)
                wv = a["w_out"].rearrange("(k p) n -> p k n", p=P)
                for i in two:
                    sp.dma_start(mixw["w_out"][:, :, 512 * i:512 * i + 512], wv[:, :, 512 * i:512 * i + 512]).then_inc(mix_loaded, 16)
                sp.dma_start(mixw["gmo"][:, :], a["g_mix_out"].partition_broadcast(P)).then_inc(mix_loaded, 16)
                sp.dma_start(mixw["gff"][:, :], a["norm_ffn"].partition_broadcast(P)).then_inc(mix_loaded, 16)
                sp.dma_start(mixw["w_r"][:, :, :], a["w_router"].rearrange("(k p) n -> p k n", p=P)).then_inc(mix_loaded, 16)
                sp.dma_start(mixw["b_r"][:, :], a["b_router"].partition_broadcast(P)).then_inc(mix_loaded, 16)
                sp.wait_ge(mix_loaded, 16 * 6)

            @block.gpsimd
            def _(pool):
                pool.sem_inc(carried, 2)
                s = Steps(pool, once, 0)
                for u in two:
                    s.then(pool.memset(qm[u][:, :], 0.0))

                def queries(k, u, m):
                    wait(pool, loaded[u], 16 * NL * (m + 1), pool_turns)
                    for half in two:
                        view = lambda t: t[u][HD * half:HD * half + HD, :].rearrange("p (j c) -> p j c", c=2 * TS)[
                            :, :, TS * half:TS * half + TS]
                        ins = pool.tensor_copy(view(qm), view(q2))
                    ins.then_inc(masked, 1)
                    wait(pool, masked, k + 1, pool_turns)

                def carry(k, u, m, i, chain):
                    wait(pool, softened, at(k, i) + 1 + 2, pool_turns)
                    if units[i] is None:
                        chain.then(pool.tensor_copy(later_s[:, 0, :], soft_s[:, 0:P]))
                        for b in range(1, PT):
                            ins = pool.tensor_tensor(later_s[:, b, :], later_s[:, b - 1, :], soft_s[:, P * b:P * b + P], ALU.add)
                            if b < PT - 1:
                                chain.then(ins)
                        ins.then_inc(carried, 1)
                        wait(pool, carried, at(k, i) + 1 + 2, pool_turns)
                        return
                    wait(pool, tailed, at(k, i) + 2, pool_turns)
                    wait(pool, carried, at(k, i) + 2, pool_turns)
                    old, new, s_ = later[:, i % 2], later[:, (i + 1) % 2], soft[:, i % 2]
                    seen = W if first[i] else lo[i - 1]
                    if lo[i] < seen:
                        ins = pool.tensor_copy(new[:, lo[i]:seen], s_[:, lo[i]:seen])
                    if seen < W:
                        ins = pool.tensor_tensor(new[:, seen:W], old[:, seen:W], s_[:, seen:W], ALU.add)
                    ins.then_inc(carried, 1)

                def emit(steps):
                    chain = Steps(pool, pool_chain, (PT - 1) * steps[0][0], pool_turns)
                    for k, u, m, i in steps:
                        if i == NU - 4:
                            wait(pool, carried, at(k, i) + 2, pool_turns)
                            queries(k, u, m)
                        carry(k, u, m, i, chain)
                    assert chain.n == (PT - 1) * (len(steps) // NU)
                over_units(pool, nh, NU, emit)

            @block.tensor
            def _(pe):
                pe.sem_inc(tailed, 2)
                pe.sem_inc(summed, 2)

                def scores(k, u, m, i):
                    if i == 0:
                        pe.wait_ge(keys_loaded[u], 16 * 2 * (m + 1))
                    pe.wait_ge(weighed, at(k, i) + 1)
                    if units[i] is None:
                        pe.wait_ge(loaded[u], 16 * NL * (m + 1))
                        pe.wait_ge(masked, k + 1)
                        pe.matmul(zs[:, S0:W], kT[u][:, SEQ:TOK], qT[u][:, SEQ:TOK], start=True, stop=True,
                                  skip_group_check=True)
                        for b in range(PT):
                            for j in range(NB // 2):
                                mm = pe.matmul(zs[:, W + P * b + 2 * TS * j:W + P * b + 2 * TS * (j + 1)],
                                               ckT[u][:, j, P * (PT - 1 - b):P * (PT - b)], qm[u][:, 2 * TS * j:2 * TS * (j + 1)],
                                               start=(b == 0 and j == 0), stop=True, skip_group_check=True)
                    else:
                        q0, j = units[i]
                        mm = pe.matmul(zp[:, i % 4, lo[i]:W], kT[u][:, P * j:P * j + P], qT[u][:, P * q0 + lo[i]:P * q0 + W],
                                       start=True, stop=True, skip_group_check=True)
                    mm.then_inc(scored, 1)

                def add(region, lhsT, rhs):
                    return pe.matmul(region, lhsT, rhs, start=False, stop=True, skip_group_check=True)

                def tails(k, u, m, i):
                    pe.wait_ge(softened, at(k, i) + 1 + 2)
                    if units[i] is None:
                        add(zs[:, S0:W], c["identb"][:, :], c["stick_s"][:, :])
                        add(zs[:, S0:W], c["negtri"][:, :], soft_s[:, 0:P])
                        add(zs[:, W:2 * W], c["negtri"][:, :], soft_s[:, P:WS])
                        pe.wait_ge(carried, at(k, i) + 1 + 2)
                        mm = add(zs[:, W:2 * W], c["negones"][:, :], later_s[:, :, :].rearrange("p b n -> p (b n)"))
                    else:
                        z = zp[:, i % 4, :]
                        if diag[i]:
                            add(z[:, lo[i]:lo[i] + P], c["identb"][:, :], c["stick"][:, :])
                        mm = add(z[:, lo[i]:W], c["negtri"][:, :], soft[:, i % 2, lo[i]:W])
                        if not first[i]:
                            pe.wait_ge(carried, at(k, i) + 2)
                            mm = add(z[:, lo[i - 1]:W], c["negones"][:, :], later[:, i % 2, lo[i - 1]:W])
                    mm.then_inc(tailed, 1)

                def values(k, u, m, i):
                    pe.wait_ge(weighed, at(k, i) + 1 + 4)
                    if i == 0:
                        pe.wait_ge(loaded[u], 16 * NL * (m + 1))
                    if units[i] is None:
                        pe.wait_ge(written, 3 * k + 1 + 1)
                        mm = sample_values(pe, c, op[:, 0, :], 0, P, None, wgt_s[:, 0:P],
                                           lambda kt, b: wgt_s[:, P * (PT - kt) + TS * b:P * (PT - kt) + TS * b + TS],
                                           v[u], cv[u], oT, oT_done, oT_copied, k, pe_turns)
                    else:
                        q0, j = units[i]
                        if first[i]:
                            pe.wait_ge(written, 3 * k + 1)
                        for t in range(max(j - q0, 0), 4):
                            mm = pe.matmul(op[:, 1 if q0 == 0 else 0, HD * t:HD * t + HD], wgt[:, i % 2, P * t:P * t + P],
                                           v[u][:, j, :], start=first[i], stop=last[i], skip_group_check=True)
                    mm.then_inc(summed, 1)

                def emit(steps):
                    n = len(steps)
                    scores(*steps[0])
                    scores(*steps[1])
                    for x in range(n):
                        if x + 2 < n:
                            scores(*steps[x + 2])
                        tails(*steps[x])
                        if x:
                            values(*steps[x - 1])
                    values(*steps[-1])
                over_units(pe, nh, NU, emit)

            @block.scalar
            def _(act):
                act.sem_inc(weighed, 4)

                def parts(i, t, ts):
                    return ts[:, :] if units[i] is None else t[:, i % 2, lo[i]:W]

                def z_of(i):
                    return zs[:, S0:2 * W] if units[i] is None else zp[:, i % 4, lo[i]:W]

                def logarithms(k, u, m, i, chain):
                    act.wait_ge(scored, at(k, i) + 1)
                    act.wait_ge(softened, at(k, i) + 1)
                    t = parts(i, logs, logs_s)
                    chain.then(act.activation(t, z_of(i), ACT.Abs))
                    chain.then(act.activation(t, t, ACT.Exp, scale=-1.0))
                    act.activation(t, t, ACT.Ln, bias=c["one"][:, :]).then_inc(logged, 1)

                def weights(k, u, m, i):
                    act.wait_ge(tailed, at(k, i) + 1 + 2)
                    act.wait_ge(summed, at(k, i) + 1)
                    act.activation(parts(i, wgt, wgt_s), z_of(i), ACT.Exp).then_inc(weighed, 1)

                def emit(steps):
                    chain = Steps(act, act_chain, 2 * NU * steps[0][0])
                    logarithms(*steps[0], chain)
                    for x, st in enumerate(steps):
                        if x + 1 < len(steps):
                            logarithms(*steps[x + 1], chain)
                        weights(*st)
                    assert chain.n == 2 * len(steps)
                over_units(act, nh, NU, emit)

            @block.vector
            def _(dve):
                dve.sem_inc(softened, 2)
                dve.sem_inc(written, 1)

                def soften(k, u, m, i, chain):
                    dve.wait_ge(logged, at(k, i) + 1)
                    dve.wait_ge(tailed, at(k, i) + 1)
                    dve.wait_ge(carried, at(k, i) + 1)
                    if units[i] is None:
                        z, t, s_, keep = zs[:, S0:2 * W], logs_s[:, :], soft_s[:, :], "keep_stick_s"
                    else:
                        z, t, s_, keep = zp[:, i % 4, lo[i]:W], logs[:, i % 2, lo[i]:W], soft[:, i % 2, lo[i]:W], "keep_stick"
                    ins = dve.scalar_tensor_tensor(out=s_, in0=z, scalar=0.0, in1=t, op0=ALU.max, op1=ALU.add)
                    if units[i] is None or diag[i]:
                        chain.then(ins)
                        ins = dve.tensor_tensor(s_[:, 0:P], s_[:, 0:P], c[keep][:, :], ALU.mult)
                    ins.then_inc(softened, 1)

                def write(k, u, m, i):
                    if units[i] is None:
                        dve.wait_ge(oT_done, k + 1)
                        dve.tensor_copy(oT[:, :], op[0:HD, 0, 0:P]).then_inc(oT_copied, 1)
                    elif not last[i]:
                        return
                    dve.wait_ge(summed, at(k, i) + 1 + 2)
                    cols = ds(HD * (h0 + k), HD)
                    if units[i] is None:
                        dve.nop().then_inc(head_free, 1)
                        ins = dve.tensor_copy(merged[:, QT, cols], op[:, 0, P:P + HD])
                    else:
                        q0 = units[i][0]
                        ins = dve.tensor_copy(merged[:, q0:q0 + 4, cols],
                                              op[:, 1 if q0 == 0 else 0, 0:4 * HD].rearrange("p (t d) -> p t d", d=HD))
                    ins.then_inc(written, 1)

                ND = sum(diag) + 1

                def emit(steps):
                    chain = Steps(dve, dve_chain, ND * steps[0][0])
                    soften(*steps[0], chain)
                    for x in range(len(steps)):
                        if x + 1 < len(steps):
                            soften(*steps[x + 1], chain)
                        if x:
                            write(*steps[x - 1])
                    write(*steps[-1])
                    assert chain.n == ND * (len(steps) // NU)
                over_units(dve, nh, NU, emit)


def shift(n, u, m, d):
    if d < 0:
        return (n - 1, 0, m) if u else (n - 1, 1, m - 1)
    return (n + 1, 0, m + 1) if u else (n + 1, 1, m)


def over_tile_steps(e, step):
    step(0, 0, 0)
    step(1, 1, 0)
    with e.Fori(1, NT // 2) as m:
        step(2 * m, 0, m)
        step(2 * m + 1, 1, m)
    step(NT - 1, 0, NT // 2)
    step(NT, 1, NT // 2)


def among(x):
    return not isinstance(x, int) or 0 <= x < NT


def mixing(nc, c, a, dram, merged, h, xn, logits, released, mixw):
    with ExitStack() as ctx:
        sb = lambda n, s, d=F32: ctx.enter_context(nc.sbuf_tensor("mix_" + n, s, d))
        ps = lambda n, s: ctx.enter_context(nc.psum_tensor("mix_" + n, s, F32))
        sem = lambda n: ctx.enter_context(nc.semaphore("mix_" + n))
        two = range(2)
        w_out, w_r, b_r, gmo, gff = (mixw[n] for n in ("w_out", "w_r", "b_r", "gmo", "gff"))
        xr = sb("xr", [P, 2, D])
        m2 = sb("m2", [P, D])
        mT = [sb(f"mT{u}", [P, KD, P]) for u in two]
        xT = sb("xT", [P, KD, P])
        sq = sb("sq", [P, D])
        sm = sb("sm", [P, 2, 3])
        sh = sb("sh", [P, 2])
        tm = ps("tm", [P, 2, 512])
        tx = ps("tx", [P, 2, 512])
        om = ps("om", [P, 2, 512])
        lg = ps("lg", [P, 512])

        own = sem("sp_turns")
        x_loaded = [sem(f"x_loaded{u}") for u in two]
        act_chain = sem("act_chain")
        m_scale = sem("m_scale")
        m_normed = sem("m_normed")
        m_turned = sem("m_turned")
        m_copied = sem("m_copied")
        mixed = sem("mixed")
        h_ready = sem("h_ready")
        h_scale = sem("h_scale")
        x_normed = sem("x_normed")
        x_turned = sem("x_turned")
        x_copied = sem("x_copied")
        routed = sem("routed")
        logits_ready = sem("logits_ready")
        xs = sb("xs", [P, D])
        x_staged = sem("x_staged")
        row_chain = sem("row_chain")

        with nc.Block() as block:
            @block.sync
            def _(sp):
                def load(n, u, m):
                    wait(sp, h_ready, n - 1, own)
                    sp.dma_start(xr[:, u, :], a["x"][ds(n * P, P), :]).then_inc(x_loaded[u], 16)
                over_tiles(sp, load)

            @block.tensor
            def _(pe):
                def turn(src, dst, ready, copied, n, done):
                    pe.wait_ge(ready, n + 1)
                    for half in two:
                        wait(pe, copied, 2 * (n - 1) + half + 1)
                        for j in range(4 * half, 4 * half + 4):
                            mm = pe.transpose(dst[:, half, P * (j % 4):P * (j % 4) + P], src(j), c["ident"][:, :])
                        mm.then_inc(done, 1)

                def mix(n, u, m):
                    for half in two:
                        pe.wait_ge(m_copied, 2 * n + 2)
                        wait(pe, h_ready, n)
                        for k in range(KD):
                            mm = pe.matmul(om[:, half, :], mT[u][:, k, :], w_out[:, k, 512 * half:512 * half + 512],
                                           start=(k == 0), stop=(k == KD - 1))
                    mm.then_inc(mixed, 1)

                def route(n):
                    pe.wait_ge(x_copied, 2 * n + 2)
                    wait(pe, logits_ready, n)
                    for k in range(KD):
                        mm = pe.matmul(lg[:, 0:NG + NE], xT[:, k, :], w_r[:, k, :], start=(k == 0), stop=(k == KD - 1))
                    mm.then_inc(routed, 1)

                def step(n, u, m):
                    if among(n):
                        mix(n, u, m)
                    if among(n - 1):
                        turn(lambda j: xs[:, P * j:P * j + P], tx, x_staged, x_copied, n - 1, x_turned)
                    if among(n + 1):
                        turn(lambda j: m2[:, P * j:P * j + P], tm, m_normed, m_copied, n + 1, m_turned)
                    if among(n - 1):
                        route(n - 1)
                turn(lambda j: m2[:, P * j:P * j + P], tm, m_normed, m_copied, 0, m_turned)
                over_tile_steps(pe, step)

            @block.scalar
            def _(act):
                PER = 6

                def group_scale(n, u, m):
                    s = Steps(act, act_chain, PER * n)
                    wait(act, m_normed, n - 1)
                    for g, (h0, nh) in enumerate(GROUPS):
                        s.then(act.activation(sq[:, 0:HD * nh], merged[:, ds(n, 1), HD * h0:HD * (h0 + nh)]
                                              .rearrange("p a w -> p (a w)"), ACT.Square, accum_out=sm[:, u, g:g + 1]))
                    s.then(act.activation(sm[:, u, 0:1], sm[:, u, 0:1], ACT.Ln, bias=c["eps"][:, :], scale=1.0 / (HD * HA)))
                    s.then(act.activation(sm[:, u, 1:3], sm[:, u, 1:3], ACT.Ln, bias=c["eps"][:, :], scale=1.0 / (HD * HB)))
                    s.then(act.activation(sm[:, u, :], sm[:, u, :], ACT.Exp, scale=-0.5))
                    act.sem_inc(m_scale, 1)
                    assert s.n == PER

                def row_scale(n, u, m):
                    s = Steps(act, row_chain, 2 * n)
                    act.wait_ge(h_ready, n + 1)
                    wait(act, x_normed, n - 1)
                    s.then(act.activation(sq[:, :], h[:, ds(n, 1), :].rearrange("p a w -> p (a w)"), ACT.Square,
                                          accum_out=sh[:, u:u + 1]))
                    s.then(act.activation(sh[:, u:u + 1], sh[:, u:u + 1], ACT.Ln, bias=c["eps"][:, :], scale=1.0 / D))
                    act.activation(sh[:, u:u + 1], sh[:, u:u + 1], ACT.Exp, scale=-0.5).then_inc(h_scale, 1)

                def copies(src, dst, turned, free, count, n, done):
                    for half in two:
                        act.wait_ge(turned, 2 * n + half + 1)
                        wait(act, free, count)
                        act.activation(dst[:, 4 * half:4 * half + 4, :].rearrange("p j n -> p (j n)"), src[:, half, :],
                                       ACT.Copy).then_inc(done, 1)

                def stage(n, u, m):
                    act.wait_ge(x_normed, n + 1)
                    wait(act, x_turned, 2 * n)
                    act.activation(xs[:, :], xn[:, ds(n, 1), :].rearrange("p a w -> p (a w)"), ACT.Copy).then_inc(x_staged, 1)

                def step(n, u, m):
                    if among(n - 1):
                        row_scale(*shift(n, u, m, -1))
                    if among(n + 1):
                        group_scale(*shift(n, u, m, 1))
                    if among(n - 1):
                        stage(*shift(n, u, m, -1))
                        copies(tx, xT, x_turned, routed, n - 1, n - 1, x_copied)
                    if among(n + 1):
                        copies(tm, mT[1 - u], m_turned, mixed, n, n + 1, m_copied)
                group_scale(0, 0, 0)
                copies(tm, mT[0], m_turned, mixed, 0, 0, m_copied)
                over_tile_steps(act, step)

            @block.vector
            def _(dve):
                def norm_heads(n, u, m):
                    dve.wait_ge(m_scale, n + 1)
                    wait(dve, m_turned, 2 * n)
                    for g, (h0, nh) in enumerate(GROUPS):
                        cols = slice(HD * h0, HD * (h0 + nh))
                        ins = dve.scalar_tensor_tensor(out=m2[:, cols], in0=merged[:, ds(n, 1), cols].rearrange("p a w -> p (a w)"),
                                                       scalar=sm[:, u, g:g + 1], in1=gmo[:, cols], op0=ALU.mult, op1=ALU.mult)
                    ins.then_inc(m_normed, 1)

                def norm_rows(n, u, m):
                    dve.wait_ge(h_scale, n + 1)
                    row = lambda t: t[:, ds(n, 1), :].rearrange("p a w -> p (a w)")
                    dve.scalar_tensor_tensor(out=row(xn), in0=row(h), scalar=sh[:, u:u + 1], in1=gff[:, :],
                                             op0=ALU.mult, op1=ALU.mult).then_inc(x_normed, 1)

                def residual(n, u, m):
                    dve.wait_ge(x_loaded[u], 16 * (m + 1))
                    dve.wait_ge(mixed, n + 1)
                    dve.tensor_tensor(h[:, ds(n, 1), :].rearrange("p a w -> p (a w)"), om[:, :, :].rearrange("p a w -> p (a w)"),
                                      xr[:, u, :], ALU.add).then_inc(h_ready, 1)

                def take_logits(n):
                    dve.wait_ge(routed, n + 1)
                    dve.tensor_tensor(logits[:, ds(n, 1), :].rearrange("p a w -> p (a w)"), lg[:, 0:NG + NE], b_r[:, :],
                                      ALU.add).then_inc(logits_ready, 1)

                def step(n, u, m):
                    if among(n - 1):
                        norm_rows(*shift(n, u, m, -1))
                    if among(n + 1):
                        norm_heads(*shift(n, u, m, 1))
                    if among(n):
                        residual(n, u, m)
                    if among(n - 1):
                        take_logits(n - 1)
                norm_heads(0, 0, 0)
                over_tile_steps(dve, step)

            @block.gpsimd
            def _(pool):
                for s in released:
                    pool.sem_clear(s)


def routing(nc, c, a, dram, xn, logits, gates, slots, owner):
    with ExitStack() as ctx:
        sb = lambda n, s, d=F32: ctx.enter_context(nc.sbuf_tensor("route_" + n, s, d))
        ps = lambda n, s: ctx.enter_context(nc.psum_tensor("route_" + n, s, F32))
        sem = lambda n: ctx.enter_context(nc.semaphore("route_" + n))
        I32 = mybir.dt.int32
        ge, gs, es, t4, gh, le, l2, oh1, oh2 = (sb(n, [P, NT, 4]) for n in
                                               ("ge", "gs", "es", "t4", "gh", "le", "l2", "oh1", "oh2"))
        m1, m2, pg, w1, den = (sb(n, [P, NT]) for n in ("m1", "m2", "pg", "w1", "den"))
        t16 = sb("t16", [P, NT, NG, EG])
        M1 = sb("M1", [P, NT, NG, EG])
        M2 = sb("M2", [P, NT, NG, EG])
        M = sb("M", [P, NT, NE])
        S = sb("S", [P, NT + 1, NE])
        pos = sb("pos", [P, NT, NE])
        cnt = sb("cnt", [P, NE])
        cmp = sb("cmp", [P, NE, NT])
        nb = sb("nb", [P, NE])
        cum = sb("cum", [P, NE])
        ones16 = sb("ones16", [P, NE])
        bcmp = sb("bcmp", [P, SLOTBLOCKS, NE])
        bown = sb("bown", [P, SLOTBLOCKS])
        half = sb("half", [P, 1])
        slotf = sb("slotf", [P, 2, NT])
        desc_i = sb("desc_i", [P, 4], I32)
        desc = sb("desc", [P, 4])
        step_i = sb("step_i", [P, NT], I32)
        steps_ = sb("steps", [P, NT])
        blk_i = sb("blk_i", [P, SLOTBLOCKS], I32)
        blk = sb("blk", [P, SLOTBLOCKS])
        rank = ps("rank", [P, 512])
        cp = ps("cp", [P, 512])
        iotas = sem("iotas")
        chain = sem("chain")
        to_act = sem("to_act")
        from_act = sem("from_act")
        counted = sem("counted")
        chosen = sem("chosen")
        placed = sem("placed")
        scattered = sem("scattered")

        with nc.Block() as block:
            @block.gpsimd
            def _(pool):
                pool.iota(desc_i[:, :], pattern=[[-1, 4]], base=4, channel_multiplier=0)
                pool.iota(step_i[:, :], pattern=[[BS, NT]], base=0, channel_multiplier=0)
                pool.iota(blk_i[:, :], pattern=[[1, SLOTBLOCKS]], base=0, channel_multiplier=0).then_inc(iotas, 1)
                pool.wait_ge(placed, 1)
                for n in range(NT):
                    for k in range(2):
                        pool.indirect_dma_start(out=dram["grouped"],
                                                out_offset=bass.IndirectOffsetOnAxis(ap=slots[:, k, n:n + 1], axis=0),
                                                in_=xn[:, n, :], in_offset=None).then_inc(scattered, 16)
                pool.wait_ge(scattered, 16 * 2 * NT)

            @block.scalar
            def _(act):
                act.wait_ge(to_act, 1)
                act.activation(gs[:, :, :], ge[:, :, :], ACT.Exp).then_inc(from_act, 1)
                act.wait_ge(to_act, 2)
                act.activation(w1[:, :], m1[:, :], ACT.Exp).then_inc(from_act, 1)

            @block.tensor
            def _(pe):
                pe.wait_ge(chosen, 1)
                Mf = M[:, :, :].rearrange("p n e -> p (n e)")
                Sf = S[:, 0:NT, :].rearrange("p n e -> p (n e)")
                pe.matmul(rank[:, 0:NT * NE], c["keep_stick"][:, :], Mf, start=True, stop=False)
                pe.matmul(rank[:, 0:NT * NE], c["ones"][:, :], Sf, start=False, stop=True)
                pe.matmul(cp[:, 0:NE], c["ones"][:, :], S[:, NT, :], start=True, stop=True).then_inc(counted, 1)

            @block.vector
            def _(dve):
                s = Steps(dve, chain, 0)
                t = s.then
                bc = lambda x: x.unsqueeze(2).to_broadcast([P, NT, 4])
                G = logits[:, :, 0:NG]
                E4 = logits[:, :, NG:].rearrange("p n (g e) -> p n g e", e=EG)
                dve.wait_ge(iotas, 1)
                t(dve.tensor_copy(desc[:, :], desc_i[:, :]))
                t(dve.tensor_copy(steps_[:, :], step_i[:, :]))
                t(dve.tensor_copy(blk[:, :], blk_i[:, :]))
                desc_b = desc[:, :].unsqueeze(1).to_broadcast([P, NT, 4])

                def first_max(x, top, out):
                    t(dve.tensor_reduce(top[:, :], x, AX.X, ALU.max))
                    t(dve.tensor_tensor(t4[:, :, :], x, bc(top[:, :]), ALU.is_equal))
                    t(dve.tensor_tensor(t4[:, :, :], t4[:, :, :], desc_b, ALU.mult))
                    t(dve.tensor_reduce(den[:, :], t4[:, :, :], AX.X, ALU.max))
                    t(dve.tensor_tensor(out[:, :, :], t4[:, :, :], bc(den[:, :]), ALU.is_equal))

                first_max(G, m1, gh)
                t(dve.tensor_tensor(ge[:, :, :], G, bc(m1[:, :]), ALU.subtract))
                dve.sem_inc(to_act, 1)
                dve.wait_ge(from_act, 1)
                t(dve.tensor_reduce(pg[:, :], gs[:, :, :], AX.X, ALU.add))
                t(dve.reciprocal(pg[:, :], pg[:, :]))
                t(dve.tensor_tensor(t16[:, :, :, :], E4, gh[:, :, :].unsqueeze(3).to_broadcast([P, NT, NG, EG]), ALU.mult))
                t(dve.tensor_reduce(le[:, :, :], t16[:, :, :, :].rearrange("p n g e -> p n e g"), AX.X, ALU.add))
                first_max(le[:, :, :], m1, oh1)
                t(dve.scalar_tensor_tensor(out=l2[:, :, :].rearrange("p n e -> p (n e)"), in0=oh1[:, :, :].rearrange("p n e -> p (n e)"),
                                           scalar=NEG, in1=le[:, :, :].rearrange("p n e -> p (n e)"), op0=ALU.mult, op1=ALU.add))
                first_max(l2[:, :, :], m2, oh2)
                t(dve.tensor_tensor(m1[:, :], m2[:, :], m1[:, :], ALU.subtract))
                dve.sem_inc(to_act, 1)
                dve.wait_ge(from_act, 2)
                t(dve.tensor_scalar(den[:, :], w1[:, :], 1.0, None, ALU.add))
                t(dve.reciprocal(den[:, :], den[:, :]))
                t(dve.tensor_tensor(gates[:, 0, :], den[:, :], pg[:, :], ALU.mult))
                t(dve.tensor_tensor(gates[:, 1, :], gates[:, 0, :], w1[:, :], ALU.mult))
                for Mk, oh in ((M1, oh1), (M2, oh2)):
                    t(dve.tensor_tensor(Mk[:, :, :, :], gh[:, :, :].unsqueeze(3).to_broadcast([P, NT, NG, EG]),
                                        oh[:, :, :].unsqueeze(2).to_broadcast([P, NT, NG, EG]), ALU.mult))
                f = lambda x: x[:, :, :, :].rearrange("p n g e -> p n (g e)")
                t(dve.tensor_tensor(M[:, :, :], f(M1), f(M2), ALU.add))
                t(dve.memset(S[:, 0, :], 0.0))
                for n in range(NT):
                    t(dve.tensor_tensor(S[:, n + 1, :], S[:, n, :], M[:, n, :], ALU.add))
                dve.sem_inc(chosen, 1)
                dve.wait_ge(counted, 1)
                t(dve.tensor_copy(cnt[:, :], cp[:, 0:NE]))
                t(dve.memset(ones16[:, :], 1.0))
                t(dve.tensor_tensor(cmp[:, :, :], cnt[:, :].unsqueeze(2).to_broadcast([P, NE, NT]),
                                    steps_[:, :].unsqueeze(1).to_broadcast([P, NE, NT]), ALU.is_gt))
                t(dve.tensor_reduce(nb[:, :], cmp[:, :, :], AX.X, ALU.add))
                t(dve.tensor_tensor_scan(cum[:, :], ones16[:, :], nb[:, :], 0.0, ALU.mult, ALU.add))
                t(dve.tensor_tensor(bcmp[:, :, :], blk[:, :].unsqueeze(2).to_broadcast([P, SLOTBLOCKS, NE]),
                                    cum[:, :].unsqueeze(1).to_broadcast([P, SLOTBLOCKS, NE]), ALU.is_ge))
                t(dve.tensor_reduce(bown[:, :], bcmp[:, :, :], AX.X, ALU.add))
                t(dve.tensor_scalar(bown[:, :], bown[:, :], float(NE - 1), None, ALU.min))
                t(dve.tensor_copy(owner[:, 0:SLOTBLOCKS], bown[0:1, :]))
                t(dve.tensor_scalar(half[:, :], cum[:, NE - 1:NE], 0.5, 0.25 - LEAST_PAIRS, ALU.mult, ALU.add))
                t(dve.tensor_copy(owner[:, SLOTBLOCKS:SLOTBLOCKS + 1], half[0:1, :]))
                t(dve.tensor_tensor(cum[:, :], cum[:, :], nb[:, :], ALU.subtract))
                t(dve.tensor_scalar(cum[:, :], cum[:, :], float(BS), None, ALU.mult))
                t(dve.tensor_tensor(pos[:, :, :], rank[:, 0:NT * NE].rearrange("p (n e) -> p n e", e=NE),
                                    cum[:, :].unsqueeze(1).to_broadcast([P, NT, NE]), ALU.add))
                for k, Mk in enumerate((M1, M2)):
                    t(dve.tensor_tensor(M[:, :, :], f(Mk), pos[:, :, :], ALU.mult))
                    t(dve.tensor_reduce(slotf[:, k, :], M[:, :, :], AX.X, ALU.add))
                    t(dve.tensor_copy(slots[:, k, :], slotf[:, k, :]))
                dve.sem_inc(placed, 1)


def log_sigmoid_parts(act, x, t, chain, done, one):
    chain.then(act.activation(t, x, ACT.Abs))
    chain.then(act.activation(t, t, ACT.Exp, scale=-1.0))
    act.activation(t, t, ACT.Ln, bias=one).then_inc(done, 1)


def experts(nc, c, a, dram, owner, wg, wp, gpl):
    with ExitStack() as ctx:
        sb = lambda n, s, d=F32: ctx.enter_context(nc.sbuf_tensor("exp_" + n, s, d))
        ps = lambda n, s: ctx.enter_context(nc.psum_tensor("exp_" + n, s, F32))
        sem = lambda n: ctx.enter_context(nc.semaphore("exp_" + n))
        two = range(2)
        FT = DE // P
        TG = KD // 2
        YC = 4
        wgu = [sb(f"wgu{u}", [P, KD, 2 * DE]) for u in two]
        wd = [sb(f"wd{u}", [P, FT, D]) for u in two]
        xg = [sb(f"xg{u}", [ROWS, 2, D]) for u in two]
        xT = [sb(f"xT{u}", [P, KD, BS]) for u in two]
        logs = sb("logs", [P, FT * BS])
        sig = sb("sig", [P, FT * BS])
        hid = [sb(f"hid{u}", [P, FT * BS]) for u in two]
        y = [sb(f"y{u}", [ROWS, 2, D]) for u in two]
        tp = ps("tp", [P, 2, 512])
        gu = ps("gu", [P, 2, 2, 512])
        yp = ps("yp", [P, 2, 512])

        own, pool_turns = sem("sp_turns"), sem("pool_turns")
        up_loaded = [sem(f"up_loaded{u}") for u in two]
        down_loaded = [sem(f"down_loaded{u}") for u in two]
        x_loaded = [sem(f"x_loaded{u}") for u in two]
        turned = sem("turned")
        copied = sem("copied")
        upped = sem("upped")
        logged = sem("logged")
        summed = sem("summed")
        expd = sem("expd")
        hidden = sem("hidden")
        downed = sem("downed")
        y_taken = sem("y_taken")
        y_stored = [sem(f"y_stored{u}") for u in two]
        act_chain = sem("act_chain")
        dve_chain = sem("dve_chain")
        ple_loaded = sem("ple_loaded")

        def over_blocks(e, step):
            pairs = e.value_load(owner[0:1, SLOTBLOCKS:SLOTBLOCKS + 1], min_val=0, max_val=PAIRS - LEAST_PAIRS) + LEAST_PAIRS
            step(0, 0, 0, None)
            step(1, 1, 0, None)
            with e.Fori(1, pairs) as m:
                step(2 * m, 0, m, None)
                step(2 * m + 1, 1, m, None)
            step(2 * pairs, 0, pairs, "last")
            return pairs

        def behind(b):
            return not (isinstance(b, int) and b == 0)

        def rows(b):
            return dram["grouped"][ds(b * BS, BS), :].rearrange("(t p) n -> p t n", p=ROWS)

        with nc.Block() as block:
            @block.sync
            def _(sp):
                wv = a["w_ple_gate"].rearrange("(k p) n -> p k n", p=P)

                def step(b, u, m, last):
                    if last is None:
                        e = sp.value_load(owner[0:1, ds(b, 1)], min_val=0, max_val=NE - 1)
                        wait(sp, upped, b - 1, own)
                        sp.dma_start(wgu[u][:, :, :], a["w_gu"][ds(e, 1)].rearrange("a p k f -> (a p) k f"))\
                          .then_inc(up_loaded[u], 16)
                        bb, uu, _ = shift(b, u, m, 1)
                        wait(sp, turned, TG * b, own)
                        sp.dma_start(xg[uu][:, :, :], rows(bb)).then_inc(x_loaded[uu], 16)
                    if last:
                        for i in two:
                            cols = slice(512 * i, 512 * i + 512)
                            sp.dma_start(wg[:, :, cols], wv[:, :, cols]).then_inc(ple_loaded, 16)
                        sp.dma_start(wp[:, :, :], a["w_ple"].rearrange("(k p) n -> p k n", p=P)).then_inc(ple_loaded, 16)
                        sp.dma_start(gpl[:, :], a["norm_ple"].partition_broadcast(P)).then_inc(ple_loaded, 16)
                    if not (isinstance(b, int) and b < 2):
                        wait(sp, y_taken, YC * (b - 1), own)
                        sp.dma_start(rows(b - 2), y[u][:, :, :]).then_inc(y_stored[u], 16)
                    if last:
                        wait(sp, y_taken, YC * b, own)
                        sp.dma_start(rows(b - 1), y[1][:, :, :]).then_inc(y_stored[1], 16)
                sp.dma_start(xg[0][:, :, :], rows(0)).then_inc(x_loaded[0], 16)
                pairs = over_blocks(sp, step)
                for u in two:
                    wait(sp, y_stored[u], 16 * pairs, own)
                    wait(sp, x_loaded[u], 16 * (pairs + 1 - u), own)
                sp.wait_ge(ple_loaded, 16 * 4)

            @block.gpsimd
            def _(pool):
                def step(b, u, m, last):
                    if last is None:
                        e = pool.value_load(owner[0:1, ds(b, 1)], min_val=0, max_val=NE - 1)
                        wait(pool, downed, YC * (b - 1), pool_turns)
                        pool.dma_start(wd[u][:, :, :], a["w_ed"][ds(e, 1)].rearrange("a (f p) n -> p (a f) n", p=P))\
                            .then_inc(down_loaded[u], 16)
                over_blocks(pool, step)

            @block.tensor
            def _(pe):
                def turn(b, u, m, groups):
                    if 0 in groups:
                        pe.wait_ge(x_loaded[u], 16 * (m + 1))
                    for g in groups:
                        wait(pe, copied, TG * b + g - 1)
                        for k in (2 * g, 2 * g + 1):
                            for t in two:
                                col = BS * (k % 2) + ROWS * t
                                mm = pe.transpose(tp[:, g % 2, col:col + ROWS], xg[u][:, t, P * k:P * k + P],
                                                  c["ident"][0:ROWS, 0:ROWS])
                        mm.then_inc(turned, 1)

                def up(u, part, f):
                    for k in range(KD):
                        mm = pe.matmul(gu[:, u, part, BS * f:BS * f + BS], wgu[u][:, k, DE * part + P * f:DE * part + P * f + P],
                                       xT[u][:, k, :], start=(k == 0 and f == 0), stop=(k == KD - 1), skip_group_check=True)
                    return mm

                def down(b, u, m):
                    pe.wait_ge(hidden, b + 1)
                    pe.wait_ge(down_loaded[u], 16 * (m + 1))
                    for t in two:
                        for half in two:
                            wait(pe, y_taken, YC * b + 2 * t + half - 1)
                            for f in range(FT):
                                mm = pe.matmul(yp[0:ROWS, half, :], hid[u][:, BS * f + ROWS * t:BS * f + ROWS * t + ROWS],
                                               wd[u][:, f, 512 * half:512 * half + 512], start=(f == 0), stop=(f == FT - 1))
                            mm.then_inc(downed, 1)

                def step(b, u, m, last):
                    if last is None:
                        pe.wait_ge(copied, TG * (b + 1))
                        pe.wait_ge(up_loaded[u], 16 * (m + 1))
                        wait(pe, hidden, b - 1)
                        up(u, 0, 0)
                        turn(*shift(b, u, m, 1), (0, 1))
                        up(u, 0, 1)
                        turn(*shift(b, u, m, 1), (2, 3))
                    if behind(b):
                        down(*shift(b, u, m, -1))
                    if last is None:
                        up(u, 1, 0)
                        up(u, 1, 1).then_inc(upped, 1)
                turn(0, 0, 0, range(TG))
                over_blocks(pe, step)

            @block.scalar
            def _(act):
                def copies(b, u):
                    for g in range(TG):
                        act.wait_ge(turned, TG * b + g + 1)
                        wait(act, upped, b - 1)
                        act.activation(xT[u][:, 2 * g:2 * g + 2, :].rearrange("p j n -> p (j n)"), tp[:, g % 2, 0:2 * BS],
                                       ACT.Copy).then_inc(copied, 1)

                def step(b, u, m, last):
                    if behind(b):
                        bb, uu, _ = shift(b, u, m, -1)
                        s = Steps(act, act_chain, 2 * bb)
                        act.wait_ge(upped, bb + 1)
                        log_sigmoid_parts(act, gu[:, uu, 0, 0:FT * BS], logs[:, :], s, logged, c["one"][:, :])
                        act.wait_ge(summed, bb + 1)
                        act.activation(sig[:, :], logs[:, :], ACT.Exp).then_inc(expd, 1)
                    if last is None:
                        copies(b + 1, 1 - u)
                copies(0, 0)
                over_blocks(act, step)

            @block.vector
            def _(dve):
                def step(b, u, m, last):
                    if not behind(b):
                        return
                    bb, uu, m1 = shift(b, u, m, -1)
                    s = Steps(dve, dve_chain, bb)
                    dve.wait_ge(logged, bb + 1)
                    dve.scalar_tensor_tensor(out=logs[:, :], in0=gu[:, uu, 0, 0:FT * BS], scalar=0.0, in1=logs[:, :],
                                             op0=ALU.min, op1=ALU.subtract).then_inc(summed, 1)
                    dve.wait_ge(expd, bb + 1)
                    wait(dve, downed, YC * (bb - 1))
                    s.then(dve.tensor_tensor(hid[uu][:, :], gu[:, uu, 0, 0:FT * BS], sig[:, :], ALU.mult))
                    dve.tensor_tensor(hid[uu][:, :], hid[uu][:, :], gu[:, uu, 1, 0:FT * BS], ALU.mult).then_inc(hidden, 1)
                    wait(dve, y_stored[uu], 16 * m1)
                    for t in two:
                        for half in two:
                            dve.wait_ge(downed, YC * bb + 2 * t + half + 1)
                            dve.tensor_copy(y[uu][:, t, 512 * half:512 * half + 512], yp[0:ROWS, half, :]).then_inc(y_taken, 1)
                over_blocks(dve, step)


def split_upper(act, w, high, done):
    for half in range(2):
        cols = slice(512 * half, 512 * half + 512)
        act.activation(high[:, :, cols], w[:, :, cols], ACT.Copy).then_inc(done, 1)


def split_lower(dve, w, high, low, split, done):
    for half in range(2):
        cols = slice(512 * half, 512 * half + 512)
        dve.wait_ge(split, half + 1)
        dve.tensor_tensor(low[:, :, cols], w[:, :, cols], high[:, :, cols].bitcast(F32), ALU.subtract).then_inc(done, 1)


def split_product(pe, out, xT, xT_low, w, w_low, cols):
    for k in range(KD):
        for i, (xs, ws) in enumerate(((xT, w_low), (xT_low, w), (xT, w))):
            mm = pe.matmul(out, xs[:, k, :], ws[:, k, cols], start=(k == 0 and i == 0), stop=(k == KD - 1 and i == 2))
    return mm


def embedding(nc, c, a, dram, h, gates, slots, wg, wp, gpl):
    with ExitStack() as ctx:
        sb = lambda n, s, d=F32: ctx.enter_context(nc.sbuf_tensor("ple_" + n, s, d))
        ps = lambda n, s: ctx.enter_context(nc.psum_tensor("ple_" + n, s, F32))
        sem = lambda n: ctx.enter_context(nc.semaphore("ple_" + n))
        two = range(2)
        KP = DP // P
        pT = [sb(f"pT{u}", [P, KP, P]) for u in two]
        rows = [sb(f"rows{u}", [P, 2, D]) for u in two]
        hn = sb("hn", [P, D])
        hT = [sb(f"hT{u}", [P, KD, P], F32R) for u in two]
        hT_low = [sb(f"hT_low{u}", [P, KD, P], F32R) for u in two]
        wg_high = sb("wg_high", [P, KD, D], F32R)
        wg_low = sb("wg_low", [P, KD, D], F32R)
        sq = sb("sq", [P, D])
        sh = sb("sh", [P, 2])
        logs = sb("logs", [P, D])
        y = sb("y", [P, 2, D])
        tp = ps("tp", [P, 2, 512])
        gp = ps("gp", [P, 2, 2, 512])
        pp = ps("pp", [P, 2, 512])

        own = sem("sp_turns")
        p_loaded = [sem(f"p_loaded{u}") for u in two]
        gathered = [sem(f"gathered{u}") for u in two]
        added = sem("added")
        scaled = sem("scaled")
        normed = sem("normed")
        turned = sem("turned")
        copied = sem("copied")
        lowered = sem("lowered")
        split_high = sem("split_high")
        split_low = sem("split_low")
        gated = sem("gated")
        pled = sem("pled")
        logged = sem("logged")
        summed = sem("summed")
        expd = sem("expd")
        y_ready = sem("y_ready")
        y_stored = [sem(f"y_stored{u}") for u in two]
        chain = sem("chain")
        act_chain = sem("act_chain")
        add_chain = sem("add_chain")
        log_chain = sem("log_chain")

        with nc.Block() as block:
            @block.sync
            def _(sp):
                def step(n, u, m):
                    if among(n):
                        wait(sp, pled, n - 1, own)
                        sp.dma_start(pT[u][:, :, :], a["pT"][ds(n, 1)].rearrange("a p k n -> p (a k) n")).then_inc(p_loaded[u], 16)
                    if among(n - 1):
                        bb, uu, mm = shift(n, u, m, -1)
                        wait(sp, y_ready, bb + 1, own)
                        sp.dma_start(a["y"][ds(bb * P, P), :], y[:, uu, :]).then_inc(y_stored[uu], 16)
                over_tile_steps(sp, step)
                for u in two:
                    sp.wait_ge(y_stored[u], 16 * ((NT + 1 - u) // 2))

            @block.gpsimd
            def _(pool):
                for n in range(NT):
                    wait(pool, added, n - 1)
                    for k in two:
                        pool.indirect_dma_start(out=rows[n % 2][:, k, :], out_offset=None, in_=dram["grouped"],
                                                in_offset=bass.IndirectOffsetOnAxis(ap=slots[:, k, n:n + 1], axis=0))\
                            .then_inc(gathered[n % 2], 16)

            @block.tensor
            def _(pe):
                def turn(n):
                    pe.wait_ge(normed, n + 1)
                    for half in two:
                        wait(pe, lowered, 2 * (n - 1) + half + 1)
                        for j in range(4 * half, 4 * half + 4):
                            mm = pe.transpose(tp[:, half, P * (j % 4):P * (j % 4) + P], hn[:, P * j:P * j + P], c["ident"][:, :])
                        mm.then_inc(turned, 1)

                def gate(u, half, n):
                    cols = slice(512 * half, 512 * half + 512)
                    if isinstance(n, int) and n == 0:
                        pe.wait_ge(split_low, half + 1)
                    return split_product(pe, gp[:, u, half, :], hT[u], hT_low[u], wg_high, wg_low, cols)

                def step(n, u, m):
                    if among(n):
                        pe.wait_ge(lowered, 2 * n + 2)
                        wait(pe, y_ready, n - 1)
                        gate(u, 0, n)
                    if among(n + 1):
                        turn(n + 1)
                    if among(n):
                        gate(u, 1, n).then_inc(gated, 1)
                        pe.wait_ge(p_loaded[u], 16 * (m + 1))
                        wait(pe, y_ready, n)
                        for half in two:
                            cols = slice(512 * half, 512 * half + 512)
                            for k in range(KP):
                                mm = pe.matmul(pp[:, half, :], pT[u][:, k, :], wp[:, k, cols], start=(k == 0), stop=(k == KP - 1))
                        mm.then_inc(pled, 1)
                turn(0)
                over_tile_steps(pe, step)

            @block.scalar
            def _(act):
                def scale(n, u, m):
                    s = Steps(act, act_chain, 2 * n)
                    act.wait_ge(added, n + 1)
                    wait(act, normed, n - 1)
                    s.then(act.activation(sq[:, :], h[:, ds(n, 1), :].rearrange("p a w -> p (a w)"), ACT.Square, accum_out=sh[:, u:u + 1]))
                    s.then(act.activation(sh[:, u:u + 1], sh[:, u:u + 1], ACT.Ln, bias=c["eps"][:, :], scale=1.0 / D))
                    act.activation(sh[:, u:u + 1], sh[:, u:u + 1], ACT.Exp, scale=-0.5).then_inc(scaled, 1)

                def copies(n, u):
                    for half in two:
                        act.wait_ge(turned, 2 * n + half + 1)
                        wait(act, gated, n - 1)
                        act.activation(hT[u][:, 4 * half:4 * half + 4, :].rearrange("p j n -> p (j n)"), tp[:, half, :],
                                       ACT.Copy).then_inc(copied, 1)

                def step(n, u, m):
                    if among(n + 1):
                        scale(*shift(n, u, m, 1))
                    if among(n - 1):
                        bb, uu, _ = shift(n, u, m, -1)
                        s = Steps(act, log_chain, 2 * bb)
                        act.wait_ge(gated, bb + 1)
                        wait(act, y_ready, bb)
                        log_sigmoid_parts(act, gp[:, uu, :, :].rearrange("p a n -> p (a n)"), logs[:, :], s, logged,
                                          c["one"][:, :])
                    if among(n + 1):
                        copies(n + 1, 1 - u)
                    if among(n - 1):
                        act.wait_ge(summed, bb + 1)
                        act.activation(logs[:, :], logs[:, :], ACT.Exp).then_inc(expd, 1)
                split_upper(act, wg, wg_high, split_high)
                scale(0, 0, 0)
                copies(0, 0)
                over_tile_steps(act, step)

            @block.vector
            def _(dve):
                def add(n, u, m):
                    s = Steps(dve, add_chain, n)
                    dve.wait_ge(gathered[u], 32 * (m + 1))
                    row = h[:, ds(n, 1), :].rearrange("p a w -> p (a w)")
                    s.then(dve.scalar_tensor_tensor(out=row, in0=rows[u][:, 0, :], scalar=gates[:, 0, ds(n, 1)],
                                                    in1=row, op0=ALU.mult, op1=ALU.add))
                    dve.scalar_tensor_tensor(out=row, in0=rows[u][:, 1, :], scalar=gates[:, 1, ds(n, 1)],
                                             in1=row, op0=ALU.mult, op1=ALU.add).then_inc(added, 1)

                def norm(n, u, m):
                    dve.wait_ge(scaled, n + 1)
                    wait(dve, turned, 2 * n)
                    dve.scalar_tensor_tensor(out=hn[:, :], in0=h[:, ds(n, 1), :].rearrange("p a w -> p (a w)"), scalar=sh[:, u:u + 1], in1=gpl[:, :],
                                             op0=ALU.mult, op1=ALU.mult).then_inc(normed, 1)

                def log_sigmoid(n, u):
                    dve.wait_ge(logged, n + 1)
                    dve.scalar_tensor_tensor(out=logs[:, :], in0=gp[:, u, :, :].rearrange("p a n -> p (a n)"), scalar=0.0,
                                             in1=logs[:, :], op0=ALU.min, op1=ALU.subtract).then_inc(summed, 1)

                def finish(n, u, m):
                    s = Steps(dve, chain, n)
                    dve.wait_ge(pled, n + 1)
                    dve.wait_ge(expd, n + 1)
                    wait(dve, y_stored[u], 16 * m)
                    s.then(dve.tensor_tensor(y[:, u, :], pp[:, :, :].rearrange("p a n -> p (a n)"), logs[:, :], ALU.mult))
                    dve.tensor_tensor(y[:, u, :], y[:, u, :], h[:, ds(n, 1), :].rearrange("p a w -> p (a w)"), ALU.add)\
                        .then_inc(y_ready, 1)

                def lower(n, u):
                    for half in two:
                        dve.wait_ge(copied, 2 * n + half + 1)
                        wait(dve, gated, n - 1)
                        hi = hT[u][:, 4 * half:4 * half + 4, :].rearrange("p j n -> p (j n)")
                        lo = hT_low[u][:, 4 * half:4 * half + 4, :].rearrange("p j n -> p (j n)")
                        dve.tensor_tensor(lo, tp[:, half, :], hi.bitcast(F32), ALU.subtract).then_inc(lowered, 1)

                def step(n, u, m):
                    if among(n + 1):
                        add(*shift(n, u, m, 1))
                        norm(*shift(n, u, m, 1))
                    if among(n - 1):
                        bb, uu, mm = shift(n, u, m, -1)
                        log_sigmoid(bb, uu)
                        finish(bb, uu, mm)
                    if among(n + 1):
                        lower(n + 1, 1 - u)
                split_lower(dve, wg, wg_high, wg_low, split_high, split_low)
                add(0, 0, 0)
                norm(0, 0, 0)
                lower(0, 0)
                over_tile_steps(dve, step)


def program(nc, a, dram):
    with ExitStack() as ctx:
        sb = lambda n, s, d=F32: ctx.enter_context(nc.sbuf_tensor(n, s, d))
        sem = lambda n: ctx.enter_context(nc.semaphore(n))
        dram["q_heads"] = dram["qkT"][0:KD].rearrange("j (r d) n -> (j r) d n", d=HD)
        dram["k_heads"] = dram["qkT"][KD:2 * KD].rearrange("j (r d) n -> (j r) d n", d=HD)
        c = constants(sb)
        zeroed = sem("zeroed")
        released = projection(nc, c, a, dram, zeroed)
        h = sb("h", [P, NT, D])
        logits = sb("logits", [P, NT, NG + NE])
        gates = sb("gates", [P, 2, NT])
        slots = sb("slots", [P, 2, NT], mybir.dt.uint32)
        owner = sb("owner", [1, SLOTBLOCKS + 1], mybir.dt.int32)
        with ExitStack() as mid:
            sbm = lambda n, s, d=F32: mid.enter_context(nc.sbuf_tensor(n, s, d))
            merged = h
            attention(nc, c, a, dram, merged, False, released)
            attention(nc, c, a, dram, merged, True, released)
            mixw = {"w_out": sbm("w_out", [P, KD, D]), "w_r": sbm("w_router", [P, KD, NG + NE]),
                    "b_r": sbm("b_router", [P, NG + NE]), "gmo": sbm("g_mix_out", [P, D]), "gff": sbm("norm_ffn", [P, D])}
            sticks(nc, c, a, dram, merged, mixw)
            with nc.sbuf_tensor("xn", [P, NT, D], F32) as xn:
                mixing(nc, c, a, dram, merged, h, xn, logits, released, mixw)
                routing(nc, c, a, dram, xn, logits, gates, slots, owner)
        wg = sb("w_ple_gate", [P, KD, D])
        wp = sb("w_ple", [P, DP // P, D])
        gpl = sb("norm_ple", [P, D])
        experts(nc, c, a, dram, owner, wg, wp, gpl)
        embedding(nc, c, a, dram, h, gates, slots, wg, wp, gpl)


def kernel(**inputs):
    import numpy as np
    import concourse.bacc as bacc
    from concourse.bass_utils import run_bass_kernel_spmd

    i = {k: np.asarray(v) for k, v in inputs.items()}
    x = np.concatenate([i["x_prompt"][0], i["x_sample"].reshape(NB * TS, D)])
    p = np.concatenate([i["p_prompt"][0, 0], i["p_sample"][0].reshape(NB * TS, DP)])
    kc = np.concatenate([i["cache_a_k"][0], i["cache_b_k"][0], i["cache_c_k"][0]], axis=2)
    vc = np.concatenate([i["cache_a_v"][0], i["cache_b_v"][0], i["cache_c_v"][0]], axis=2)
    cols = lambda v: v[0].reshape(-1, P).T
    host = {
        "x": x,
        "xT": x.reshape(NT, P, KD, P).transpose(0, 3, 2, 1),
        "pT": p.reshape(NT, P, DP // P, P).transpose(0, 3, 2, 1),
        "cache_kT": kc.transpose(2, 0, 3, 1).reshape(H, NB // 2, P, PAST).transpose(0, 2, 1, 3),
        "cache_v": vc.transpose(2, 0, 1, 3).reshape(H, NB, PT, P, HD).transpose(0, 3, 1, 2, 4),
        "cache_logf": i["cache_a_logf"][0].transpose(2, 0, 1).reshape(HA * NB, PAST),
        "norm_mix": cols(i["norm_mix"]), "g_mix_out": i["g_mix_out"][0],
        "norm_ffn": i["norm_ffn"][0], "norm_ple": i["norm_ple"][0],
        "w_in": i["w_in"][0], "b_f": i["b_f"][0], "g_qa": i["g_qa"][0], "g_ka": i["g_ka"][0],
        "g_qb": i["g_qb"][0], "g_kb": i["g_kb"][0], "rel_bias": i["rel_bias"][0], "w_out": i["w_out"][0],
        "w_router": np.concatenate([i["w_router_group"][0], i["w_router_expert"][0]], axis=1),
        "b_router": np.concatenate([i["b_router_group"][0], i["b_router_expert"][0]]),
        "w_gu": np.concatenate([i[n][0].reshape(NE, KD, P, DE) for n in ("w_exp_gate", "w_exp_up")], axis=3)
                  .transpose(0, 2, 1, 3),
        "w_ed": i["w_exp_down"][0],
        "w_ple": i["w_ple"][0], "w_ple_gate": i["w_ple_gate"][0],
    }
    outs = {"y": (TOK, D), "k_all": (TOK, D), "v_all": (TOK, D), "logf_all": (TOK, HA)}
    scratch = {"qkT": (2 * KD, P, TOK), "lfs": (HA, NB * TS), "c": (2, HA, TOK), "c_past": (HA, NB, PAST),
               "bias": (HB, EXT), "bias_hankel": (HB, P, 3 * P), "grouped": (NT * FILLS * ROWS, D)}

    nc = bacc.Bacc("TRN2", target_bir_lowering=False, num_devices=1)
    arrays, a, dram = {}, {}, {}
    for name, v in host.items():
        arrays["in_" + name] = np.ascontiguousarray(v)
        a[name] = nc.dram_tensor("in_" + name, v.shape, F32, kind="ExternalInput").ap()
    for name, shape in outs.items():
        a[name] = nc.dram_tensor("out_" + name, shape, F32, kind="ExternalOutput").ap()
    for name, shape in scratch.items():
        dram[name] = nc.dram_tensor("scratch_" + name, shape, F32, kind="Internal").ap()
    program(nc, a, dram)
    r = run_bass_kernel_spmd(nc, [arrays], core_ids=[0]).results[0]

    y, k, v, f = (r["out_" + n] for n in ("y", "k_all", "v_all", "logf_all"))

    def rows(t, lo, n, prompt, keep=0):
        t = t.reshape(TOK, -1, HD)[:, lo:lo + n]
        return t[keep:SEQ].reshape(1, 1, SEQ - keep, n, HD) if prompt else t[SEQ:].reshape(1, NB, TS, n, HD)

    res = [y[:SEQ].reshape(1, SEQ, D), y[SEQ:].reshape(NB, TS, D)]
    for prompt in (True, False):
        res += [rows(k, 0, HA, prompt), rows(v, 0, HA, prompt),
                f[:SEQ].reshape(1, 1, SEQ, HA) if prompt else f[SEQ:].reshape(1, NB, TS, HA),
                rows(k, HA, HB, prompt, SEQ - PAST), rows(v, HA, HB, prompt, SEQ - PAST),
                rows(k, HA + HB, HC, prompt), rows(v, HA + HB, HC, prompt)]
    return tuple(np.ascontiguousarray(t) for t in res)
```
